# Optimizing a Trainium2 kernel written in Bass

```python
import jax, jax.numpy as jnp
from jax import lax
import numpy as np
import math
import jax
import jax.numpy as jnp

D_MODEL = 1024
BATCH = 1
SEQ = 512
DEPTH = 2

H_A = 8
NOPE = 64
ROPE_D = 32
V_A = 64
Q_LORA = 256
KV_LORA = 128
W_A = H_A * V_A
H_B = 8
HD_B = 64
W_B = H_B * HD_B
H_C = 8
HD_C = 64
W_C = H_C * HD_C
DECAY_LORA = 64
AAA_LORA = 64
MV_LORA = 32
SHIFT_COLS = 3 * W_C + DECAY_LORA + AAA_LORA
ROPE_THETA = 10000.0
Q_BLOCK = 128
RWKV_DECAY_SCALE = 0.606531
GN_EPS = 64e-5
EPS = 1e-6
NEG_INF = -1e30

IN_SIZES = (Q_LORA, KV_LORA, ROPE_D, W_A,
            W_B, W_B, W_B, H_B, W_B,
            SHIFT_COLS, W_C,
            3 * D_MODEL)
IN_COLS = sum(IN_SIZES)
RWKV_SIZES = (W_C, W_C, W_C, DECAY_LORA, AAA_LORA)


def rmsnorm(x, g, eps=EPS):
    xf = x.astype(jnp.float32)
    y = xf * lax.rsqrt(jnp.mean(xf * xf, axis=-1, keepdims=True) + eps)
    return (y * g.astype(jnp.float32)).astype(x.dtype)

def split_cols(p, sizes):
    idx = np.cumsum(np.array(sizes))[:-1].tolist()
    return jnp.split(p, idx, axis=-1)

def rope_tables(seq):
    inv = ROPE_THETA ** (-jnp.arange(0, ROPE_D, 2, dtype=jnp.float32) / ROPE_D)
    ang = jnp.arange(seq, dtype=jnp.float32)[:, None] * inv[None, :]
    return jnp.cos(ang)[:, None, :], jnp.sin(ang)[:, None, :]

def apply_rope(x, cos, sin):
    half = ROPE_D // 2
    x1 = x[..., :half].astype(jnp.float32)
    x2 = x[..., half:].astype(jnp.float32)
    out = jnp.concatenate([x1 * cos - x2 * sin, x2 * cos + x1 * sin], axis=-1)
    return out.astype(x.dtype)

def causal_block_attention(q, k, v, cum=None):
    B, H, S, Dk = q.shape
    Dv = v.shape[-1]
    nb = S // Q_BLOCK
    scale = Dk ** -0.5
    kpos = jnp.arange(S)
    q_blocks = q.reshape(B, H, nb, Q_BLOCK, Dk).transpose(2, 0, 1, 3, 4)
    use_decay = cum is not None
    xs = (jnp.arange(nb), q_blocks)
    if use_decay:
        xs = xs + (cum.reshape(B, H, nb, Q_BLOCK).transpose(2, 0, 1, 3),)

    def block(args):
        i, qb = args[0], args[1]
        s = jnp.einsum('bhqd,bhkd->bhqk', qb, k).astype(jnp.float32) * scale
        if use_decay:
            s = s + args[2][..., :, None] - cum[:, :, None, :]
        qpos = i * Q_BLOCK + jnp.arange(Q_BLOCK)
        s = jnp.where(kpos[None, :] <= qpos[:, None], s, NEG_INF)
        p = jax.nn.softmax(s, axis=-1)
        return jnp.einsum('bhqk,bhkd->bhqd', p.astype(v.dtype), v)

    o = lax.map(block, xs)
    return o.transpose(1, 0, 3, 2, 4).reshape(B, S, H * Dv)

def mla_branch(c_q, c_kv, k_r, gate, qa_g, w_uq, kva_g, w_ukv, q_g, knope_g, krope_g, cos, sin):
    B, S, _ = c_q.shape
    q = (rmsnorm(c_q, qa_g) @ w_uq).reshape(B, S, H_A, NOPE + ROPE_D)
    q = rmsnorm(q, q_g)
    q = jnp.concatenate([q[..., :NOPE], apply_rope(q[..., NOPE:], cos, sin)], axis=-1)
    kv = (rmsnorm(c_kv, kva_g) @ w_ukv).reshape(B, S, H_A, NOPE + V_A)
    k_nope = rmsnorm(kv[..., :NOPE], knope_g)
    v = kv[..., NOPE:]
    k_rope = apply_rope(rmsnorm(k_r, krope_g)[:, :, None, :], cos, sin)
    k = jnp.concatenate([k_nope, jnp.broadcast_to(k_rope, (B, S, H_A, ROPE_D))], axis=-1)
    o = causal_block_attention(q.transpose(0, 2, 1, 3), k.transpose(0, 2, 1, 3), v.transpose(0, 2, 1, 3))
    return o * jax.nn.silu(gate)

def fox_branch(fq, fk, fv, ff, gate, b_f, q_g, k_g):
    B, S, _ = fq.shape
    q = rmsnorm(fq.reshape(B, S, H_B, HD_B), q_g)
    k = rmsnorm(fk.reshape(B, S, H_B, HD_B), k_g)
    v = fv.reshape(B, S, H_B, HD_B)
    log_f = jax.nn.log_sigmoid((ff + b_f).astype(jnp.float32))
    cum = jnp.cumsum(log_f, axis=1).transpose(0, 2, 1)
    o = causal_block_attention(q.transpose(0, 2, 1, 3), k.transpose(0, 2, 1, 3), v.transpose(0, 2, 1, 3), cum)
    return o * jax.nn.silu(gate)

def rwkv7_scan(r, w, k, v, kk, a):
    B, S, H, N = r.shape

    def step(state, inp):
        r_t, w_t, k_t, v_t, kk_t, a_t = inp
        sa = jnp.einsum('bhvk,bhk->bhv', state, -kk_t)
        state = (state * w_t[:, :, None, :] + sa[..., None] * (kk_t * a_t)[:, :, None, :]
                 + v_t[..., None] * k_t[:, :, None, :])
        return state, jnp.einsum('bhvk,bhk->bhv', state, r_t)

    xs = tuple(t.transpose(1, 0, 2, 3) for t in (r, w, k, v, kk, a))
    _, y = lax.scan(step, jnp.zeros((B, H, N, N), jnp.float32), xs)
    return y.transpose(1, 0, 2, 3)

def rwkv_branch(r, k, v, wl, al, gate, w0, w_up, a0, a_up, k_k, k_a, r_k, lnx_g, lnx_b):
    B, S, _ = r.shape
    f32 = jnp.float32
    heads = lambda t: t.astype(f32).reshape(B, S, H_C, HD_C)
    w = jnp.exp(-RWKV_DECAY_SCALE * jax.nn.sigmoid((w0 + jnp.tanh(wl) @ w_up).astype(f32)))
    a = jax.nn.sigmoid((a0 + al @ a_up).astype(f32))
    kk = heads(k * k_k)
    kk = kk / jnp.maximum(jnp.sqrt(jnp.sum(kk * kk, axis=-1, keepdims=True)), 1e-12)
    k_mod = k.astype(f32) * (1.0 + (a - 1.0) * k_a.astype(f32))
    r_h, w_h, k_h, v_h, a_h = heads(r), heads(w), heads(k_mod), heads(v), heads(a)
    y = rwkv7_scan(r_h, w_h, k_h, v_h, kk, a_h)
    mu = jnp.mean(y, axis=-1, keepdims=True)
    var = jnp.mean(jnp.square(y - mu), axis=-1, keepdims=True)
    y = ((y - mu) * lax.rsqrt(var + GN_EPS)).reshape(B, S, W_C) * lnx_g.astype(f32) + lnx_b.astype(f32)
    bonus = jnp.sum(r_h * k_h * r_k.astype(f32), axis=-1, keepdims=True) * v_h
    out = (y + bonus.reshape(B, S, W_C)) * jax.nn.silu(gate.astype(f32))
    return out.astype(gate.dtype)

def first_inputs(seed: int = 0) -> dict:
    key = jax.random.key(seed)
    ks = iter(jax.random.split(key, 48))
    f32 = jnp.float32
    L, Lv = DEPTH, DEPTH - 1

    def nrm(shape, scale):
        return scale * jax.random.normal(next(ks), shape, f32)

    def gain(shape):
        return 1.0 + nrm(shape, 0.02)

    x = jax.random.normal(next(ks), (BATCH, SEQ, D_MODEL), f32)
    return {
        "x": x,
        "norm_g": gain((L, D_MODEL)),
        "w_in": nrm((L, D_MODEL, IN_COLS), D_MODEL ** -0.5),
        "mla_qa_g": gain((L, Q_LORA)),
        "mla_w_uq": nrm((L, Q_LORA, H_A * (NOPE + ROPE_D)), Q_LORA ** -0.5),
        "mla_kva_g": gain((L, KV_LORA)),
        "mla_w_ukv": nrm((L, KV_LORA, H_A * (NOPE + V_A)), KV_LORA ** -0.5),
        "mla_q_g": gain((L, NOPE + ROPE_D)),
        "mla_knope_g": gain((L, NOPE)),
        "mla_krope_g": gain((L, ROPE_D)),
        "fox_b_f": jnp.broadcast_to(jnp.linspace(1.0, 6.0, H_B, dtype=f32), (L, H_B)) + nrm((L, H_B), 0.1),
        "fox_q_g": gain((L, HD_B)),
        "fox_k_g": gain((L, HD_B)),
        "rwkv_mu": jax.random.uniform(next(ks), (L, SHIFT_COLS), f32),
        "rwkv_w0": nrm((L, W_C), 1.0),
        "rwkv_w_up": nrm((L, DECAY_LORA, W_C), 0.5 * DECAY_LORA ** -0.5),
        "rwkv_a0": nrm((L, W_C), 0.5),
        "rwkv_a_up": nrm((L, AAA_LORA, W_C), 0.5 * AAA_LORA ** -0.5),
        "rwkv_k_k": 0.85 + nrm((L, W_C), 0.1),
        "rwkv_k_a": 1.0 + nrm((L, W_C), 0.1),
        "rwkv_r_k": nrm((L, H_C, HD_C), 0.1),
        "rwkv_lnx_g": gain((L, W_C)),
        "rwkv_lnx_b": nrm((L, W_C), 0.02),
        "rwkv_v0": nrm((Lv, W_C), 0.5),
        "rwkv_v_down": nrm((Lv, W_C, MV_LORA), W_C ** -0.5),
        "rwkv_v_up": nrm((Lv, MV_LORA, W_C), 0.5 * MV_LORA ** -0.5),
        "w_pa": nrm((L, W_A, D_MODEL), W_A ** -0.5),
        "w_pb": nrm((L, W_B, D_MODEL), W_B ** -0.5),
        "w_pc": nrm((L, W_C, D_MODEL), W_C ** -0.5),
        "w_out": nrm((L, D_MODEL, D_MODEL), D_MODEL ** -0.5),
    }

def first_block(x, norm_g, w_in, mla_qa_g, mla_w_uq, mla_kva_g, mla_w_ukv, mla_q_g, mla_knope_g,
              mla_krope_g, fox_b_f, fox_q_g, fox_k_g, rwkv_mu, rwkv_w0, rwkv_w_up, rwkv_a0, rwkv_a_up,
              rwkv_k_k, rwkv_k_a, rwkv_r_k, rwkv_lnx_g, rwkv_lnx_b, rwkv_v0, rwkv_v_down, rwkv_v_up,
              w_pa, w_pb, w_pc, w_out):
    S = x.shape[1]
    cos, sin = rope_tables(S)
    v_first = None
    for l in range(DEPTH):
        h = rmsnorm(x, norm_g[l])
        p = h @ w_in[l]
        (c_q, c_kv, k_r, gate_a, fq, fk, fv, ff, gate_b,
         shift_cols, gate_c, merge_cols) = split_cols(p, IN_SIZES)

        o_a = mla_branch(c_q, c_kv, k_r, gate_a, mla_qa_g[l], mla_w_uq[l], mla_kva_g[l], mla_w_ukv[l],
                         mla_q_g[l], mla_knope_g[l], mla_krope_g[l], cos, sin)
        o_b = fox_branch(fq, fk, fv, ff, gate_b, fox_b_f[l], fox_q_g[l], fox_k_g[l])
        prev = jnp.pad(shift_cols, ((0, 0), (1, 0), (0, 0)))[:, :-1]
        shifted = shift_cols + rwkv_mu[l] * (prev - shift_cols)
        r, k, v, wl, al = split_cols(shifted, RWKV_SIZES)
        if l == 0:
            v_first = v
        else:
            nu = jax.nn.sigmoid(rwkv_v0[l - 1] + (v @ rwkv_v_down[l - 1]) @ rwkv_v_up[l - 1])
            v = v + (v_first - v) * nu
        o_c = rwkv_branch(r, k, v, wl, al, gate_c, rwkv_w0[l], rwkv_w_up[l], rwkv_a0[l], rwkv_a_up[l],
                          rwkv_k_k[l], rwkv_k_a[l], rwkv_r_k[l], rwkv_lnx_g[l], rwkv_lnx_b[l])

        g_a, g_b, g_c = jnp.split(merge_cols, 3, axis=-1)
        merged = (jax.nn.sigmoid(g_a) * (o_a @ w_pa[l])
                  + jax.nn.sigmoid(g_b) * (o_b @ w_pb[l])
                  + jax.nn.sigmoid(g_c) * (o_c @ w_pc[l]))
        x = x + (merged @ w_out[l]).astype(x.dtype)
    return x


A_WIDTH = 512
A_CONV = 3
B_WIDTH = 512
B_CONV = 31
C_HEADS = 8
C_HEAD_DIM = 64
IDX_HEADS = 8
IDX_DIM = 32
TOPK_MAX = 256
DIFF_HEADS = 4
DIFF_HEAD_DIM = 64
NUM_BUCKETS = 32
MAX_DISTANCE = 128
N_ATTN_HEADS = C_HEADS + DIFF_HEADS
N_GROUPS = 4
EXPERTS_PER_GROUP = 8
N_EXPERTS = N_GROUPS * EXPERTS_PER_GROUP
TOP_E = 2
D_EXPERT = 512
MOE_BLOCK = 128
N_EVEN = (DEPTH + 1) // 2
N_ODD = DEPTH // 2

AB_SIZES = (A_WIDTH, A_WIDTH, A_WIDTH, B_WIDTH, B_WIDTH)
AB_IN = 3 * A_WIDTH + 2 * B_WIDTH
C_WIDTH = C_HEADS * C_HEAD_DIM
DIFF_QK = DIFF_HEADS * 2 * DIFF_HEAD_DIM
DIFF_V = DIFF_HEADS * 2 * DIFF_HEAD_DIM
CD_SIZES = (C_WIDTH, C_WIDTH, C_WIDTH, IDX_HEADS * IDX_DIM, IDX_DIM, IDX_HEADS, DIFF_QK, DIFF_QK, DIFF_V)
CD_IN = 3 * C_WIDTH + IDX_HEADS * IDX_DIM + IDX_DIM + IDX_HEADS + 2 * DIFF_QK + DIFF_V


def rmsnorm_2(x, g):
    xf = x.astype(jnp.float32)
    y = xf * lax.rsqrt(jnp.mean(xf * xf, axis=-1, keepdims=True) + EPS)
    return (y * g.astype(jnp.float32)).astype(x.dtype)

def layernorm(x, g, b):
    xf = x.astype(jnp.float32)
    mu = jnp.mean(xf, axis=-1, keepdims=True)
    var = jnp.mean(jnp.square(xf - mu), axis=-1, keepdims=True)
    y = (xf - mu) * lax.rsqrt(var + EPS) * g.astype(jnp.float32) + b.astype(jnp.float32)
    return y.astype(x.dtype)

def modulate(h, shift, scale):
    return h * (1 + scale[:, None, :]) + shift[:, None, :]

def split_cols_2(z, sizes):
    cuts = [int(v) for v in np.cumsum(sizes)[:-1]]
    return jnp.split(z, cuts, axis=-1)

def causal_depthwise_conv(u, w):
    width, ch = w.shape
    return lax.conv_general_dilated(u, w[:, None, :].astype(u.dtype), window_strides=(1,),
                                    padding=[(width - 1, 0)],
                                    dimension_numbers=('NWC', 'WIO', 'NWC'),
                                    feature_group_count=ch)

def rel_bucket(dist):
    max_exact = NUM_BUCKETS // 2
    n = jnp.maximum(dist, 0)
    log_ratio = jnp.log(jnp.maximum(n, 1).astype(jnp.float32) / max_exact) / math.log(MAX_DISTANCE / max_exact)
    large = max_exact + (log_ratio * (NUM_BUCKETS - max_exact)).astype(jnp.int32)
    return jnp.where(n < max_exact, n, jnp.minimum(large, NUM_BUCKETS - 1))

def conv_mixers(h, w_in, conv_a, conv_b, conv_b_bias, ln_g, ln_b, w_out):
    gate_b, gate_c, x_a, val_b, glu_gate = split_cols_2(h @ w_in, AB_SIZES)
    y_a = gate_b * causal_depthwise_conv(gate_c * x_a, conv_a)
    u = causal_depthwise_conv(val_b * jax.nn.sigmoid(glu_gate), conv_b) + conv_b_bias
    y_b = jax.nn.silu(layernorm(u, ln_g, ln_b))
    return jnp.concatenate([y_a, y_b], axis=-1) @ w_out

def attn_mixers(h, positions, w_in, rel_bias, diff_lam, diff_norm_g, w_out, lambda_init):
    bsz, seq, _ = h.shape
    n_blocks = seq // Q_BLOCK
    topk = min(TOPK_MAX, seq // 4)
    q_c, k_c, v_c, q_idx, k_idx, w_idx, q_d, k_d, v_d = split_cols_2(h @ w_in, CD_SIZES)
    q_c = q_c.reshape(bsz, seq, C_HEADS, C_HEAD_DIM)
    k_c = k_c.reshape(bsz, seq, C_HEADS, C_HEAD_DIM)
    v_c = v_c.reshape(bsz, seq, C_HEADS, C_HEAD_DIM)
    q_idx = q_idx.reshape(bsz, seq, IDX_HEADS, IDX_DIM)
    q_d = q_d.reshape(bsz, seq, DIFF_HEADS, 2, DIFF_HEAD_DIM)
    k_d = k_d.reshape(bsz, seq, DIFF_HEADS, 2, DIFF_HEAD_DIM)
    q1, q2 = q_d[..., 0, :], q_d[..., 1, :]
    k1, k2 = k_d[..., 0, :], k_d[..., 1, :]
    v_d = v_d.reshape(bsz, seq, DIFF_HEADS, 2 * DIFF_HEAD_DIM)
    lam_f = diff_lam.astype(jnp.float32)
    lam = jnp.exp(jnp.sum(lam_f[0] * lam_f[1])) - jnp.exp(jnp.sum(lam_f[2] * lam_f[3])) + lambda_init
    bias_c = rel_bias[:, :C_HEADS]
    bias_d = rel_bias[:, C_HEADS:]
    scale_c = C_HEAD_DIM ** -0.5
    scale_d = DIFF_HEAD_DIM ** -0.5
    scale_idx = (IDX_DIM * IDX_HEADS) ** -0.5
    gather_rows = jax.vmap(lambda a, i: a[i])

    def block(j):
        s0 = j * Q_BLOCK
        take = lambda a: lax.dynamic_slice_in_dim(a, s0, Q_BLOCK, axis=1)
        pos_q = take(positions)
        causal = positions[:, None, :] <= pos_q[:, :, None]
        rel = jnp.einsum('bqhd,bsd->bqhs', take(q_idx), k_idx)
        score = jnp.einsum('bqhs,bqh->bqs', jax.nn.relu(rel), take(w_idx)).astype(jnp.float32) * scale_idx
        score = jnp.where(causal, score, -jnp.inf)
        _, sel = lax.top_k(score, topk)
        k_sel = gather_rows(k_c, sel)
        v_sel = gather_rows(v_c, sel)
        pos_sel = gather_rows(positions, sel)
        dist_c = pos_q[:, :, None] - pos_sel
        logit_c = (jnp.einsum('bqhd,bqkhd->bhqk', take(q_c), k_sel).astype(jnp.float32) * scale_c
                   + jnp.moveaxis(bias_c[rel_bucket(dist_c)], -1, 1))
        logit_c = jnp.where((dist_c >= 0)[:, None], logit_c, -jnp.inf)
        p_c = jax.nn.softmax(logit_c, axis=-1).astype(v_sel.dtype)
        out_c = jnp.einsum('bhqk,bqkhd->bqhd', p_c, v_sel)
        dist_d = pos_q[:, :, None] - positions[:, None, :]
        b_d = jnp.moveaxis(bias_d[rel_bucket(dist_d)], -1, 1)
        mask_d = causal[:, None]

        def softmax_map(qb, kk):
            lg = jnp.einsum('bqhd,bshd->bhqs', qb, kk).astype(jnp.float32) * scale_d + b_d
            return jax.nn.softmax(jnp.where(mask_d, lg, -jnp.inf), axis=-1)

        attn = softmax_map(take(q1), k1) - lam * softmax_map(take(q2), k2)
        out_d = jnp.einsum('bhqs,bshd->bqhd', attn.astype(v_d.dtype), v_d)
        return out_c, out_d

    out_c, out_d = lax.map(block, jnp.arange(n_blocks))
    out_c = jnp.moveaxis(out_c, 0, 1).reshape(bsz, seq, C_WIDTH)
    out_d = jnp.moveaxis(out_d, 0, 1).reshape(bsz, seq, DIFF_HEADS, 2 * DIFF_HEAD_DIM)
    out_d = (rmsnorm_2(out_d, diff_norm_g) * (1 - lambda_init)).reshape(bsz, seq, DIFF_V)
    return jnp.concatenate([out_c, out_d], axis=-1) @ w_out

def hier_moe(h, wr_g, br_g, wr_e, br_e, w_gate, w_up, w_down):
    bsz, seq, d = h.shape
    n_tok = bsz * seq
    xf = h.reshape(n_tok, d)
    p_group = jax.nn.softmax((xf @ wr_g + br_g).astype(jnp.float32), axis=-1)
    p_top, g_sel = lax.top_k(p_group, 1)
    fine = (xf @ wr_e + br_e).astype(jnp.float32).reshape(n_tok, N_GROUPS, EXPERTS_PER_GROUP)
    fine = jnp.take_along_axis(fine, g_sel[:, :, None], axis=1)[:, 0]
    e_val, e_sel = lax.top_k(fine, TOP_E)
    gate = (p_top * jax.nn.softmax(e_val, axis=-1)).reshape(-1)
    expert_id = (g_sel * EXPERTS_PER_GROUP + e_sel).reshape(-1)
    token_id = jnp.repeat(jnp.arange(n_tok, dtype=jnp.int32), TOP_E)
    n_assign = n_tok * TOP_E
    order = jnp.argsort(expert_id)
    e_sorted = expert_id[order]
    counts = jnp.bincount(expert_id, length=N_EXPERTS)
    starts = jnp.cumsum(counts) - counts
    padded = (counts + MOE_BLOCK - 1) // MOE_BLOCK * MOE_BLOCK
    pad_end = jnp.cumsum(padded)
    pad_start = pad_end - padded
    dest = pad_start[e_sorted] + jnp.arange(n_assign, dtype=jnp.int32) - starts[e_sorted]
    n_blocks = -(-n_assign // MOE_BLOCK) + N_EXPERTS
    n_rows = n_blocks * MOE_BLOCK
    row_token = jnp.full((n_rows,), n_tok, jnp.int32).at[dest].set(token_id[order])
    row_gate = jnp.zeros((n_rows,), gate.dtype).at[dest].set(gate[order])
    block_expert = jnp.minimum(jnp.searchsorted(pad_end, jnp.arange(n_blocks, dtype=jnp.int32) * MOE_BLOCK, side='right'),
                               N_EXPERTS - 1)
    x_rows = jnp.concatenate([xf, jnp.zeros((1, d), xf.dtype)], axis=0)[row_token].reshape(n_blocks, MOE_BLOCK, d)

    def expert_block(args):
        xb, e = args
        return (jax.nn.silu(xb @ w_gate[e]) * (xb @ w_up[e])) @ w_down[e]

    y_rows = lax.map(expert_block, (x_rows, block_expert)).reshape(n_rows, d)
    y_rows = y_rows * row_gate[:, None].astype(y_rows.dtype)
    out = jnp.zeros((n_tok + 1, d), y_rows.dtype).at[row_token].add(y_rows)[:n_tok]
    return out.reshape(bsz, seq, d)

def second_inputs(seed: int = 0) -> dict:
    key = jax.random.key(seed)
    ks = jax.random.split(key, 32)
    f32 = jnp.float32

    def nrm(k, shape, scale):
        return jax.random.normal(k, shape, f32) * scale

    return {
        'x': nrm(ks[0], (BATCH, SEQ, D_MODEL), 1.0),
        'c': nrm(ks[1], (BATCH, D_MODEL), 1.0),
        'positions': jnp.broadcast_to(jnp.arange(SEQ, dtype=jnp.int32), (BATCH, SEQ)),
        'rel_bias': nrm(ks[2], (NUM_BUCKETS, N_ATTN_HEADS), 0.5),
        'norm_g': 1.0 + nrm(ks[3], (DEPTH, 2, D_MODEL), 0.1),
        'final_norm_g': 1.0 + nrm(ks[4], (D_MODEL,), 0.1),
        'ada_w': nrm(ks[5], (DEPTH, D_MODEL, 6 * D_MODEL), 0.5 * D_MODEL ** -0.5),
        'ada_b': nrm(ks[6], (DEPTH, 6 * D_MODEL), 0.02),
        'ab_w_in': nrm(ks[7], (N_EVEN, D_MODEL, AB_IN), D_MODEL ** -0.5),
        'ab_conv_a': nrm(ks[8], (N_EVEN, A_CONV, A_WIDTH), A_CONV ** -0.5),
        'ab_conv_b': nrm(ks[9], (N_EVEN, B_CONV, B_WIDTH), B_CONV ** -0.5),
        'ab_conv_b_bias': nrm(ks[10], (N_EVEN, B_WIDTH), 0.02),
        'ab_ln_g': 1.0 + nrm(ks[11], (N_EVEN, B_WIDTH), 0.1),
        'ab_ln_b': nrm(ks[12], (N_EVEN, B_WIDTH), 0.02),
        'ab_w_out': nrm(ks[13], (N_EVEN, A_WIDTH + B_WIDTH, D_MODEL), (A_WIDTH + B_WIDTH) ** -0.5),
        'cd_w_in': nrm(ks[14], (N_ODD, D_MODEL, CD_IN), D_MODEL ** -0.5),
        'diff_lam': nrm(ks[15], (N_ODD, 4, DIFF_HEAD_DIM), 0.1),
        'diff_norm_g': 1.0 + nrm(ks[16], (N_ODD, 2 * DIFF_HEAD_DIM), 0.1),
        'cd_w_out': nrm(ks[17], (N_ODD, C_WIDTH + DIFF_V, D_MODEL), (C_WIDTH + DIFF_V) ** -0.5),
        'moe_wr_g': nrm(ks[18], (DEPTH, D_MODEL, N_GROUPS), D_MODEL ** -0.5),
        'moe_br_g': nrm(ks[19], (DEPTH, N_GROUPS), 0.01),
        'moe_wr_e': nrm(ks[20], (DEPTH, D_MODEL, N_EXPERTS), D_MODEL ** -0.5),
        'moe_br_e': nrm(ks[21], (DEPTH, N_EXPERTS), 0.01),
        'moe_w_gate': nrm(ks[22], (DEPTH, N_EXPERTS, D_MODEL, D_EXPERT), D_MODEL ** -0.5),
        'moe_w_up': nrm(ks[23], (DEPTH, N_EXPERTS, D_MODEL, D_EXPERT), D_MODEL ** -0.5),
        'moe_w_down': nrm(ks[24], (DEPTH, N_EXPERTS, D_EXPERT, D_MODEL), D_EXPERT ** -0.5),
    }

def second_block(x, c, positions, rel_bias, norm_g, final_norm_g, ada_w, ada_b,
              ab_w_in, ab_conv_a, ab_conv_b, ab_conv_b_bias, ab_ln_g, ab_ln_b, ab_w_out,
              cd_w_in, diff_lam, diff_norm_g, cd_w_out,
              moe_wr_g, moe_br_g, moe_wr_e, moe_br_e, moe_w_gate, moe_w_up, moe_w_down):
    cond = jax.nn.silu(c)
    for i in range(DEPTH):
        mod = cond @ ada_w[i] + ada_b[i]
        sh1, sc1, g1, sh2, sc2, g2 = jnp.split(mod, 6, axis=-1)
        h = modulate(rmsnorm_2(x, norm_g[i, 0]), sh1, sc1)
        j = i // 2
        if i % 2 == 0:
            y = conv_mixers(h, ab_w_in[j], ab_conv_a[j], ab_conv_b[j], ab_conv_b_bias[j],
                            ab_ln_g[j], ab_ln_b[j], ab_w_out[j])
        else:
            lambda_init = 0.8 - 0.6 * math.exp(-0.3 * i)
            y = attn_mixers(h, positions, cd_w_in[j], rel_bias, diff_lam[j], diff_norm_g[j],
                            cd_w_out[j], lambda_init)
        x = x + g1[:, None, :] * y
        h = modulate(rmsnorm_2(x, norm_g[i, 1]), sh2, sc2)
        x = x + g2[:, None, :] * hier_moe(h, moe_wr_g[i], moe_br_g[i], moe_wr_e[i], moe_br_e[i],
                                          moe_w_gate[i], moe_w_up[i], moe_w_down[i])
    return rmsnorm_2(x, final_norm_g)


def setup_inputs(seed=0):
    out = dict(first_inputs(seed))
    for name, value in second_inputs(seed + 1).items():
        if name != "x":
            out[name + "_2"] = value
    return out


def reference(
    x, norm_g, w_in, mla_qa_g, mla_w_uq, mla_kva_g, mla_w_ukv, mla_q_g, mla_knope_g,
    mla_krope_g, fox_b_f, fox_q_g, fox_k_g, rwkv_mu, rwkv_w0, rwkv_w_up, rwkv_a0, rwkv_a_up,
    rwkv_k_k, rwkv_k_a, rwkv_r_k, rwkv_lnx_g, rwkv_lnx_b, rwkv_v0, rwkv_v_down, rwkv_v_up, w_pa,
    w_pb, w_pc, w_out, c_2, positions_2, rel_bias_2, norm_g_2, final_norm_g_2, ada_w_2, ada_b_2,
    ab_w_in_2, ab_conv_a_2, ab_conv_b_2, ab_conv_b_bias_2, ab_ln_g_2, ab_ln_b_2, ab_w_out_2,
    cd_w_in_2, diff_lam_2, diff_norm_g_2, cd_w_out_2, moe_wr_g_2, moe_br_g_2, moe_wr_e_2,
    moe_br_e_2, moe_w_gate_2, moe_w_up_2, moe_w_down_2,
):
    x = first_block(
        x, norm_g, w_in, mla_qa_g, mla_w_uq, mla_kva_g, mla_w_ukv, mla_q_g, mla_knope_g,
        mla_krope_g, fox_b_f, fox_q_g, fox_k_g, rwkv_mu, rwkv_w0, rwkv_w_up, rwkv_a0, rwkv_a_up,
        rwkv_k_k, rwkv_k_a, rwkv_r_k, rwkv_lnx_g, rwkv_lnx_b, rwkv_v0, rwkv_v_down, rwkv_v_up,
        w_pa, w_pb, w_pc, w_out,
    )
    return second_block(
        x, c_2, positions_2, rel_bias_2, norm_g_2, final_norm_g_2, ada_w_2, ada_b_2, ab_w_in_2,
        ab_conv_a_2, ab_conv_b_2, ab_conv_b_bias_2, ab_ln_g_2, ab_ln_b_2, ab_w_out_2, cd_w_in_2,
        diff_lam_2, diff_norm_g_2, cd_w_out_2, moe_wr_g_2, moe_br_g_2, moe_wr_e_2, moe_br_e_2,
        moe_w_gate_2, moe_w_up_2, moe_w_down_2,
    )


_drawn_inputs = setup_inputs


def setup_inputs(seed=0):
    import zlib

    import numpy as np

    out = dict(_drawn_inputs(seed))
    spreads = {}
    factors = {'mla_qa_g': 8.0,
     'mla_kva_g': 8.0,
     'mla_q_g': 8.0,
     'mla_knope_g': 8.0,
     'mla_krope_g': 8.0,
     'fox_q_g': 8.0,
     'fox_k_g': 8.0,
     'rwkv_k_k': 3.587,
     'rwkv_lnx_g': 4.075,
     'rwkv_lnx_b': 4.476,
     'ab_conv_b_bias_2': 8.0,
     'ab_ln_g_2': 14.773,
     'ab_ln_b_2': 64.0,
     'diff_lam_2': 2.983,
     'diff_norm_g_2': 15.286,
     'moe_br_g_2': 64.0,
     'moe_br_e_2': 64.0,
     'rel_bias_2': 3.773,
     'norm_g_2': 2.727,
     'ada_b_2': 3.682}
    for name, (base, spread) in spreads.items():
        noise = np.random.default_rng([zlib.crc32(name.encode()), seed]).standard_normal(out[name].shape)
        drawn = base * np.exp(spread * noise) if base else spread * noise
        out[name] = jnp.asarray(drawn.astype(out[name].dtype))
    for name, factor in factors.items():
        out[name] = (out[name] * factor).astype(out[name].dtype)
    return out
```

```python
from contextlib import ExitStack, contextmanager

import numpy as np

import concourse.bass as bass
from concourse import mybir

F32 = mybir.dt.float32
I32 = mybir.dt.int32
ALU = mybir.AluOpType
ACT = mybir.ActivationFunctionType
AX = mybir.AxisListType

P = 128
SEQ = 512
TILES = SEQ // P
D = 1024
DC = D // P
DEPTH = 2
BANK = 512

HEADS = 8
NOPE, ROPE, V_A, Q_LORA, KV_LORA = 64, 32, 64, 256, 128
HD = 64
QK_A = NOPE + ROPE
W = HEADS * HD
WC = W // P
SHIFT = 3 * W + 2 * HD
MV = 32
DECAY = 0.606531
GN_EPS = 64e-5
EPS = 1e-6
MASKED = -1e30
CH = 64
NCH = SEQ // CH
SUB = 16

COL = {}
_at = 0
for _name, _n in (("cq", Q_LORA), ("ckv", KV_LORA), ("kr", ROPE), ("gate_a", W), ("fq", W), ("fk", W), ("fv", W),
                  ("ff", HEADS), ("gate_b", W), ("shift", SHIFT), ("gate_c", W), ("ga", D), ("gb", D), ("gc", D)):
    COL[_name] = _at
    _at += _n
IN_COLS = _at


class Count:

    def __init__(self, sem):
        self.sem, self.base, self.total = sem, 0, 0

    def at(self, n):
        return self.sem, self.base + n

    def inc(self, n=1, times=1):
        self.total += n * times
        return self.sem, n


class Chip:

    def __init__(self, nc, ctx):
        self.nc, self.ctx = nc, ctx
        self.free, self.made = [], 0
        self.bank = [ctx.enter_context(nc.psum_tensor(f"bank{i}", [P, BANK], F32)) for i in range(8)]

    def name_tables(self, t):
        self.ident, self.causal_add, self.ones, self.head_ones = t["ident"], t["causal_add"], t["ones"], t["head_ones"]
        self.chunk_masks = t["chunk_masks"].rearrange("p (n t) -> p n t", n=4)
        self.sub_lower, self.sub_upper, self.off_sub = t["sub_lower"], t["sub_upper"], t["off_sub"]
        self.chunk_keep, self.bucket_from, self.rank8 = t["chunk_keep"], t["bucket_from"], t["rank8"]
        self.cos = t["cos"].rearrange("p (t d) -> p t d", t=TILES)
        self.sin = t["sin"].rearrange("p (t d) -> p t d", t=TILES)

    def sb(self, name, shape, dt=F32):
        return self.ctx.enter_context(self.nc.sbuf_tensor(name, shape, dt))

    @contextmanager
    def stage(self, name):
        st = Stage(self, name)
        with ExitStack() as ctx:
            st.ctx = ctx
            st.block = ctx.enter_context(self.nc.Block())
            yield st
        for c in st.counts:
            c.base += c.total
            c.total = 0
            self.free.append(c)


class Stage:
    serial = 0

    def __init__(self, chip, name):
        self.chip, self.name, self.counts = chip, name, []
        Stage.serial += 1
        self.id = Stage.serial

    def sb(self, name, shape, dt=F32):
        return self.ctx.enter_context(self.chip.nc.sbuf_tensor(f"{name}_{self.id}", shape, dt))

    def count(self, name):
        if self.chip.free:
            c = self.chip.free.pop(0)
        else:
            self.chip.made += 1
            c = Count(self.chip.ctx.enter_context(self.chip.nc.semaphore(f"count{self.chip.made}")))
        self.counts.append(c)
        return c

    def chain(self, eng, name):
        c, n = self.count(name), [0]

        def link(ins):
            n[0] += 1
            ins.then_inc(*c.inc())
            eng.wait_ge(*c.at(n[0]))
        return link


def product(pe, out, pairs):
    for n, (lhsT, rhs) in enumerate(pairs):
        last = pe.matmul(out, lhsT, rhs, start=(n == 0), stop=(n == len(pairs) - 1))
    return last


def over(ap, shape, axis):
    return ap.unsqueeze(axis).to_broadcast(shape)


def gemm(chip, name, loads, jobs, slots=3):
    with chip.stage(name) as st:
        weights = [st.sb(f"w{i}", [P, DC * 512]) for i in range(min(slots, len(loads)))]
        n_slots = len(weights)
        loaded = [st.count("weights_loaded") for _ in weights]
        summed = st.count("sums_ready")
        freed = {"act": st.count("bank_freed_by_act"), "dve": st.count("bank_freed_by_dve")}
        last_job = {}
        for g, job in enumerate(jobs):
            last_job[job[0]] = g

        @st.block.sync
        def _(sp):
            for i, load in enumerate(loads):
                if i >= n_slots:
                    sp.wait_ge(*summed.at(last_job[i - n_slots] + 1))
                dst, src = load(weights[i % n_slots])
                sp.dma_start(dst, src).then_inc(*loaded[i % n_slots].inc(16))

        @st.block.tensor
        def _(pe):
            for g, (load, pairs, out, eng, _) in enumerate(jobs):
                if g >= 8:
                    who = jobs[g - 8][3]
                    pe.wait_ge(*freed[who].at(sum(j[3] == who for j in jobs[:g - 7])))
                if load is not None:
                    pe.wait_ge(*loaded[load % n_slots].at(16 * (load // n_slots + 1)))
                w = weights[load % n_slots] if load is not None else None
                product(pe, out(chip.bank[g % 8]), pairs(w)).then_inc(*summed.inc())

        def evacuate(eng, who):
            for g, (_, _, out, e, fn) in enumerate(jobs):
                if e == who:
                    eng.wait_ge(*summed.at(g + 1))
                    fn(eng, out(chip.bank[g % 8])).then_inc(*freed[who].inc())

        @st.block.scalar
        def _(act):
            evacuate(act, "act")

        @st.block.vector
        def _(dve):
            evacuate(dve, "dve")



class Roots:

    def __init__(self, st):
        self.asked, self.rooted = st.count("square_ready"), st.count("root_ready")
        self.n = self.served = 0

    def serve(self, act, ap, factor=1.0):
        self.served += 1
        act.wait_ge(*self.asked.at(self.served))
        act.activation(ap, ap, ACT.Sqrt, scale=factor ** -2).then_inc(*self.rooted.inc())

    def __call__(self, dve, link, ap, ins):
        self.n += 1
        ins.then_inc(*self.asked.inc())
        dve.wait_ge(*self.rooted.at(self.n))
        link(dve.reciprocal(ap, ap))


def group_rms(dve, link, root, out, x, sq, r, n, gain=None):
    shape = list(x.shape)
    link(dve.tensor_tensor(sq, x, x, ALU.mult))
    link(dve.tensor_reduce(r, sq, AX.X, ALU.add))
    root(dve, link, r, dve.tensor_scalar(r, r, 1.0 / n, EPS, ALU.mult, ALU.add))
    link(dve.tensor_tensor(out, x, over(r, shape, 2), ALU.mult))
    if gain is not None:
        link(dve.tensor_tensor(out, out, over(gain, shape, 1), ALU.mult))


def rotate(dve, link, x, cos, sin, tmp, heads):
    h = ROPE // 2
    shape = [P, TILES, heads, h]
    c, s = over(cos, shape, 2), over(sin, shape, 2)
    x1, x2 = x[:, :, :, 0:h], x[:, :, :, h:ROPE]
    t = [tmp[:, i].rearrange("p (t h d) -> p t h d", t=TILES, h=heads) for i in range(4)]
    for i, (a, b) in enumerate(((x1, c), (x2, s), (x2, c), (x1, s))):
        ins = dve.tensor_tensor(t[i], a, b, ALU.mult)
        link(ins)
    link(dve.tensor_tensor(x1, t[0], t[1], ALU.subtract))
    link(dve.tensor_tensor(x2, t[2], t[3], ALU.add))



def norm_to_fm(chip, x, fm, finish, rows=None):
    with chip.stage("norm") as st:
        xn = st.sb("xn", [P, TILES, D])
        ss = st.sb("ss", [P, TILES])
        squared, normed = st.count("squares_summed"), st.count("tile_normed")
        turned, moved = st.count("chunk_transposed"), st.count("chunk_moved")

        root = Roots(st)

        @st.block.scalar
        def _(act):
            for t in range(TILES):
                act.activation(xn[:, t, :], x[:, t, :], ACT.Square, accum_out=ss[:, t:t + 1]).then_inc(*squared.inc())
            root.serve(act, ss[:, :])
            for c in range(DC):
                act.wait_ge(*turned.at(c + 1))
                finish(act, fm[:, c, :], chip.bank[c % 4][:, :], c).then_inc(*moved.inc())

        @st.block.vector
        def _(dve):
            link = st.chain(dve, "norm_step")
            dve.wait_ge(*squared.at(TILES))
            root(dve, link, ss[:, :], dve.tensor_scalar(ss[:, :], ss[:, :], 1.0 / D, EPS, ALU.mult, ALU.add))
            for t in range(TILES):
                if rows is None:
                    dve.tensor_scalar(xn[:, t, :], x[:, t, :], ss[:, t:t + 1], None, ALU.mult).then_inc(*normed.inc())
                else:
                    link(dve.scalar_tensor_tensor(xn[:, t, :], x[:, t, :], ss[:, t:t + 1], rows[0], ALU.mult, ALU.mult))
                    dve.tensor_tensor(xn[:, t, :], xn[:, t, :], rows[1], ALU.add).then_inc(*normed.inc())

        @st.block.tensor
        def _(pe):
            pe.wait_ge(*normed.at(TILES))
            for c in range(DC):
                if c >= 4:
                    pe.wait_ge(*moved.at(c - 3))
                for t in range(TILES):
                    last = pe.transpose(chip.bank[c % 4][:, t * P:(t + 1) * P], xn[:, t, c * P:(c + 1) * P], chip.ident)
                last.then_inc(*turned.inc())


def cols_of(dram, c0, n):
    kc = dram.shape[0] // P

    def load(slot):
        return slot[:, 0:kc * n].rearrange("p (k n) -> p k n", k=kc), dram[:, c0:c0 + n].rearrange("(k p) n -> p k n", p=P)
    return load


def tm_jobs(load, act_fm, kc, n, c0, cn, evac, start=0):
    jobs = []
    for t in range(TILES):
        def pairs(w, t=t):
            wv = w[:, 0:kc * n].rearrange("p (k n) -> p k n", k=kc)
            return [(act_fm[:, k, t * P:(t + 1) * P], wv[:, k, c0:c0 + cn]) for k in range(kc)]
        eng = "act" if t % 2 else "dve"
        jobs.append((load, pairs, lambda b, cn=cn: b[:, 0:cn], eng, evac(t)))
    return jobs


def fm_job(load, act_fm, kc, n, c0, cn, eng, evac):
    def pairs(w):
        wv = w[:, 0:kc * n].rearrange("p (k n) -> p k n", k=kc)
        return [(wv[:, k, c0:c0 + cn], act_fm[:, k, :]) for k in range(kc)]
    return (load, pairs, lambda b, cn=cn: b[0:cn, :], eng, evac)


def copy_to(dst):
    def fn(eng, psum):
        if eng.engine == mybir.EngineType.DVE:
            return eng.tensor_copy(dst, psum)
        return eng.activation(dst, psum, ACT.Copy)
    return fn


def project_fm(chip, name, act_fm, dram, c0, chunks, evac_of, eng="act"):
    kc = dram.shape[0] // P
    loads, jobs = [], []
    for c in range(0, chunks, 4):
        n = min(4, chunks - c) * P
        loads.append(cols_of(dram, c0 + c * P, n))
        for i in range(n // P):
            e = eng(c + i) if callable(eng) else eng
            jobs.append(fm_job(len(loads) - 1, act_fm, kc, n, i * P, P, e, evac_of(c + i)))
    gemm(chip, name, loads, jobs)


def attention(chip, name, q, k, v, dk, out_fm, gate, dv=HD, heads=HEADS, causal=True, scale=1.0, bias=None, masks=None):
    steps = heads * TILES
    with chip.stage(name) as st:
        qT = [st.sb(f"qT{i}", [dk, SEQ]) for i in range(2)]
        kT = [st.sb(f"kT{i}", [dk, SEQ]) for i in range(2)]
        prob = [st.sb(f"prob{i}", [P, SEQ]) for i in range(4)]
        pT = [st.sb(f"pT{i}", [P, TILES, SEQ]) for i in range(2)]
        nmax, sums = st.sb("nmax", [P, steps]), st.sb("sums", [P, steps])
        if bias is not None:
            bias_sb = [st.sb(f"bias{i}", [P, TILES, SEQ]) for i in range(2)]
            loaded = [st.count(f"bias{i}_loaded") for i in range(2)]
            parts = len(bias(0))
        turned, qmoved, kmoved = st.count("qk_transposed"), st.count("q_moved"), st.count("k_moved")
        scored, maxed, exped = st.count("scored"), st.count("max_found"), st.count("exp_done")
        normed, pturned, pmoved = st.count("probs_normed"), st.count("probs_transposed"), st.count("probs_moved")
        summed, stored = st.count("head_summed"), st.count("head_stored")
        B = chip.bank
        width = [(i + 1) * P if causal else SEQ for i in range(TILES)]

        if bias is not None:
            @st.block.sync
            def _(sp):
                for h in range(heads):
                    if h >= 2:
                        sp.wait_ge(*maxed.at(TILES * (h - 1)))
                    for dst, src in bias(h):
                        sp.dma_start(dst(bias_sb[h % 2]), src).then_inc(*loaded[h % 2].inc(16))

        @st.block.tensor
        def _(pe):
            def transpose_qk(h):
                if h >= 1:
                    pe.wait_ge(*qmoved.at(h))
                    pe.wait_ge(*kmoved.at(h))
                for t in range(TILES):
                    pe.transpose(B[0][0:dk, t * P:(t + 1) * P], q[:, t, h, :], chip.ident)
                    last = pe.transpose(B[1][0:dk, t * P:(t + 1) * P], k[:, t, h, :], chip.ident)
                last.then_inc(*turned.inc())

            def score(s):
                h, i = divmod(s, TILES)
                if i == 0:
                    pe.wait_ge(*qmoved.at(h + 1))
                    pe.wait_ge(*kmoved.at(h + 1))
                if s >= 2:
                    pe.wait_ge(*exped.at(s - 1))
                pe.matmul(B[2 + s % 2][:, 0:width[i]], qT[h % 2][:, i * P:(i + 1) * P], kT[h % 2][:, 0:width[i]],
                          start=True, stop=True).then_inc(*scored.inc())

            def transpose_probs(s):
                pe.wait_ge(*normed.at(s + 1))
                if s >= 2:
                    pe.wait_ge(*pmoved.at(s - 1))
                for j in range(width[s % TILES] // P):
                    last = pe.transpose(B[4 + s % 2][:, j * P:(j + 1) * P], prob[s % 4][:, j * P:(j + 1) * P], chip.ident)
                last.then_inc(*pturned.inc())

            def weigh(h):
                pe.wait_ge(*pmoved.at(TILES * (h + 1)))
                if h >= 2:
                    pe.wait_ge(*stored.at(h - 1))
                for j in range(TILES):
                    a = j * P if causal else 0
                    p0 = out_fm(h).base_partition()
                    last = pe.matmul(B[6 + h % 2][p0:p0 + dv, a:SEQ], v(h, j), pT[h % 2][:, j, a:SEQ],
                                     start=(j == 0), stop=(j == TILES - 1))
                last.then_inc(*summed.inc())

            transpose_qk(0)
            for s in range(steps + 3):
                if s < steps:
                    score(s)
                    if s % TILES == 1 and s // TILES + 1 < heads:
                        transpose_qk(s // TILES + 1)
                if 2 <= s < steps + 2:
                    transpose_probs(s - 2)
                if s >= 3 and (s - 3) % TILES == TILES - 1:
                    weigh((s - 3) // TILES)

        @st.block.scalar
        def _(act):
            def move_q(h):
                act.wait_ge(*turned.at(h + 1))
                if h >= 2:
                    act.wait_ge(*scored.at(TILES * (h - 1)))
                act.activation(qT[h % 2][:, :], B[0][0:dk, :], ACT.Copy).then_inc(*qmoved.inc())

            move_q(0)
            for s in range(steps + 2):
                if s < steps:
                    act.wait_ge(*maxed.at(s + 1))
                    if s >= 4:
                        act.wait_ge(*pturned.at(s - 3))
                    n = width[s % TILES]
                    src = B[2 + s % 2][:, 0:n]
                    act.activation(prob[s % 4][:, 0:n], src, ACT.Exp, bias=nmax[:, s:s + 1],
                                   accum_out=sums[:, s:s + 1]).then_inc(*exped.inc())
                    if s % TILES == 1 and s // TILES + 1 < heads:
                        move_q(s // TILES + 1)
                if s >= 2:
                    h, i = divmod(s - 2, TILES)
                    n = width[i]
                    act.wait_ge(*pturned.at(s - 1))
                    if h >= 2:
                        act.wait_ge(*summed.at(h - 1))
                    act.activation(pT[h % 2][:, 0:n // P, i * P:(i + 1) * P],
                                   B[4 + s % 2][:, 0:n].rearrange("p (j q) -> p j q", q=P), ACT.Copy).then_inc(*pmoved.inc())

        @st.block.vector
        def _(dve):
            link = st.chain(dve, "softmax_step")

            def move_k(h):
                dve.wait_ge(*turned.at(h + 1))
                if h >= 2:
                    dve.wait_ge(*scored.at(TILES * (h - 1)))
                dve.tensor_copy(kT[h % 2][:, :], B[1][0:dk, :]).then_inc(*kmoved.inc())

            def find_max(s):
                h, i = divmod(s, TILES)
                n = width[i]
                dve.wait_ge(*scored.at(s + 1))
                bank = B[2 + s % 2]
                if bias is None:
                    diag = bank[:, n - P:n]
                    link(dve.tensor_tensor(diag, diag, chip.causal_add, ALU.add))
                else:
                    if i == 0:
                        dve.wait_ge(*loaded[h % 2].at(16 * parts * (h // 2 + 1)))
                    link(dve.scalar_tensor_tensor(bank[:, :], bank[:, :], scale, bias_sb[h % 2][:, i, :], ALU.mult, ALU.add))
                    link(dve.tensor_tensor(bank[:, :], bank[:, :], masks[:, i, :], ALU.add))
                dve.tensor_reduce(nmax[:, s:s + 1], bank[:, 0:n], AX.X, ALU.max, negate=True).then_inc(*maxed.inc())

            def norm(s):
                n = width[s % TILES]
                dve.wait_ge(*exped.at(s + 1))
                link(dve.reciprocal(sums[:, s:s + 1], sums[:, s:s + 1]))
                dve.tensor_scalar(prob[s % 4][:, 0:n], prob[s % 4][:, 0:n], sums[:, s:s + 1], None,
                                  ALU.mult).then_inc(*normed.inc())

            def store(h):
                dve.wait_ge(*summed.at(h + 1))
                o = out_fm(h)
                src = B[6 + h % 2][o.base_partition():o.base_partition() + dv, :]
                if gate is None:
                    dve.tensor_copy(o, src).then_inc(*stored.inc())
                else:
                    dve.tensor_tensor(o, src, gate(h), ALU.mult).then_inc(*stored.inc())

            move_k(0)
            for s in range(steps + 4):
                if s < steps:
                    find_max(s)
                    if s % TILES == 1 and s // TILES + 1 < heads:
                        move_k(s // TILES + 1)
                if 1 <= s < steps + 1:
                    norm(s - 1)
                if s >= 3 and (s - 3) % TILES == TILES - 1 and s - 3 < steps:
                    store((s - 3) // TILES)


def head_rows(fm):
    return lambda h: fm[HD * (h % 2):HD * (h % 2) + HD, h // 2, :]


def merge(chip, l, io, fm, o_fm, c0, w_p, merged, first):
    with ExitStack() as ctx:
        sg = ctx.enter_context(chip.nc.sbuf_tensor(f"merge_gate_{l}_{c0}", [P, DC, SEQ], F32))

        def sigmoid_of(c):
            return lambda act, ps: act.activation(sg[:, c, :], ps, ACT.Sigmoid)
        project_fm(chip, "merge_gate", fm, io["w_in"][l], c0, DC, sigmoid_of)

        def times_gate(c):
            dst = merged if first else sg
            return lambda dve, ps: dve.tensor_tensor(dst[:, c, :], ps, sg[:, c, :], ALU.mult)
        project_fm(chip, "merge_product", o_fm, w_p, 0, DC, times_gate, eng="dve")
        if not first:
            with chip.stage("merge_sum") as st:
                @st.block.vector
                def _(dve):
                    dve.tensor_tensor(merged[:, :, :], merged[:, :, :], sg[:, :, :], ALU.add)


def silu_gate(chip, fm, dram, c0, gate):
    project_fm(chip, "gate", fm, dram, c0, WC, lambda c: lambda act, ps: act.activation(gate[:, c, :], ps, ACT.Silu))



def mla(chip, l, io, par, row, fm, o_fm):
    with ExitStack() as ctx:
        def sb(name, shape):
            return ctx.enter_context(chip.nc.sbuf_tensor(f"mla_{name}_{l}", shape, F32))
        w_in = io["w_in"][l]
        n_in = Q_LORA + KV_LORA + ROPE
        gate = sb("gate", [P, WC, SEQ])
        silu_gate(chip, fm, w_in, COL["gate_a"], gate)
        q, k = sb("q", [P, TILES, HEADS, QK_A]), sb("k", [P, TILES, HEADS, QK_A])
        v = sb("v", [P, TILES, HEADS, V_A])
        with ExitStack() as inner:
            def sbi(name, shape):
                return inner.enter_context(chip.nc.sbuf_tensor(f"mla_{name}_{l}", shape, F32))
            low = sbi("low", [P, TILES, n_in])
            cqT, ckvT = sbi("cqT", [P, 2, SEQ]), sbi("ckvT", [P, 1, SEQ])
            tmp, ss = sbi("tmp", [P, TILES, HEADS * QK_A]), sbi("ss", [P, TILES * HEADS])
            gemm(chip, "mla_low", [cols_of(w_in, 0, n_in)],
                 tm_jobs(0, fm, DC, n_in, 0, n_in, lambda t: copy_to(low[:, t, :])))
            with chip.stage("mla_norm") as st:
                normed, turned = st.count("low_normed"), st.count("low_transposed")
                root = Roots(st)

                @st.block.vector
                def _(dve):
                    link = st.chain(dve, "norm_step")
                    for a, n in ((0, Q_LORA), (Q_LORA, KV_LORA), (Q_LORA + KV_LORA, ROPE)):
                        gain = row("krope_g") if n == ROPE else None
                        group_rms(dve, link, root, low[:, :, a:a + n], low[:, :, a:a + n], tmp[:, :, 0:n], ss[:, 0:TILES], n, gain)
                    kr = low[:, :, Q_LORA + KV_LORA:n_in].unsqueeze(2)
                    rotate(dve, link, kr, chip.cos, chip.sin, tmp[:, :, 0:TILES * ROPE // 2], 1)
                    dve.tensor_copy(k[:, :, :, NOPE:QK_A],
                                    low[:, :, Q_LORA + KV_LORA:n_in].unsqueeze(2).to_broadcast([P, TILES, HEADS, ROPE])
                                    ).then_inc(*normed.inc())

                @st.block.tensor
                def _(pe):
                    pe.wait_ge(*normed.at(1))
                    for c in range(3):
                        for t in range(TILES):
                            last = pe.transpose(chip.bank[c][:, t * P:(t + 1) * P], low[:, t, c * P:(c + 1) * P], chip.ident)
                        last.then_inc(*turned.inc())

                @st.block.scalar
                def _(act):
                    for _ in range(3):
                        root.serve(act, ss[:, 0:TILES])
                    for c in range(3):
                        act.wait_ge(*turned.at(c + 1))
                        dst, gain = (cqT[:, c, :], par("qa_g", c)) if c < 2 else (ckvT[:, 0, :], par("kva_g", 0))
                        act.activation(dst, chip.bank[c][:, :], ACT.Copy, scale=gain)

            half = HEADS * QK_A // 2
            loads = [cols_of(io["mla_w_uq"][l], 0, 2 * half)] + [cols_of(io["mla_w_ukv"][l], 0, 2 * BANK)]
            jobs = []
            for c in range(2):
                jobs += tm_jobs(0, cqT, 2, 2 * half, c * half, half,
                                lambda t, c=c: copy_to(q[:, t, :, :].rearrange("p h d -> p (h d)")[:, c * half:(c + 1) * half]))
            for c in range(2):
                def pairs_of(t, c):
                    def pairs(w):
                        return [(ckvT[:, 0, t * P:(t + 1) * P], w[:, c * BANK:(c + 1) * BANK])]
                    return pairs
                for t in range(TILES):
                    def split(eng, ps, t=t, c=c):
                        kv = ps.rearrange("p (h d) -> p h d", h=4)
                        eng.tensor_copy(k[:, t, 4 * c:4 * c + 4, 0:NOPE], kv[:, :, 0:NOPE])
                        return eng.tensor_copy(v[:, t, 4 * c:4 * c + 4, :], kv[:, :, NOPE:2 * NOPE])
                    jobs.append((1, pairs_of(t, c), lambda b: b[:, :], "dve", split))
            gemm(chip, "mla_up", loads, jobs)
            with chip.stage("mla_heads") as st:
                root = Roots(st)

                @st.block.scalar
                def _(act):
                    root.serve(act, ss[:, :], QK_A ** -0.5)
                    root.serve(act, ss[:, :])

                @st.block.vector
                def _(dve):
                    link = st.chain(dve, "heads_step")
                    G = TILES * HEADS
                    qg = q[:, :, :, :].rearrange("p t h d -> p (t h) d")
                    kg = k[:, :, :, :].rearrange("p t h d -> p (t h) d")[:, :, 0:NOPE]
                    t96 = tmp[:, :, :].rearrange("p t (h d) -> p (t h) d", h=HEADS)
                    group_rms(dve, link, root, qg, qg, t96, ss[:, :], QK_A, row("q_g"))
                    rotate(dve, link, q[:, :, :, NOPE:QK_A], chip.cos, chip.sin,
                           tmp[:, :, 0:G * ROPE // 2], HEADS)
                    group_rms(dve, link, root, kg, kg, t96[:, :, 0:NOPE], ss[:, :], NOPE, row("knope_g"))
        attention(chip, "mla_attention", q, k, lambda h, j: v[:, j, h, :], QK_A, head_rows(o_fm), head_rows(gate))


def fox(chip, l, io, par, row, fm, o_fm):
    DK = HD + 2
    with ExitStack() as ctx:
        def sb(name, shape):
            return ctx.enter_context(chip.nc.sbuf_tensor(f"fox_{name}_{l}", shape, F32))
        w_in = io["w_in"][l]
        gate = sb("gate", [P, WC, SEQ])
        silu_gate(chip, fm, w_in, COL["gate_b"], gate)
        q, k = sb("q", [P, TILES, HEADS, DK]), sb("k", [P, TILES, HEADS, DK])
        v = sb("v", [P, TILES, HEADS, HD])
        with ExitStack() as inner:
            def sbi(name, shape):
                return inner.enter_context(chip.nc.sbuf_tensor(f"fox_{name}_{l}", shape, F32))
            ff = sbi("ff", [HEADS, 3, SEQ])
            tmp, ss = sbi("tmp", [P, TILES, HEADS, HD]), sbi("ss", [P, TILES * HEADS])
            loads = [cols_of(w_in, COL["ff"], HEADS)]
            jobs = [fm_job(0, fm, DC, HEADS, 0, HEADS, "act",
                           lambda act, ps: act.activation(ff[:, 0, :], ps, ACT.Identity, bias=par("b_f", 0)[0:HEADS]))]
            for n, (name, dst) in enumerate((("fq", q), ("fk", k), ("fv", v))):
                loads.append(cols_of(w_in, COL[name], W))

                def into(t, dst=dst):
                    def fn(eng, ps):
                        return copy_to(dst[:, t, :, 0:HD])(eng, ps.rearrange("p (h d) -> p h d", h=HEADS))
                    return fn
                jobs += tm_jobs(n + 1, fm, DC, W, 0, W, into)
            gemm(chip, "fox_in", loads, jobs)

            with chip.stage("fox_heads") as st:
                absed, exped, logged = st.count("abs_ready"), st.count("exp_ready"), st.count("log_ready")
                summed, turned = st.count("cumsum_ready"), st.count("cumsum_transposed")
                root = Roots(st)

                @st.block.scalar
                def _(act):
                    act.wait_ge(*absed.at(1))
                    act.activation(ff[:, 1, :], ff[:, 1, :], ACT.Exp).then_inc(*exped.inc())
                    act.wait_ge(*exped.at(1))
                    act.activation(ff[:, 1, :], ff[:, 1, :], ACT.Ln, bias=1.0).then_inc(*logged.inc())
                    root.serve(act, ss[:, :], HD ** -0.5)
                    root.serve(act, ss[:, :])

                @st.block.vector
                def _(dve):
                    link = st.chain(dve, "heads_step")
                    link(dve.tensor_scalar(ff[:, 1, :], ff[:, 0, :], -1.0, None, ALU.mult))
                    dve.tensor_tensor(ff[:, 1, :], ff[:, 0, :], ff[:, 1, :], ALU.min).then_inc(*absed.inc())
                    link(dve.memset(ff[:, 2, :], 1.0))
                    dve.wait_ge(*logged.at(1))
                    link(dve.scalar_tensor_tensor(ff[:, 0, :], ff[:, 0, :], 0.0, ff[:, 1, :], ALU.min, ALU.subtract))
                    dve.tensor_tensor_scan(ff[:, 1, :], ff[:, 2, :], ff[:, 0, :], 0.0, ALU.mult, ALU.add).then_inc(*summed.inc())
                    G = TILES * HEADS
                    for x, gain in ((q, "fox_q_g"), (k, "fox_k_g")):
                        xg = x[:, :, :, :].rearrange("p t h d -> p (t h) d")[:, :, 0:HD]
                        group_rms(dve, link, root, xg, xg, tmp[:, :, :, :].rearrange("p t h d -> p (t h) d"), ss[:, :], HD,
                                  row(gain))
                    dve.wait_ge(*turned.at(1))
                    cum = chip.bank[0][:, 0:G].rearrange("p (t h) -> p t h", t=TILES)
                    dve.tensor_copy(q[:, :, :, HD], cum)
                    dve.memset(q[:, :, :, HD + 1], 1.0)
                    dve.memset(k[:, :, :, HD], 1.0)
                    dve.tensor_scalar(k[:, :, :, HD + 1], cum, -1.0, None, ALU.mult)

                @st.block.tensor
                def _(pe):
                    pe.wait_ge(*summed.at(1))
                    for t in range(TILES):
                        last = pe.transpose(chip.bank[0][:, t * HEADS:(t + 1) * HEADS], ff[:, 1, t * P:(t + 1) * P],
                                            chip.ident[0:HEADS, 0:HEADS])
                    last.then_inc(*turned.inc())
        attention(chip, "fox_attention", q, k, lambda h, j: v[:, j, h, :], DK, head_rows(o_fm), head_rows(gate))


def rwkv(chip, l, io, par, fm, o_fm, v_first):
    nc = chip.nc
    w_in = io["w_in"][l]
    with ExitStack() as ctx:
        def sb(name, shape):
            return ctx.enter_context(nc.sbuf_tensor(f"rwkv_{name}_{l}", shape, F32))
        bonus = o_fm
        left = sb("left", [P, WC, 2, SEQ])
        right = sb("right", [P, WC, 2, SEQ])
        vT = sb("v", [P, WC, SEQ])
        p_end = sb("p_end", [P, WC, NCH])
        with ExitStack() as inner:
            def sbi(name, shape):
                return inner.enter_context(nc.sbuf_tensor(f"rwkv_{name}_{l}", shape, F32))
            shifted = sbi("shifted", [P, 9, SEQ])
            r, k, lora = shifted[:, 0:4, :], shifted[:, 4:8, :], shifted[:, 8, :]
            lw = sbi("lw", [P, WC, SEQ])
            a = sbi("a", [P, WC, SEQ])
            wup = sbi("wup", [P, 2, W])
            lead = sbi("lead", [P, 2, SEQ + 1])
            n_chunks = SHIFT // P
            with chip.stage("rwkv_in") as st:
                weights = [st.sb(f"w{i}", [P, DC, P]) for i in range(3)]
                loaded = [st.count(f"w{i}_loaded") for i in range(3)]
                small = st.count("lora_loaded")
                summed, moved, freed = st.count("sums_ready"), st.count("chunk_moved"), st.count("chunk_shifted")

                @st.block.sync
                def _(sp):
                    sp.dma_start(wup[0:HD, 0, :], io["rwkv_w_up"][l]).then_inc(*small.inc(16))
                    sp.dma_start(wup[HD:P, 0, :], io["rwkv_a_up"][l]).then_inc(*small.inc(16))
                    for c in range(n_chunks):
                        if c >= 3:
                            sp.wait_ge(*summed.at(c - 2))
                        c0 = COL["shift"] + c * P
                        sp.dma_start(weights[c % 3][:, :, :], w_in[:, c0:c0 + P].rearrange("(k p) n -> p k n", p=P)
                                     ).then_inc(*loaded[c % 3].inc(16))
                    sp.wait_ge(*small.at(32))

                @st.block.tensor
                def _(pe):
                    for c in range(n_chunks):
                        pe.wait_ge(*loaded[c % 3].at(16 * (c // 3 + 1)))
                        if c >= 4:
                            pe.wait_ge(*moved.at(c - 3))
                        product(pe, chip.bank[c % 4][:, :], [(weights[c % 3][:, k_, :], fm[:, k_, :]) for k_ in range(DC)]
                                ).then_inc(*summed.inc())

                @st.block.scalar
                def _(act):
                    for n in range(2):
                        act.activation(lead[:, n, 0:1], chip.ident[:, 0:1], ACT.Copy, scale=0.0)
                    for c in range(n_chunks):
                        act.wait_ge(*summed.at(c + 1))
                        if c >= 2:
                            act.wait_ge(*freed.at(c - 1))
                        act.activation(lead[:, c % 2, 1:SEQ + 1], chip.bank[c % 4][:, :], ACT.Copy).then_inc(*moved.inc())

                @st.block.vector
                def _(dve):
                    link = st.chain(dve, "shift_step")
                    diff = st.sb("diff", [P, SEQ])
                    for c in range(n_chunks):
                        dst = r[:, c, :] if c < 4 else k[:, c - 4, :] if c < 8 else vT[:, c - 8, :] if c < 12 else lora
                        dve.wait_ge(*moved.at(c + 1))
                        x = lead[:, c % 2, :]
                        link(dve.tensor_tensor(diff[:, :], x[:, 0:SEQ], x[:, 1:SEQ + 1], ALU.subtract))
                        ins = dve.scalar_tensor_tensor(dst, diff[:, :], par("mu", c), x[:, 1:SEQ + 1], ALU.mult, ALU.add)
                        ins.then_inc(*freed.inc())
                        dve.wait_ge(*freed.at(c + 1))

            with chip.stage("rwkv_lora") as st:
                tanhed, summed, used = st.count("tanh_ready"), st.count("sums_ready"), st.count("sums_used")
                if l == 0:
                    @st.block.vector
                    def _(dve):
                        dve.tensor_copy(v_first[:, :, :], vT[:, :, :])
                else:
                    nu = lead[:, :, 0:SEQ]
                    vdown, vup, vd = st.sb("vdown", [P, WC, MV]), st.sb("vup", [MV, W]), st.sb("vd", [MV, SEQ])
                    vloaded, vdowned, vmoved = st.count("v_loaded"), st.count("v_down_done"), st.count("v_down_moved")
                    vsummed, nued, vdone = st.count("v_up_done"), st.count("nu_ready"), st.count("v_mixed")

                    @st.block.sync
                    def _(sp):
                        sp.dma_start(vdown[:, :, :], io["rwkv_v_down"][l - 1].rearrange("(k p) n -> p k n", p=P)
                                     ).then_inc(*vloaded.inc(16))
                        sp.dma_start(vup[:, :], io["rwkv_v_up"][l - 1]).then_inc(*vloaded.inc(16))

                    @st.block.vector
                    def _(dve):
                        link = st.chain(dve, "mix_step")
                        dve.wait_ge(*vdowned.at(1))
                        dve.tensor_copy(vd[:, :], chip.bank[4][0:MV, :]).then_inc(*vmoved.inc())
                        for c in range(WC):
                            diff = st.sb(f"vdiff{c}", [P, SEQ])
                            link(dve.tensor_tensor(diff[:, :], v_first[:, c, :], vT[:, c, :], ALU.subtract))
                            dve.wait_ge(*nued.at(c + 1))
                            link(dve.tensor_tensor(diff[:, :], diff[:, :], nu[:, c % 2, :], ALU.mult))
                            dve.tensor_tensor(vT[:, c, :], vT[:, c, :], diff[:, :], ALU.add).then_inc(*vdone.inc())

                @st.block.scalar
                def _(act):
                    act.activation(lora[0:HD, :], lora[0:HD, :], ACT.Tanh).then_inc(*tanhed.inc())
                    for c in range(WC):
                        act.wait_ge(*summed.at(c + 1))
                        act.activation(lw[:, c, :], chip.bank[2 * (c % 2)][:, :], ACT.Sigmoid, bias=par("w0", c))
                        act.activation(a[:, c, :], chip.bank[2 * (c % 2) + 1][:, :], ACT.Sigmoid,
                                       bias=par("a0", c)).then_inc(*used.inc())
                    if l > 0:
                        for c in range(WC):
                            act.wait_ge(*vsummed.at(c + 1))
                            if c >= 2:
                                act.wait_ge(*vdone.at(c - 1))
                            act.activation(nu[:, c % 2, :], chip.bank[5 + c % 2][:, :], ACT.Sigmoid,
                                           bias=par("v0", c)).then_inc(*nued.inc())

                @st.block.tensor
                def _(pe):
                    pe.wait_ge(*tanhed.at(1))
                    for c in range(WC):
                        if c >= 2:
                            pe.wait_ge(*used.at(c - 1))
                        cols = slice(c * P, (c + 1) * P)
                        pe.matmul(chip.bank[2 * (c % 2)][:, :], wup[0:HD, 0, cols], lora[0:HD, :], start=True, stop=True)
                        pe.matmul(chip.bank[2 * (c % 2) + 1][:, :], wup[HD:P, 0, cols], lora[HD:P, :],
                                  start=True, stop=True).then_inc(*summed.inc())
                    if l > 0:
                        pe.wait_ge(*vloaded.at(32))
                        product(pe, chip.bank[4][0:MV, :], [(vdown[:, c, :], vT[:, c, :]) for c in range(WC)]
                                ).then_inc(*vdowned.inc())
                        pe.wait_ge(*vmoved.at(1))
                        for c in range(WC):
                            if c >= 2:
                                pe.wait_ge(*nued.at(c - 1))
                            pe.matmul(chip.bank[5 + c % 2][:, :], vup[:, c * P:(c + 1) * P], vd[:, :],
                                      start=True, stop=True).then_inc(*vsummed.inc())

            with chip.stage("rwkv_operands") as st:
                cum, kk, e = st.sb("cum", [P, SEQ]), st.sb("kk", [P, SEQ]), st.sb("e", [P, 3, SEQ])
                km, sq = st.sb("km", [P, SEQ]), st.sb("sq", [P, SEQ])
                cummed, exped, consumed = st.count("cum_ready"), st.count("exps_ready"), st.count("exps_used")
                squared, normed = st.count("squares_ready"), st.count("norms_ready")
                rked, bonused = st.count("rk_ready"), st.count("bonus_summed")
                root = Roots(st)

                @st.block.tensor
                def _(pe):
                    for c in range(WC):
                        pe.wait_ge(*squared.at(c + 1))
                        pe.matmul(chip.bank[0][:, :], chip.head_ones, sq[:, :], start=True, stop=True).then_inc(*normed.inc())
                        pe.wait_ge(*rked.at(c + 1))
                        pe.matmul(chip.bank[1][:, :], chip.head_ones, sq[:, :], start=True, stop=True).then_inc(*bonused.inc())

                @st.block.scalar
                def _(act):
                    for c in range(WC):
                        act.wait_ge(*cummed.at(c + 1))
                        act.activation(e[:, 0, :], cum[:, :], ACT.Exp).then_inc(*exped.inc())
                        act.activation(e[:, 1, :], cum[:, :], ACT.Exp, scale=-1.0).then_inc(*exped.inc())
                        act.activation(e[:, 2, :], e[:, 2, :], ACT.Exp).then_inc(*exped.inc())
                        root.serve(act, sq[:, :])

                @st.block.vector
                def _(dve):
                    link = st.chain(dve, "operand_step")
                    for c in range(WC):
                        link(dve.tensor_scalar(lw[:, c, :], lw[:, c, :], -DECAY, None, ALU.mult))
                        link(dve.tensor_tensor_scan(cum[:, :], chip.chunk_keep, lw[:, c, :], 0.0, ALU.mult, ALU.add))
                        dve.tensor_tensor(e[:, 2, :], cum[:, :], lw[:, c, :], ALU.subtract).then_inc(*cummed.inc())
                        link(dve.tensor_scalar(kk[:, :], k[:, c, :], par("k_k", c), None, ALU.mult))
                        dve.tensor_tensor(sq[:, :], kk[:, :], kk[:, :], ALU.mult).then_inc(*squared.inc())
                        link(dve.tensor_scalar(km[:, :], a[:, c, :], 1.0, par("k_a", c), ALU.subtract, ALU.mult))
                        link(dve.scalar_tensor_tensor(km[:, :], km[:, :], 1.0, k[:, c, :], ALU.add, ALU.mult))
                        dve.wait_ge(*normed.at(c + 1))
                        root(dve, link, sq[:, :], dve.tensor_scalar(sq[:, :], chip.bank[0][:, :], 1e-24, None, ALU.max))
                        link(dve.tensor_tensor(kk[:, :], kk[:, :], sq[:, :], ALU.mult))
                        link(dve.tensor_tensor(sq[:, :], r[:, c, :], km[:, :], ALU.mult))
                        link(dve.tensor_scalar(sq[:, :], sq[:, :], par("r_k", c), None, ALU.mult))
                        dve.sem_inc(rked.sem, 1)
                        rked.inc()
                        dve.wait_ge(*exped.at(3 * c + 3))
                        link(dve.tensor_copy(p_end[:, c, :], e[:, 0, :].rearrange("p (n c) -> p n c", c=CH)[:, :, CH - 1]))
                        link(dve.tensor_tensor(right[:, c, 0, :], kk[:, :], e[:, 2, :], ALU.mult))
                        link(dve.tensor_tensor(right[:, c, 1, :], r[:, c, :], e[:, 0, :], ALU.mult))
                        link(dve.tensor_tensor(left[:, c, 1, :], km[:, :], e[:, 1, :], ALU.mult))
                        link(dve.tensor_tensor(kk[:, :], kk[:, :], a[:, c, :], ALU.mult))
                        link(dve.tensor_tensor(left[:, c, 0, :], kk[:, :], e[:, 1, :], ALU.mult))
                        dve.wait_ge(*bonused.at(c + 1))
                        link(dve.tensor_tensor(bonus[:, c, :], chip.bank[1][:, :], vT[:, c, :], ALU.mult))

        y = sb("y", [P, TILES, W])
        rwkv_core(chip, l, left, right, vT, p_end, y)

        gate, ln = sb("gate", [P, WC, SEQ]), sb("ln", [P, WC, SEQ])
        silu_gate(chip, fm, w_in, COL["gate_c"], gate)
        with chip.stage("rwkv_out") as st:
            sq, ms = st.sb("sq", [P, TILES * HEADS, HD]), st.sb("ms", [P, 2, TILES * HEADS])
            normed, turned, scaled = st.count("y_normed"), st.count("y_transposed"), st.count("y_scaled")
            root = Roots(st)

            @st.block.vector
            def _(dve):
                link = st.chain(dve, "out_step")
                yg = y[:, :, :].rearrange("p t (h d) -> p (t h) d", h=HEADS)
                shape = [P, TILES * HEADS, HD]
                link(dve.tensor_reduce(ms[:, 0, :], yg, AX.X, ALU.add))
                link(dve.tensor_scalar(ms[:, 0, :], ms[:, 0, :], 1.0 / HD, None, ALU.mult))
                link(dve.tensor_tensor(yg, yg, over(ms[:, 0, :], shape, 2), ALU.subtract))
                link(dve.tensor_tensor(sq[:, :, :], yg, yg, ALU.mult))
                link(dve.tensor_reduce(ms[:, 1, :], sq[:, :, :], AX.X, ALU.add))
                root(dve, link, ms[:, 1, :], dve.tensor_scalar(ms[:, 1, :], ms[:, 1, :], 1.0 / HD, GN_EPS, ALU.mult, ALU.add))
                dve.tensor_tensor(yg, yg, over(ms[:, 1, :], shape, 2), ALU.mult).then_inc(*normed.inc())
                for c in range(WC):
                    dve.wait_ge(*scaled.at(c + 1))
                    link(dve.tensor_tensor(o_fm[:, c, :], ln[:, c, :], bonus[:, c, :], ALU.add))
                    link(dve.tensor_tensor(o_fm[:, c, :], o_fm[:, c, :], gate[:, c, :], ALU.mult))

            @st.block.tensor
            def _(pe):
                pe.wait_ge(*normed.at(1))
                for c in range(WC):
                    for t in range(TILES):
                        last = pe.transpose(chip.bank[c][:, t * P:(t + 1) * P], y[:, t, c * P:(c + 1) * P], chip.ident)
                    last.then_inc(*turned.inc())

            @st.block.scalar
            def _(act):
                root.serve(act, ms[:, 1, :])
                for c in range(WC):
                    act.wait_ge(*turned.at(c + 1))
                    act.activation(ln[:, c, :], chip.bank[c][:, :], ACT.Identity, scale=par("lnx_g", c),
                                   bias=par("lnx_b", c)).then_inc(*scaled.inc())


def rwkv_core(chip, l, left, right, vT, p_end, y):
    nc = chip.nc
    with ExitStack() as ctx:
        def sb(name, shape):
            return ctx.enter_context(nc.sbuf_tensor(f"core_{name}_{l}", shape, F32))
        btm, ktm = sb("btm", [P, TILES, W]), sb("ktm", [P, TILES, W])
        vpar = sb("vpar", [P, 2, TILES, W])
        G = [sb(f"G{s}", [P, 4, 4, P]) for s in range(2)]
        M, Q, E, X, XT = ([sb(f"{n}{s}", [P, 4, P]) for s in range(2)] for n in ("M", "Q", "E", "X", "XT"))
        M2, Q2 = ([sb(f"{n}{s}", [P, 4, P]) for s in range(2)] for n in ("M2", "Q2"))
        state = [sb(f"state{s}", [P, 2, P]) for s in range(2)]
        neg_w = [sb(f"neg_w{s}", [P, 4, HD]) for s in range(2)]
        upd = [[sb(f"upd{s}{c}", [P, 4, HD]) for c in range(2)] for s in range(2)]

        with chip.stage("rwkv_turn") as st:
            turned, moved, zeroed = st.count("transposed"), st.count("moved"), st.count("zeroed")
            srcs = [("b", c) for c in range(WC)] + [("k", c) for c in range(WC)] + [("v", c) for c in range(WC)]

            def source(kind, c):
                return left[:, c, 0, :] if kind == "b" else left[:, c, 1, :] if kind == "k" else vT[:, c, :]

            @st.block.gpsimd
            def _(pool):
                for s in range(2):
                    pool.memset(state[s][:, :, :], 0.0)
                    pool.memset(neg_w[s][:, :, :], 0.0)
                    for c in range(2):
                        pool.memset(upd[s][c][:, :, :], 0.0)
                pool.memset(vpar[:, :, :, :], 0.0).then_inc(*zeroed.inc())

            @st.block.tensor
            def _(pe):
                for n, (kind, c) in enumerate(srcs):
                    if n >= 4:
                        pe.wait_ge(*moved.at(n - 3))
                    for t in range(TILES):
                        last = pe.transpose(chip.bank[n % 4][:, t * P:(t + 1) * P], source(kind, c)[:, t * P:(t + 1) * P],
                                            chip.ident)
                    last.then_inc(*turned.inc())

            @st.block.vector
            def _(dve):
                dve.wait_ge(*zeroed.at(1))
                for n, (kind, c) in enumerate(srcs):
                    dve.wait_ge(*turned.at(n + 1))
                    src = chip.bank[n % 4][:, :].rearrange("p (t f) -> p t f", t=TILES)
                    cols = slice(c * P, (c + 1) * P)
                    if kind == "v":
                        dve.tensor_copy(vpar[0:CH, 0, :, cols], src[0:CH])
                        dve.tensor_copy(vpar[CH:P, 1, :, cols], src[CH:P]).then_inc(*moved.inc())
                    else:
                        dve.tensor_copy((btm if kind == "b" else ktm)[:, :, cols], src).then_inc(*moved.inc())

        def phases(s, t):
            heads = range(4 * s, 4 * s + 4)
            tok = slice(t * P, (t + 1) * P)

            def half(h):
                return slice(HD * (h % 2), HD * (h % 2) + HD)

            def all_heads(bank):
                return bank[:, :].rearrange("p (h n) -> p h n", h=4)

            def each(pe, bank, lhsT, rhs):
                for i in range(4):
                    last = pe.matmul(bank[:, i * P:(i + 1) * P], lhsT[s][:, i, :], rhs[s][:, i, :], start=True, stop=True)
                return last

            def p_scores(pe, b):
                for i, h in enumerate(heads):
                    for n in range(2):
                        last = pe.matmul(b[i][:, 2 * n * P:2 * (n + 1) * P].rearrange("p (n t) -> p n t", n=2),
                                         left[half(h), h // 2, n, tok], right[half(h), h // 2, :, tok], start=True, stop=True)
                return last

            def e_scores(dve, link, b):
                for i in range(4):
                    last = dve.tensor_tensor(G[s][:, i, :, :], b[i][:, :].rearrange("p (n t) -> p n t", n=4),
                                             chip.chunk_masks, ALU.mult)
                return last
            yield p_scores, e_scores

            def p_turned(pe, b):
                for i, h in enumerate(heads):
                    last = pe.matmul(b[h % 2][:, (i // 2) * P:(i // 2 + 1) * P], right[half(h), h // 2, 0, tok],
                                     left[half(h), h // 2, 0, tok], start=True, stop=True)
                return last

            def e_turned(dve, link, b):
                for o in range(2):
                    dve.tensor_tensor(Q[s][:, :, :].rearrange("p (a o) n -> p a o n", o=2)[:, :, o, :],
                                      b[o][:, 0:2 * P].rearrange("p (a n) -> p a n", a=2),
                                      over(chip.sub_lower, [P, 2, P], 1), ALU.mult)
                dve.tensor_tensor(E[s][:, :, :], G[s][:, :, 0, :], over(chip.off_sub, [P, 4, P], 1), ALU.mult)
                link(dve.tensor_tensor(M[s][:, :, :], G[s][:, :, 0, :], over(chip.sub_upper, [P, 4, P], 1), ALU.mult))
                return dve.tensor_tensor(X[s][:, :, :], over(chip.ident, [P, 4, P], 1), M[s][:, :, :], ALU.subtract)
            yield p_turned, e_turned

            def square(m, q, m2, q2, update, last_one):
                def p(pe, b):
                    each(pe, b[0], q, m)
                    last = each(pe, b[1], m, q)
                    if update:
                        last = each(pe, b[2], q, X)
                    return last

                def e(dve, link, b):
                    dve.tensor_copy(m2[s][:, :, :], all_heads(b[0]))
                    last = dve.tensor_copy(q2[s][:, :, :], all_heads(b[1]))
                    if update:
                        last = dve.tensor_tensor(X[s][:, :, :], X[s][:, :, :], all_heads(b[2]), ALU.add)
                    return last
                return p, e
            yield square(M, Q, M2, Q2, False, False)
            yield square(M2, Q2, M, Q, True, False)
            yield square(M, Q, M2, Q2, True, True)

            def p_last(pe, b):
                return each(pe, b[0], Q2, X)

            def e_add(dve, link, b):
                return dve.tensor_tensor(X[s][:, :, :], X[s][:, :, :], all_heads(b[0]), ALU.add)
            yield p_last, e_add

            def p_xt(pe, b):
                for i in range(4):
                    last = pe.transpose(b[0][:, i * P:(i + 1) * P], X[s][:, i, :], chip.ident)
                return last
            yield p_xt, lambda dve, link, b: dve.tensor_copy(XT[s][:, :, :], all_heads(b[0]))

            def p_f(pe, b):
                each(pe, b[0], XT, E)
                return each(pe, b[1], E, XT)

            def e_f(dve, link, b):
                dve.tensor_copy(M[s][:, :, :], all_heads(b[0]))
                return dve.tensor_copy(Q[s][:, :, :], all_heads(b[1]))
            yield p_f, e_f
            yield (lambda pe, b: each(pe, b[0], M, Q)), (lambda dve, link, b: dve.tensor_copy(Q2[s][:, :, :], all_heads(b[0])))
            yield (lambda pe, b: each(pe, b[0], Q2, X)), e_add

            def e_sub(dve, link, b):
                return dve.tensor_tensor(X[s][:, :, :], X[s][:, :, :], all_heads(b[0]), ALU.subtract)
            yield (lambda pe, b: each(pe, b[0], Q, X)), e_sub

            for par_ in range(2):
                rows = slice(par_ * CH, (par_ + 1) * CH)

                def heads_v(i, par_=par_):
                    return vpar[:, par_, t, (4 * s + i) * HD:(4 * s + i + 1) * HD]

                def p_w(pe, b, heads_v=heads_v):
                    for pr in range(2):
                        pe.matmul(b[0][:, pr * P:(pr + 1) * P], right[:, 2 * s + pr, 0, tok], state[s][:, pr, :],
                                  start=True, stop=False, skip_group_check=True)
                        for i in (2 * pr, 2 * pr + 1):
                            last = pe.matmul(b[0][:, i * HD:(i + 1) * HD], G[s][:, i, 2, :], heads_v(i),
                                             start=False, stop=(i % 2 == 1), skip_group_check=True)
                    return last

                def e_w(dve, link, b, rows=rows):
                    return dve.tensor_scalar(neg_w[s][rows, :, :], b[0][rows, 0:4 * HD].rearrange("p (h v) -> p h v", h=4),
                                             -1.0, None, ALU.mult)
                yield p_w, e_w

                def p_u(pe, b):
                    for i in range(4):
                        last = pe.matmul(b[0][:, i * HD:(i + 1) * HD], X[s][:, i, :], neg_w[s][:, i, :], start=True, stop=True)
                    return last

                def e_u(dve, link, b, rows=rows, par_=par_):
                    return dve.tensor_copy(upd[s][par_][rows, :, :], b[0][rows, 0:4 * HD].rearrange("p (h v) -> p h v", h=4))
                yield p_u, e_u

                def p_y(pe, b, par_=par_, heads_v=heads_v):
                    for pr in range(2):
                        pe.matmul(b[1][:, pr * P:(pr + 1) * P], right[:, 2 * s + pr, 1, tok], state[s][:, pr, :],
                                  start=True, stop=False, skip_group_check=True)
                        for i in (2 * pr, 2 * pr + 1):
                            pe.matmul(b[1][:, i * HD:(i + 1) * HD], G[s][:, i, 1, :], upd[s][par_][:, i, :],
                                      start=False, stop=False, skip_group_check=True)
                            pe.matmul(b[1][:, i * HD:(i + 1) * HD], G[s][:, i, 3, :], heads_v(i),
                                      start=False, stop=(i % 2 == 1), skip_group_check=True)
                    for pr in range(2):
                        c0 = (2 * s + pr) * P
                        pe.matmul(b[0][:, pr * P:(pr + 1) * P], btm[:, t, c0:c0 + P],
                                  upd[s][par_][:, 2 * pr:2 * pr + 2, :], start=True, stop=False)
                        last = pe.matmul(b[0][:, pr * P:(pr + 1) * P], ktm[:, t, c0:c0 + P],
                                         vpar[:, par_, t, c0:c0 + P], start=False, stop=True)
                    return last

                def e_y(dve, link, b, rows=rows, par_=par_):
                    dve.tensor_copy(y[rows, t, 4 * s * HD:(4 * s + 4) * HD], b[1][rows, 0:4 * HD])
                    link(dve.tensor_tensor(state[s][:, :, :], b[0][:, 0:2 * P].rearrange("p (r v) -> p r v", r=2),
                                           state[s][:, :, :], ALU.add))
                    for pr in range(2):
                        last = dve.scalar_tensor_tensor(state[s][:, pr, :], state[s][:, pr, :],
                                                        p_end[:, 2 * s + pr, 2 * t + par_:2 * t + par_ + 1],
                                                        chip.head_ones, ALU.mult, ALU.mult)
                    return last
                yield p_y, e_y

        with chip.stage("rwkv_chunks") as st:
            done, moved = st.count("products_done"), st.count("results_moved")
            rounds = [ph for t in range(TILES) for pair in zip(phases(0, t), phases(1, t)) for ph in pair]

            @st.block.tensor
            def _(pe):
                for n, (products, _) in enumerate(rounds):
                    if n >= 2:
                        pe.wait_ge(*moved.at(n - 1))
                    products(pe, chip.bank[4 * (n % 2):4 * (n % 2) + 4]).then_inc(*done.inc())

            @st.block.vector
            def _(dve):
                link = st.chain(dve, "chunk_step")
                for n, (_, move) in enumerate(rounds):
                    dve.wait_ge(*done.at(n + 1))
                    move(dve, link, chip.bank[4 * (n % 2):4 * (n % 2) + 4]).then_inc(*moved.inc())



CONV_A, CONV_B = 3, 31
NUM_BUCKETS, MAX_DISTANCE = 32, 128
IDX_HEADS, IDX_DIM = 8, 32
TOPK = min(256, SEQ // 4)
TAKEN = -3e38
DIFF_HEADS, DIFF_V = 4, 128
BIAS_HEADS = HEADS + DIFF_HEADS
GROUPS, PER_GROUP = 4, 8
EXPERTS = GROUPS * PER_GROUP
D_EXP = 512
FC = D_EXP // P

P2_AT = {}
N_P2 = 0
for _name, _n in (("c", DC), ("conv_a", CONV_A * WC), ("conv_b", CONV_B * WC), ("conv_b_bias", WC), ("ln_g", WC),
                  ("ln_b", WC), ("diff_norm_g", 1)):
    P2_AT[_name] = N_P2
    N_P2 += _n
CD = {}
_at = 0
for _name, _n in (("q_c", W), ("k_c", W), ("v_c", W), ("q_idx", IDX_HEADS * IDX_DIM), ("k_idx", IDX_DIM),
                  ("w_idx", IDX_HEADS), ("q_d", W), ("k_d", W), ("v_d", W)):
    CD[_name] = _at
    _at += _n


def modulation(chip, i, io, par, mod):
    with ExitStack() as ctx:
        cond = ctx.enter_context(chip.nc.sbuf_tensor(f"cond_{i}", [P, DC, P], F32))
        gains = ctx.enter_context(chip.nc.sbuf_tensor(f"gains_{i}", [P, 2, D], F32))
        with chip.stage("condition") as st:
            loaded = st.count("rows_loaded")

            @st.block.scalar
            def _(act):
                c = par("c")
                act.activation(cond[:, :, :], over(c, [P, DC, P], 2), ACT.Silu)

            @st.block.sync
            def _(sp):
                sp.dma_start(mod[:, :, :].rearrange("p a d -> p (a d)"), io["ada_b"][i:i + 1, :].to_broadcast([P, 6 * D])
                             ).then_inc(*loaded.inc(16))
                for n in range(2):
                    sp.dma_start(gains[:, n, :], io["norm_rows"][2 * i + n:2 * i + n + 1, :].to_broadcast([P, D])
                                 ).then_inc(*loaded.inc(16))
                sp.wait_ge(*loaded.at(48))
        loads, jobs = [], []
        flat = mod[:, :, :].rearrange("p a d -> p (a d)")
        for c in range(6 * D // BANK):
            loads.append(cols_of(io["ada_w"][i], c * BANK, BANK))

            def pairs(w):
                wv = w[:, :].rearrange("p (k n) -> p k n", k=DC)
                return [(cond[:, k, :], wv[:, k, :]) for k in range(DC)]

            def add(dve, ps, c=c):
                dst = flat[:, c * BANK:(c + 1) * BANK]
                return dve.tensor_tensor(dst, dst, ps, ALU.add)
            jobs.append((c, pairs, lambda b: b[:, :], "dve", add))
        gemm(chip, "modulation", loads, jobs)
        with chip.stage("scales") as st:
            @st.block.vector
            def _(dve):
                for n in range(2):
                    s = mod[:, 3 * n + 1, :]
                    dve.scalar_tensor_tensor(s, s, 1.0, gains[:, n, :], ALU.add, ALU.mult)


def plain(act, out, ps, c):
    return act.activation(out, ps, ACT.Copy)


def add_gated(chip, name, x, y_fm, w, gate_row):
    with ExitStack() as ctx:
        y = ctx.enter_context(chip.nc.sbuf_tensor(f"{name}_y_{Stage.serial}", [P, TILES, D], F32))
        loads, jobs = [], []
        for c in range(2):
            loads.append(cols_of(w, c * BANK, BANK))
            cols = slice(c * BANK, (c + 1) * BANK)

            def gated(t, cols=cols):
                return lambda dve, ps: dve.tensor_tensor(y[:, t, cols], ps, gate_row[:, cols], ALU.mult)
            jobs += [j[:3] + ("dve",) + j[4:] for j in tm_jobs(c, y_fm, DC, BANK, 0, BANK, gated)]
        gemm(chip, name, loads, jobs)
        with chip.stage("residual") as st:
            @st.block.vector
            def _(dve):
                dve.tensor_tensor(x[:, :, :], x[:, :, :], y[:, :, :], ALU.add)


def conv_mixers(chip, io, par, fm, x, gate_row):
    w_in = io["ab_w_in"][0]
    with ExitStack() as ctx:
        def sb(name, shape):
            return ctx.enter_context(chip.nc.sbuf_tensor(f"conv_{name}", shape, F32))
        y_fm = sb("y", [P, DC, SEQ])
        with ExitStack() as inner:
            def sbi(name, shape):
                return inner.enter_context(chip.nc.sbuf_tensor(f"conv_{name}", shape, F32))
            ua, ub = sbi("ua", [P, WC, CONV_A - 1 + SEQ]), sbi("ub", [P, WC, CONV_B - 1 + SEQ])
            gb, acc = sbi("gate_b", [P, WC, SEQ]), sbi("acc", [P, WC, SEQ])
            sq = sbi("sq", [P, WC, SEQ])
            la, lb = CONV_A - 1, CONV_B - 1
            project_fm(chip, "conv_gate_b", fm, w_in, 0, WC, lambda c: copy_to(gb[:, c, :]))
            project_fm(chip, "conv_gate_c", fm, w_in, W, WC, lambda c: copy_to(acc[:, c, :]))
            project_fm(chip, "conv_x_a", fm, w_in, 2 * W, WC,
                       lambda c: lambda dve, ps: dve.tensor_tensor(ua[:, c, la:], ps, acc[:, c, :], ALU.mult), eng="dve")
            project_fm(chip, "conv_glu", fm, w_in, 4 * W, WC, lambda c: lambda act, ps: act.activation(sq[:, c, :], ps, ACT.Sigmoid))
            project_fm(chip, "conv_val", fm, w_in, 3 * W, WC,
                       lambda c: lambda dve, ps: dve.tensor_tensor(ub[:, c, lb:], ps, sq[:, c, :], ALU.mult), eng="dve")
            with chip.stage("conv") as st:
                tapped = st.count("tap_added")
                squared, summed, centred, varied = st.count("squared"), st.count("means"), st.count("centred"), st.count("variances")
                root = Roots(st)
                meanb, rstd = st.sb("mean", [P, SEQ]), st.sb("rstd", [P, SEQ])

                @st.block.vector
                def _(dve):
                    link = st.chain(dve, "conv_step")
                    link(dve.memset(ua[:, :, 0:la], 0.0))
                    link(dve.memset(ub[:, :, 0:lb], 0.0))
                    n = 0
                    for u, taps, name, dst in ((ua, CONV_A, "conv_a", y_fm), (ub, CONV_B, "conv_b", acc)):
                        for j in range(taps):
                            for c in range(WC):
                                o, s, wj = dst[:, c, :], u[:, c, j:j + SEQ], par(name)[:, j * WC + c:j * WC + c + 1]
                                if j == 0 and name == "conv_b":
                                    ins = dve.tensor_scalar(o, s, wj, par("conv_b_bias")[:, c:c + 1], ALU.mult, ALU.add)
                                elif j == 0:
                                    ins = dve.tensor_scalar(o, s, wj, None, ALU.mult)
                                else:
                                    dve.wait_ge(*tapped.at(n - WC + 1))
                                    ins = dve.scalar_tensor_tensor(o, s, wj, o, ALU.mult, ALU.add)
                                ins.then_inc(*tapped.inc())
                                n += 1
                    dve.wait_ge(*tapped.at(n))
                    dve.sem_inc(squared.sem, 1)
                    squared.inc()
                    link(dve.tensor_tensor(y_fm[:, 0:WC, :], y_fm[:, 0:WC, :], gb[:, :, :], ALU.mult))
                    dve.wait_ge(*summed.at(1))
                    link(dve.tensor_scalar(meanb[:, :], chip.bank[0][:, :], 1.0 / W, None, ALU.mult))
                    link(dve.tensor_tensor(acc[:, :, :], acc[:, :, :], over(meanb[:, :], [P, WC, SEQ], 1), ALU.subtract))
                    dve.tensor_tensor(sq[:, :, :], acc[:, :, :], acc[:, :, :], ALU.mult).then_inc(*squared.inc())
                    dve.wait_ge(*varied.at(1))
                    root(dve, link, rstd[:, :], dve.tensor_scalar(rstd[:, :], chip.bank[1][:, :], 1.0 / W, EPS, ALU.mult, ALU.add))
                    dve.tensor_tensor(acc[:, :, :], acc[:, :, :], over(rstd[:, :], [P, WC, SEQ], 1), ALU.mult).then_inc(*centred.inc())

                @st.block.tensor
                def _(pe):
                    pe.wait_ge(*squared.at(1))
                    product(pe, chip.bank[0][:, :], [(chip.ones, acc[:, c, :]) for c in range(WC)]).then_inc(*summed.inc())
                    pe.wait_ge(*squared.at(2))
                    product(pe, chip.bank[1][:, :], [(chip.ones, sq[:, c, :]) for c in range(WC)]).then_inc(*varied.inc())

                @st.block.scalar
                def _(act):
                    root.serve(act, rstd[:, :])
                    act.wait_ge(*centred.at(1))
                    for c in range(WC):
                        act.activation(y_fm[:, WC + c, :], acc[:, c, :], ACT.Silu, scale=par("ln_g")[:, c:c + 1],
                                       bias=par("ln_b")[:, c:c + 1])
        add_gated(chip, "conv_out", x, y_fm, io["ab_w_out"][0], gate_row)


def position_bias(chip, io, scratch):
    Q4 = P // 4
    with chip.stage("position_bias") as st:
        table, before = st.sb("table", [P, 4 * BIAS_HEADS]), st.sb("before", [P, 4 * BIAS_HEADS])
        posi, pos = st.sb("posi", [P, SEQ + P], I32), st.sb("pos", [P, SEQ + P])
        steps_ = [st.sb(f"step{i}", [P, SEQ]) for i in range(4)]
        outs = [st.sb(f"out{i}", [4 * BIAS_HEADS, 4, SEQ]) for i in range(3)]
        cleared, loaded, ready = st.count("cleared"), st.count("loaded"), st.count("table_ready")
        stepped, summed, moved, stored = st.count("steps_ready"), st.count("summed"), st.count("moved"), [
            st.count(f"stored{i}") for i in range(3)]

        @st.block.gpsimd
        def _(pool):
            pool.memset(table[:, :], 0.0)
            pool.memset(before[:, :], 0.0).then_inc(*cleared.inc())

        @st.block.sync
        def _(sp):
            sp.wait_ge(*cleared.at(1))
            for n in range(4):
                rows, cols = slice(Q4 * n, Q4 * (n + 1)), slice(BIAS_HEADS * n, BIAS_HEADS * (n + 1))
                sp.dma_start(table[rows, cols], io["rel_bias"]).then_inc(*loaded.inc(16))
                sp.dma_start(before[Q4 * n + 1:Q4 * (n + 1), cols], io["rel_bias"][0:NUM_BUCKETS - 1, :]).then_inc(*loaded.inc(16))
                sp.dma_start(posi[rows, SEQ:SEQ + P], io["pos_quarter"][n:n + 1, :].to_broadcast([Q4, P])).then_inc(*loaded.inc(16))
            sp.dma_start(posi[:, 0:SEQ], io["pos_row"].to_broadcast([P, SEQ])).then_inc(*loaded.inc(16))
            for b in range(P // 4):
                sp.wait_ge(*moved.at(4 * (b + 1)))
                dst = scratch.rearrange("a t n k -> a (t n) k")[:, 4 * b:4 * b + 4, :]
                sp.dma_start(dst, outs[b % 3][:, :, :]).then_inc(*stored[b % 3].inc(16))
            for i in range(3):
                sp.wait_ge(*stored[i].at(stored[i].total))

        @st.block.vector
        def _(dve):
            link = st.chain(dve, "bias_step")
            dve.wait_ge(*loaded.at(16 * 13))
            link(dve.tensor_tensor(table[:, :], table[:, :], before[:, :], ALU.subtract))
            link(dve.tensor_copy(pos[:, :], posi[:, :]))
            link(dve.tensor_scalar(pos[:, SEQ:SEQ + P], pos[:, SEQ:SEQ + P], chip.bucket_from, None, ALU.subtract))
            for g in range(P):
                if g >= 4:
                    dve.wait_ge(*summed.at(g - 3))
                dve.tensor_scalar(steps_[g % 4][:, :], pos[:, 0:SEQ], pos[:, SEQ + g:SEQ + g + 1], None, ALU.is_le
                                  ).then_inc(*stepped.inc())

        @st.block.tensor
        def _(pe):
            for g in range(P):
                pe.wait_ge(*stepped.at(g + 1))
                if g >= 8:
                    pe.wait_ge(*moved.at(g - 7))
                pe.matmul(chip.bank[g % 8][0:4 * BIAS_HEADS, :], table[:, :], steps_[g % 4][:, :], start=True, stop=True
                          ).then_inc(*summed.inc())

        @st.block.scalar
        def _(act):
            for g in range(P):
                b = g // 4
                if g % 4 == 0 and b >= 3:
                    act.wait_ge(*stored[b % 3].at(16 * (b // 3)))
                act.wait_ge(*summed.at(g + 1))
                act.activation(outs[b % 3][:, g % 4, :], chip.bank[g % 8][0:4 * BIAS_HEADS, :], ACT.Copy).then_inc(*moved.inc())


def attn_mixers(chip, io, par, fm, x, gate_row, scratch):
    w_in = io["cd_w_in"][0]
    lambda_init = 0.8 - 0.6 * float(np.exp(-0.3))
    with ExitStack() as ctx:
        def sb(name, shape, dt=F32):
            return ctx.enter_context(chip.nc.sbuf_tensor(f"attn_{name}", shape, dt))
        y_fm = sb("y", [P, DC, SEQ])
        causal = sb("causal", [P, TILES, SEQ])
        masks = sb("masks", [P, TILES, SEQ])

        def tm_loads(names, dsts, extra=()):
            loads, jobs = [], []
            for n, (name, dst) in enumerate(zip(names, dsts)):
                loads.append(cols_of(w_in, CD[name], W))
                jobs += tm_jobs(n, fm, DC, W, 0, W, lambda t, dst=dst: copy_to(dst[:, t, :, :].rearrange("p h d -> p (h d)")))
            gemm(chip, "attn_in", loads, jobs)

        with ExitStack() as inner:
            def sbi(name, shape, dt=F32):
                return inner.enter_context(chip.nc.sbuf_tensor(f"idx_{name}", shape, dt))
            qiT, kiT, wi = sbi("q", [P, 2, SEQ]), sbi("k", [P, SEQ]), sbi("w", [P, TILES, IDX_HEADS])
            posi, pos = sbi("posi", [P, SEQ + TILES], I32), sbi("pos", [P, SEQ + TILES])
            nq, nk = IDX_HEADS * IDX_DIM, IDX_DIM

            def k_four(slot):
                view = slot[:, 0:DC * P].rearrange("p (k r n) -> p k r n", k=DC, r=4)
                return view, w_in[:, CD["k_idx"]:CD["k_idx"] + nk].rearrange("(k p) n -> p k n", p=P)
            loads = [cols_of(w_in, CD["q_idx"], nq), cols_of(w_in, CD["w_idx"], IDX_HEADS)]
            jobs = [fm_job(0, fm, DC, nq, c * P, P, "act", copy_to(qiT[:, c, :])) for c in range(2)]
            jobs += [j[:3] + ("act",) + j[4:] for j in tm_jobs(1, fm, DC, IDX_HEADS, 0, IDX_HEADS,
                     lambda t: lambda act, ps: act.activation(wi[:, t, :], ps, ACT.Copy, scale=(IDX_DIM * IDX_HEADS) ** -0.5))]
            gemm(chip, "index_in", loads, jobs)
            with chip.stage("index_key") as st:
                wk = st.sb("wk", [P, DC, 4, nk])
                loaded, summed = st.count("loaded"), st.count("summed")
                converted = st.count("converted")

                @st.block.sync
                def _(sp):
                    for r in range(4):
                        sp.dma_start(wk[:, :, r, :], w_in[:, CD["k_idx"]:CD["k_idx"] + nk].rearrange("(k p) n -> p k n", p=P)
                                     ).then_inc(*loaded.inc(16))
                    sp.dma_start(posi[:, 0:SEQ], io["pos_row"].to_broadcast([P, SEQ])).then_inc(*converted.inc(16))
                    sp.dma_start(posi[:, SEQ:SEQ + TILES], io["pos_col"]).then_inc(*converted.inc(16))

                @st.block.tensor
                def _(pe):
                    pe.wait_ge(*loaded.at(64))
                    product(pe, chip.bank[0][:, :], [(wk[:, k, :, :].rearrange("p r n -> p (r n)"), fm[:, k, :]) for k in range(DC)]
                            ).then_inc(*summed.inc())

                @st.block.scalar
                def _(act):
                    act.wait_ge(*summed.at(1))
                    act.activation(kiT[:, :], chip.bank[0][:, :], ACT.Copy)

                @st.block.vector
                def _(dve):
                    link = st.chain(dve, "mask_step")
                    dve.wait_ge(*converted.at(32))
                    link(dve.tensor_copy(pos[:, :], posi[:, :]))
                    for t in range(TILES):
                        dve.tensor_scalar(causal[:, t, :], pos[:, 0:SEQ], pos[:, SEQ + t:SEQ + t + 1], MASKED, ALU.is_gt, ALU.mult)

            with chip.stage("top_keys") as st:
                rel = [st.sb(f"rel{i}", [P, SEQ]) for i in range(2)]
                best = st.sb("best", [P, TILES, 8])
                summed, rectified, added = st.count("index_scored"), st.count("rectified"), st.count("added")

                @st.block.tensor
                def _(pe):
                    for n in range(TILES * IDX_HEADS):
                        t, h = divmod(n, IDX_HEADS)
                        if n >= 4:
                            pe.wait_ge(*rectified.at(n - 3))
                        rows = slice(IDX_DIM * (h % 4), IDX_DIM * (h % 4 + 1))
                        pe.matmul(chip.bank[n % 4][:, :], qiT[rows, h // 4, t * P:(t + 1) * P], kiT[rows, :], start=True, stop=True,
                                  tile_position=(IDX_DIM * (h % 4), 0)).then_inc(*summed.inc())

                @st.block.scalar
                def _(act):
                    for n in range(TILES * IDX_HEADS):
                        act.wait_ge(*summed.at(n + 1))
                        if n >= 2:
                            act.wait_ge(*added.at(n - 1))
                        act.activation(rel[n % 2][:, :], chip.bank[n % 4][:, :], ACT.Relu).then_inc(*rectified.inc())

                @st.block.vector
                def _(dve):
                    link = st.chain(dve, "top_step")
                    for n in range(TILES * IDX_HEADS):
                        t, h = divmod(n, IDX_HEADS)
                        dve.wait_ge(*rectified.at(n + 1))
                        base = causal[:, t, :] if h == 0 else masks[:, t, :]
                        dve.scalar_tensor_tensor(masks[:, t, :], rel[n % 2][:, :], wi[:, t, h:h + 1], base, ALU.mult, ALU.add
                                                 ).then_inc(*added.inc())
                        dve.wait_ge(*added.at(n + 1))
                    for _ in range(TOPK // 8):
                        for t in range(TILES):
                            link(dve.max(best[:, t, :], masks[:, t, :]))
                            link(dve.match_replace(masks[:, t, :], best[:, t, :], masks[:, t, :], TAKEN))
                    for t in range(TILES):
                        link(dve.tensor_scalar(masks[:, t, :], masks[:, t, :], TAKEN / 2, MASKED, ALU.is_gt, ALU.mult))
                        link(dve.tensor_tensor(masks[:, t, :], masks[:, t, :], causal[:, t, :], ALU.add))

        def bias_of(h):
            def part(n):
                rows = slice(32 * n, 32 * n + 32)
                return lambda buf: buf[rows, :, :]
            return [(part(n), scratch[n * BIAS_HEADS + h].rearrange("t n k -> n t k")) for n in range(4)]

        with ExitStack() as inner:
            q, k, v = (inner.enter_context(chip.nc.sbuf_tensor(f"topk_{n}", [P, TILES, HEADS, HD], F32)) for n in "qkv")
            tm_loads(("q_c", "k_c", "v_c"), (q, k, v))
            attention(chip, "topk_attention", q, k, lambda h, j: v[:, j, h, :], HD, head_rows(y_fm), None, causal=False,
                      scale=HD ** -0.5, bias=bias_of, masks=masks)
        with ExitStack() as inner:
            def sbi(name, shape):
                return inner.enter_context(chip.nc.sbuf_tensor(f"diff_{name}", shape, F32))
            maps = sbi("maps", [P, 2 * DIFF_HEADS, SEQ])
            q, k, v = (sbi(n, [P, TILES, 2 * DIFF_HEADS, HD]) for n in "qkv")
            tm_loads(("q_d", "k_d", "v_d"), (q, k, v))
            vd = v[:, :, :, :].rearrange("p t (h a) d -> p t h (a d)", a=2)
            attention(chip, "diff_attention", q, k, lambda h, j: vd[:, j, h // 2, :], HD, lambda h: maps[:, h, :], None, dv=DIFF_V,
                      causal=False, scale=HD ** -0.5, bias=lambda h: bias_of(HEADS + h // 2), masks=causal)
            with chip.stage("diff_out") as st:
                lam, pr, ex = st.sb("lam", [P, 4, HD]), st.sb("pr", [P, 2, HD]), st.sb("ex", [P, 4])
                sq, rr = st.sb("sq", [P, DIFF_HEADS, SEQ]), st.sb("rr", [P, DIFF_HEADS, SEQ])
                loaded, dotted, exped = st.count("loaded"), st.count("dotted"), st.count("exped")
                squared, summed = st.count("squared"), st.count("summed")
                root = Roots(st)

                @st.block.sync
                def _(sp):
                    sp.dma_start(lam[:, :, :].rearrange("p a d -> p (a d)"), io["diff_lam"].to_broadcast([P, 4 * HD])
                                 ).then_inc(*loaded.inc(16))

                @st.block.scalar
                def _(act):
                    act.wait_ge(*dotted.at(1))
                    act.activation(ex[:, 0:2], ex[:, 0:2], ACT.Exp).then_inc(*exped.inc())
                    for h in range(DIFF_HEADS):
                        root.serve(act, rr[:, h, :], 1.0 - lambda_init)

                @st.block.tensor
                def _(pe):
                    pe.wait_ge(*squared.at(1))
                    for h in range(DIFF_HEADS):
                        pe.matmul(chip.bank[h][:, :], chip.ones, sq[:, h, :], start=True, stop=True).then_inc(*summed.inc())

                @st.block.vector
                def _(dve):
                    link = st.chain(dve, "diff_step")
                    dve.wait_ge(*loaded.at(16))
                    link(dve.tensor_tensor(pr[:, :, :], lam[:, 0::2, :], lam[:, 1::2, :], ALU.mult))
                    dve.tensor_reduce(ex[:, 0:2], pr[:, :, :], AX.X, ALU.add).then_inc(*dotted.inc())
                    dve.wait_ge(*exped.at(1))
                    link(dve.tensor_tensor(ex[:, 2:3], ex[:, 1:2], ex[:, 0:1], ALU.subtract))
                    link(dve.tensor_scalar(ex[:, 2:3], ex[:, 2:3], lambda_init, None, ALU.subtract))
                    for h in range(DIFF_HEADS):
                        link(dve.scalar_tensor_tensor(maps[:, 2 * h, :], maps[:, 2 * h + 1, :], ex[:, 2:3], maps[:, 2 * h, :],
                                                      ALU.mult, ALU.add))
                    dve.tensor_tensor(sq[:, :, :], maps[:, 0::2, :], maps[:, 0::2, :], ALU.mult).then_inc(*squared.inc())
                    for h in range(DIFF_HEADS):
                        dve.wait_ge(*summed.at(h + 1))
                        root(dve, link, rr[:, h, :], dve.tensor_scalar(rr[:, h, :], chip.bank[h][:, :], 1.0 / DIFF_V, EPS,
                                                                       ALU.mult, ALU.add))
                        link(dve.scalar_tensor_tensor(y_fm[:, WC + h, :], maps[:, 2 * h, :], par("diff_norm_g"), rr[:, h, :],
                                                      ALU.mult, ALU.mult))
        add_gated(chip, "attn_out", x, y_fm, io["cd_w_out"][0], gate_row)


def route(chip, i, io, fm, gates):
    n_r = GROUPS + EXPERTS
    with ExitStack() as ctx:
        lg = ctx.enter_context(chip.nc.sbuf_tensor(f"logits_{i}", [P, TILES, n_r], F32))
        gemm(chip, "router", [cols_of(io["router_w"][i], 0, n_r)],
             [j[:3] + ("dve",) + j[4:] for j in tm_jobs(0, fm, DC, n_r, 0, n_r, lambda t: copy_to(lg[:, t, :]))])
        with chip.stage("route") as st:
            rb, m = st.sb("rb", [P, n_r]), st.sb("m", [P, 8, TILES])
            a4, g4, t4 = (st.sb(n, [P, TILES, GROUPS]) for n in ("a4", "g4", "t4"))
            fine, sel = st.sb("fine", [P, TILES, GROUPS, PER_GROUP]), st.sb("sel", [P, TILES, PER_GROUP])
            o1, o2, t8 = (st.sb(n, [P, TILES, PER_GROUP]) for n in ("o1", "o2", "t8"))
            loaded, shifted, exped = st.count("loaded"), st.count("shifted"), st.count("exped")

            @st.block.sync
            def _(sp):
                sp.dma_start(rb[:, :], io["router_b"][i:i + 1, :].to_broadcast([P, n_r])).then_inc(*loaded.inc(16))

            @st.block.scalar
            def _(act):
                act.wait_ge(*shifted.at(1))
                act.activation(a4[:, :, :], a4[:, :, :], ACT.Exp).then_inc(*exped.inc())
                act.wait_ge(*shifted.at(2))
                act.activation(m[:, 3, :], m[:, 3, :], ACT.Exp).then_inc(*exped.inc())

            @st.block.vector
            def _(dve):
                link = st.chain(dve, "route_step")

                def first_best(onehot, x, best, tmp, n):
                    shape = [P, TILES, n]
                    link(dve.tensor_reduce(best, x, AX.X, ALU.max))
                    link(dve.tensor_tensor(tmp, x, over(best, shape, 2), ALU.is_equal))
                    link(dve.tensor_tensor(tmp, tmp, over(chip.rank8[:, 0:n], shape, 1), ALU.mult))
                    link(dve.tensor_reduce(m[:, 7, :], tmp, AX.X, ALU.max))
                    link(dve.tensor_tensor(onehot, tmp, over(m[:, 7, :], shape, 2), ALU.is_equal))

                dve.wait_ge(*loaded.at(16))
                link(dve.tensor_tensor(lg[:, :, :], lg[:, :, :], over(rb[:, :], [P, TILES, n_r], 1), ALU.add))
                lgg = lg[:, :, 0:GROUPS]
                first_best(g4[:, :, :], lgg, m[:, 0, :], t4[:, :, :], GROUPS)
                dve.tensor_tensor(a4[:, :, :], lgg, over(m[:, 0, :], [P, TILES, GROUPS], 2), ALU.subtract).then_inc(*shifted.inc())
                dve.wait_ge(*exped.at(1))
                link(dve.tensor_reduce(m[:, 1, :], a4[:, :, :], AX.X, ALU.add))
                link(dve.reciprocal(m[:, 1, :], m[:, 1, :]))
                shape = [P, TILES, GROUPS, PER_GROUP]
                for t in range(TILES):
                    link(dve.tensor_tensor(fine[:, t], lg[:, t, GROUPS:n_r].rearrange("p (g e) -> p g e", g=GROUPS),
                                           over(g4[:, t, :], shape[:1] + shape[2:], 2), ALU.mult))
                    link(dve.tensor_reduce(sel[:, t, :], fine[:, t].rearrange("p g e -> p e g"), AX.X, ALU.add))
                first_best(o1[:, :, :], sel[:, :, :], m[:, 2, :], t8[:, :, :], PER_GROUP)
                link(dve.scalar_tensor_tensor(sel[:, :, :], o1[:, :, :], TAKEN, sel[:, :, :], ALU.mult, ALU.add))
                first_best(o2[:, :, :], sel[:, :, :], m[:, 3, :], t8[:, :, :], PER_GROUP)
                dve.tensor_tensor(m[:, 3, :], m[:, 3, :], m[:, 2, :], ALU.subtract).then_inc(*shifted.inc())
                dve.wait_ge(*exped.at(2))
                link(dve.tensor_scalar(m[:, 4, :], m[:, 3, :], 1.0, None, ALU.add))
                link(dve.reciprocal(m[:, 4, :], m[:, 4, :]))
                link(dve.tensor_tensor(m[:, 4, :], m[:, 4, :], m[:, 1, :], ALU.mult))
                link(dve.tensor_tensor(m[:, 5, :], m[:, 4, :], m[:, 3, :], ALU.mult))
                e8 = [P, TILES, PER_GROUP]
                link(dve.tensor_tensor(o1[:, :, :], o1[:, :, :], over(m[:, 4, :], e8, 2), ALU.mult))
                link(dve.tensor_tensor(o2[:, :, :], o2[:, :, :], over(m[:, 5, :], e8, 2), ALU.mult))
                link(dve.tensor_tensor(o1[:, :, :], o1[:, :, :], o2[:, :, :], ALU.add))
                gv = gates[:, :, :].rearrange("p t (g e) -> p t g e", g=GROUPS)
                for t in range(TILES):
                    link(dve.tensor_tensor(gv[:, t], over(g4[:, t, :], shape[:1] + shape[2:], 2),
                                           over(o1[:, t, :], shape[:1] + shape[2:], 1), ALU.mult))


def dense_experts(chip, i, io, fm, gates, acc):
    with chip.stage("experts") as st:
        wg, wu = ([st.sb(f"{n}{s}", [P, DC, D_EXP]) for s in range(2)] for n in ("wg", "wu"))
        wd = [st.sb(f"wd{s}", [P, FC, D]) for s in range(2)]
        hid = [st.sb(f"hid{s}", [P, FC, SEQ]) for s in range(2)]
        sg = [st.sb(f"sg{s}", [P, SEQ]) for s in range(2)]
        loaded = [[st.count(f"{n}{s}_loaded") for s in range(2)] for n in ("up", "down")]
        up_free, down_free = st.count("up_weights_free"), st.count("down_weights_free")
        gated, silued, multiplied = st.count("up_products"), st.count("silu_done"), st.count("hidden_ready")
        downed, added = st.count("down_product"), st.count("added")
        B = chip.bank
        E = EXPERTS
        n_down = TILES * 2

        def expert_of(name, e):
            w = io[name].rearrange("l e a n -> (l e) a n")
            return w[bass.ds(e + i * EXPERTS, 1), :, :].rearrange("o (k p) n -> p (o k) n", p=P)

        @st.block.sync
        def _(sp):
            with sp.Fori(0, E // 2) as pair:
                e0 = pair * 2
                for s in range(2):
                    sp.wait_ge(*up_free.at(e0 + s + 1))
                    for w, src in ((wg, "moe_w_gate"), (wu, "moe_w_up")):
                        sp.dma_start(w[s][:, :, :], expert_of(src, e0 + s)
                                     ).then_inc(*loaded[0][s].inc(16, E // 2))
                    sp.wait_ge(*down_free.at(e0 + s + 1))
                    sp.dma_start(wd[s][:, :, :], expert_of("moe_w_down", e0 + s)
                                 ).then_inc(*loaded[1][s].inc(16, E // 2))

        @st.block.tensor
        def _(pe):
            pe.sem_inc(up_free.sem, 2)
            up_free.inc(2)
            pe.sem_inc(down_free.sem, 2)
            down_free.inc(2)
            with pe.Fori(0, E // 2) as pair:
                e0 = pair * 2
                for s in range(2):
                    pe.wait_ge(*loaded[0][s].at(16 * e0 + 32))
                    for f in range(FC):
                        pe.wait_ge(*multiplied.at(FC * e0 + FC * s + f + 1))
                        cols = slice(f * P, (f + 1) * P)
                        product(pe, B[f % 2][:, :], [(wg[s][:, k, cols], fm[:, k, :]) for k in range(DC)])
                        ins = product(pe, B[2 + f % 2][:, :], [(wu[s][:, k, cols], fm[:, k, :]) for k in range(DC)])
                        ins.then_inc(*gated.inc(1, E // 2))
                    pe.wait_ge(*gated.at(FC * e0 + FC * (s + 1)))
                    pe.sem_inc(up_free.sem, 1)
                    up_free.inc(1, E // 2)
                    pe.wait_ge(*multiplied.at(FC * e0 + FC * (s + 1) + 2))
                    pe.wait_ge(*loaded[1][s].at(8 * e0 + 16))
                    for n in range(n_down):
                        t, d = divmod(n, 2)
                        pe.wait_ge(*added.at(n_down * e0 + n_down * s + n + 1))
                        ins = product(pe, B[4 + n % 4][:, :], [(hid[s][:, f, t * P:(t + 1) * P], wd[s][:, f, d * BANK:(d + 1) * BANK])
                                                              for f in range(FC)])
                        ins.then_inc(*downed.inc(1, E // 2))
                    pe.wait_ge(*downed.at(n_down * e0 + n_down * (s + 1)))
                    pe.sem_inc(down_free.sem, 1)
                    down_free.inc(1, E // 2)

        @st.block.scalar
        def _(act):
            with act.Fori(0, E // 2) as pair:
                e0 = pair * 2
                for s in range(2):
                    for f in range(FC):
                        act.wait_ge(*gated.at(FC * e0 + FC * s + f + 1))
                        act.wait_ge(*multiplied.at(FC * e0 + FC * s + f + 1))
                        act.activation(sg[f % 2][:, :], B[f % 2][:, :], ACT.Silu).then_inc(*silued.inc(1, E // 2))

        @st.block.vector
        def _(dve):
            dve.sem_inc(multiplied.sem, 2)
            multiplied.inc(2)
            dve.sem_inc(added.sem, 4)
            added.inc(4)
            with dve.Fori(0, E // 2) as pair:
                e0 = pair * 2
                for s in range(2):
                    for f in range(FC):
                        dve.wait_ge(*silued.at(FC * e0 + FC * s + f + 1))
                        dve.tensor_tensor(hid[s][:, f, :], B[2 + f % 2][:, :], sg[f % 2][:, :], ALU.mult
                                          ).then_inc(*multiplied.inc(1, E // 2))
                    for n in range(n_down):
                        t, d = divmod(n, 2)
                        dve.wait_ge(*downed.at(n_down * e0 + n_down * s + n + 1))
                        dst = acc[:, t, d * BANK:(d + 1) * BANK]
                        dve.scalar_tensor_tensor(dst, B[4 + n % 4][:, :], gates[:, t, bass.ds(e0 + s, 1)], dst, ALU.mult, ALU.add
                                                 ).then_inc(*added.inc(1, E // 2))


def experts(chip, i, io, fm, x, gate_row):
    with ExitStack() as ctx:
        gates = ctx.enter_context(chip.nc.sbuf_tensor(f"gates_{i}", [P, TILES, EXPERTS], F32))
        acc = ctx.enter_context(chip.nc.sbuf_tensor(f"expert_sum_{i}", [P, TILES, D], F32))
        route(chip, i, io, fm, gates)
        with chip.stage("clear") as st:
            @st.block.gpsimd
            def _(pool):
                pool.memset(acc[:, :, :], 0.0)
        dense_experts(chip, i, io, fm, gates, acc)
        with chip.stage("moe_residual") as st:
            @st.block.vector
            def _(dve):
                link = st.chain(dve, "residual_step")
                link(dve.tensor_tensor(acc[:, :, :], acc[:, :, :], over(gate_row, [P, TILES, D], 1), ALU.mult))
                dve.tensor_tensor(x[:, :, :], x[:, :, :], acc[:, :, :], ALU.add)


def second_block(chip, io, x):
    nc = chip.nc
    with ExitStack() as ctx:
        def sb(name, shape):
            return ctx.enter_context(nc.sbuf_tensor(name, shape, F32))
        fm, mod = sb("fm2", [P, DC, SEQ]), sb("mod", [P, 6, D])
        params = sb("params2", [P, N_P2])
        scratch = nc.dram_tensor("bias_scratch", [4 * BIAS_HEADS, TILES, P // 4, SEQ], F32, kind="Internal").ap()

        def par(name):
            n = {"c": DC, "conv_a": CONV_A * WC, "conv_b": CONV_B * WC, "diff_norm_g": 1}.get(name, WC)
            return params[:, P2_AT[name]:P2_AT[name] + n]
        with chip.stage("params") as st:
            loaded = st.count("params_loaded")

            @st.block.sync
            def _(sp):
                sp.dma_start(params[:, :], io["params_2"]).then_inc(*loaded.inc(16))
                sp.wait_ge(*loaded.at(16))
        for i in range(DEPTH):
            modulation(chip, i, io, par, mod)
            norm_to_fm(chip, x, fm, plain, (mod[:, 1, :], mod[:, 0, :]))
            if i == 0:
                conv_mixers(chip, io, par, fm, x, mod[:, 2, :])
            else:
                position_bias(chip, io, scratch)
                attn_mixers(chip, io, par, fm, x, mod[:, 2, :], scratch)
            norm_to_fm(chip, x, fm, plain, (mod[:, 4, :], mod[:, 3, :]))
            experts(chip, i, io, fm, x, mod[:, 5, :])
        with chip.stage("final_norm") as st:
            sq, ss, g = st.sb("sq", [P, TILES, D]), st.sb("ss", [P, TILES]), st.sb("g", [P, D])
            squared, loaded = st.count("squares_summed"), st.count("gain_loaded")
            root = Roots(st)

            @st.block.sync
            def _(sp):
                sp.dma_start(g[:, :], io["norm_rows"][2 * DEPTH:2 * DEPTH + 1, :].to_broadcast([P, D])).then_inc(*loaded.inc(16))

            @st.block.scalar
            def _(act):
                for t in range(TILES):
                    act.activation(sq[:, t, :], x[:, t, :], ACT.Square, accum_out=ss[:, t:t + 1]).then_inc(*squared.inc())
                root.serve(act, ss[:, :])

            @st.block.vector
            def _(dve):
                link = st.chain(dve, "final_step")
                dve.wait_ge(*squared.at(TILES))
                root(dve, link, ss[:, :], dve.tensor_scalar(ss[:, :], ss[:, :], 1.0 / D, EPS, ALU.mult, ALU.add))
                dve.wait_ge(*loaded.at(16))
                for t in range(TILES):
                    dve.scalar_tensor_tensor(x[:, t, :], x[:, t, :], ss[:, t:t + 1], g[:, :], ALU.mult, ALU.mult)


def first_block(chip, io, x, params, rows):
    nc = chip.nc
    with ExitStack() as ctx:
        def sb(name, shape):
            return ctx.enter_context(nc.sbuf_tensor(name, shape, F32))
        fm = sb("fm", [P, DC, SEQ])
        v_first = sb("v_first", [P, WC, SEQ])
        merged = sb("merged", [P, DC, SEQ])
        o_fm = sb("o_fm", [P, WC, SEQ])
        for l in range(DEPTH):
            def par(name, c, l=l):
                at = PAR_AT[name, l] + c
                return params[:, at:at + 1]

            def row(name, l=l):
                at, n = ROW_AT[name, l]
                return rows[:, at:at + n]

            def by_gain(act, out, ps, c, par=par):
                return act.activation(out, ps, ACT.Copy, scale=par("norm_g", c))
            norm_to_fm(chip, x, fm, by_gain)
            mla(chip, l, io, par, row, fm, o_fm)
            merge(chip, l, io, fm, o_fm, COL["ga"], io["w_pa"][l], merged, True)
            fox(chip, l, io, par, row, fm, o_fm)
            merge(chip, l, io, fm, o_fm, COL["gb"], io["w_pb"][l], merged, False)
            rwkv(chip, l, io, par, fm, o_fm, v_first)
            merge(chip, l, io, fm, o_fm, COL["gc"], io["w_pc"][l], merged, False)
            loads, jobs = [], []
            for c in range(2):
                loads.append(cols_of(io["w_out"][l], c * BANK, BANK))

                def add(t, c=c):
                    dst = x[:, t, c * BANK:(c + 1) * BANK]
                    return lambda dve, ps: dve.tensor_tensor(dst, dst, ps, ALU.add)
                jobs += [j[:3] + ("dve",) + j[4:] for j in tm_jobs(c, merged, DC, BANK, 0, BANK, add)]
            gemm(chip, "out", loads, jobs)



PAR_LIST = [("norm_g", DC), ("qa_g", 2), ("kva_g", 1), ("mu", SHIFT // P), ("w0", WC), ("a0", WC), ("k_k", WC),
            ("k_a", WC), ("r_k", WC), ("lnx_g", WC), ("lnx_b", WC), ("v0", WC), ("b_f", 1)]
PAR_AT, N_PAR = {}, 0
for _l in range(DEPTH):
    for _name, _n in PAR_LIST:
        PAR_AT[_name, _l] = N_PAR
        N_PAR += _n
ROW_LIST = [("q_g", QK_A), ("knope_g", NOPE), ("krope_g", ROPE), ("fox_q_g", HD), ("fox_k_g", HD)]
ROW_AT, N_ROW = {}, 0
for _l in range(DEPTH):
    for _name, _n in ROW_LIST:
        ROW_AT[_name, _l] = (N_ROW, _n)
        N_ROW += _n


def bucket_starts():
    exact = NUM_BUCKETS // 2
    n = np.arange(exact, 4 * MAX_DISTANCE, dtype=np.float32)
    ratio = np.log(n / np.float32(exact)) / np.float32(np.log(MAX_DISTANCE / exact))
    bucket = np.minimum(exact + (ratio * (NUM_BUCKETS - exact)).astype(np.int32), NUM_BUCKETS - 1)
    starts = [-2.0 ** 31] + list(range(1, exact)) + [n[np.argmax(bucket >= b)] for b in range(exact, NUM_BUCKETS)]
    return np.array(starts, np.float32)


def shape_constants():
    i = np.arange(P)
    row, col = i[:, None], i[None, :]
    same = (row // CH) == (col // CH)
    sub = (row // SUB) == (col // SUB)
    strict, incl = same & (row < col), same & (row <= col)
    inv = np.float32(10000.0) ** (-np.arange(0, ROPE, 2, dtype=np.float32) / np.float32(ROPE))
    ang = np.arange(SEQ, dtype=np.float32)[:, None] * inv[None, :].astype(np.float32)
    def tok(a):
        return a.reshape(TILES, P, -1).transpose(1, 0, 2).reshape(P, -1)
    keep = np.tile((np.arange(SEQ) % CH != 0)[None, :], (P, 1))
    parts = [("ident", row == col), ("causal_add", np.where(col <= row, 0.0, MASKED)),
             ("head_ones", (row // HD) == (col // HD)),
             ("chunk_masks", np.concatenate([strict, incl, strict, incl], 1)),
             ("sub_lower", sub & (row > col)), ("sub_upper", sub & (row < col)), ("off_sub", ~sub),
             ("ones", np.ones((P, P))), ("bucket_from", np.tile(bucket_starts(), 4)[:, None]),
             ("rank8", np.tile(np.arange(8, 0, -1)[None, :], (P, 1))),
             ("chunk_keep", keep), ("cos", tok(np.cos(ang))), ("sin", tok(np.sin(ang)))]
    at, where = 0, {}
    for name, a in parts:
        where[name] = (at, a.shape[1])
        at += a.shape[1]
    return np.concatenate([a.astype(np.float32) for _, a in parts], 1), where


def program(nc, io, out):
    with ExitStack() as ctx:
        chip = Chip(nc, ctx)
        x = chip.sb("x", [P, TILES, D])
        const, where = shape_constants()
        consts = chip.sb("consts", [P, const.shape[1]])
        params = chip.sb("params", [P, N_PAR])
        rows = chip.sb("rows", [P, N_ROW])
        chip.name_tables({name: consts[:, at:at + n] for name, (at, n) in where.items()})
        with chip.stage("start") as st:
            loaded = st.count("inputs_loaded")

            @st.block.sync
            def _(sp):
                sp.dma_start(x[:, :, :], io["x"].rearrange("o (t p) d -> p (o t) d", p=P)).then_inc(*loaded.inc(16))
                sp.dma_start(consts[:, :], io["shape_consts"]).then_inc(*loaded.inc(16))
                sp.dma_start(params[:, :], io["params"]).then_inc(*loaded.inc(16))
                sp.dma_start(rows[:, :], io["rows"].to_broadcast([P, N_ROW])).then_inc(*loaded.inc(16))
                sp.wait_ge(*loaded.at(64))
        first_block(chip, io, x, params, rows)
        second_block(chip, io, x)
        with chip.stage("end") as st:
            stored = st.count("output_stored")

            @st.block.sync
            def _(sp):
                sp.dma_start(out.rearrange("o (t p) d -> p (o t) d", p=P), x[:, :, :]).then_inc(*stored.inc(16))
                sp.wait_ge(*stored.at(16))



SECOND = ["ada_w", "ab_w_in", "ab_w_out", "cd_w_in", "cd_w_out", "moe_w_gate", "moe_w_up", "moe_w_down"]
WHOLE = ["x", "w_in", "mla_w_uq", "mla_w_ukv", "rwkv_w_up", "rwkv_a_up", "rwkv_v_down", "rwkv_v_up",
         "w_pa", "w_pb", "w_pc", "w_out"]


def laid_out(inputs):
    def pad(v, n):
        v = np.asarray(v, np.float32).reshape(-1)
        return np.concatenate([v, np.zeros(n * P - v.size, np.float32)]).reshape(n, P).T
    of = {"norm_g": "norm_g", "qa_g": "mla_qa_g", "kva_g": "mla_kva_g", "mu": "rwkv_mu", "w0": "rwkv_w0", "a0": "rwkv_a0",
          "k_k": "rwkv_k_k", "k_a": "rwkv_k_a", "r_k": "rwkv_r_k", "lnx_g": "rwkv_lnx_g", "lnx_b": "rwkv_lnx_b", "b_f": "fox_b_f"}
    cols, rows = [], []
    for l in range(DEPTH):
        for name, n in PAR_LIST:
            if name == "v0":
                cols.append(pad(inputs["rwkv_v0"][l - 1] if l else np.zeros(0), n))
            else:
                cols.append(pad(inputs[of[name]][l], n))
        for name, n in ROW_LIST:
            rows.append(np.asarray(inputs[name if name.startswith("fox") else "mla_" + name][l]).reshape(1, n))
    arrays = {name: np.ascontiguousarray(inputs[name]) for name in WHOLE}
    arrays["params"] = np.ascontiguousarray(np.concatenate(cols, 1))
    arrays["rows"] = np.ascontiguousarray(np.concatenate(rows, 1))
    arrays["shape_consts"] = shape_constants()[0]
    arrays.update({name: np.ascontiguousarray(inputs[name + "_2"]) for name in SECOND})
    arrays["ada_b"] = np.ascontiguousarray(inputs["ada_b_2"])
    arrays["norm_rows"] = np.ascontiguousarray(np.concatenate(
        [np.asarray(inputs["norm_g_2"]).reshape(2 * DEPTH, D), np.asarray(inputs["final_norm_g_2"]).reshape(1, D)]))
    taps = [np.asarray(inputs[n][0]) for n in ("ab_conv_a_2", "ab_conv_b_2")]
    parts = [pad(inputs["c_2"], DC)] + [pad(t[j], WC) for t in taps for j in range(t.shape[0])]
    parts += [pad(inputs[n], WC) for n in ("ab_conv_b_bias_2", "ab_ln_g_2", "ab_ln_b_2")] + [pad(inputs["diff_norm_g_2"], 1)]
    arrays["params_2"] = np.ascontiguousarray(np.concatenate(parts, 1))
    arrays["router_w"] = np.ascontiguousarray(np.concatenate([inputs["moe_wr_g_2"], inputs["moe_wr_e_2"]], 2))
    arrays["router_b"] = np.ascontiguousarray(np.concatenate([inputs["moe_br_g_2"], inputs["moe_br_e_2"]], 1))
    arrays["diff_lam"] = np.asarray(inputs["diff_lam_2"]).reshape(1, 4 * HD)
    arrays["rel_bias"] = np.ascontiguousarray(inputs["rel_bias_2"])
    pos = np.asarray(inputs["positions_2"]).reshape(SEQ)
    arrays["pos_row"] = pos.reshape(1, SEQ)
    arrays["pos_col"] = np.ascontiguousarray(pos.reshape(TILES, P).T)
    arrays["pos_quarter"] = np.ascontiguousarray(pos.reshape(TILES, 4, P // 4).transpose(1, 0, 2).reshape(4, P))
    return arrays


def kernel(**inputs):
    import concourse.bacc as _bacc
    from concourse.bass_utils import run_bass_kernel_spmd as _run

    nc = _bacc.Bacc("TRN2", target_bir_lowering=False, num_devices=1)
    arrays = {f"in_{k}": v for k, v in laid_out(inputs).items()}
    io = {k[3:]: nc.dram_tensor(k, v.shape, mybir.dt.from_np(v.dtype), kind="ExternalInput").ap() for k, v in arrays.items()}
    out = nc.dram_tensor("out", (1, SEQ, D), F32, kind="ExternalOutput").ap()
    program(nc, io, out)
    r = _run(nc, [arrays], core_ids=[0])
    return r.results[0]["out"]
```

```python
from contextlib import ExitStack, nullcontext, contextmanager

import numpy as np

import concourse.bass as bass
from concourse import mybir

F32 = mybir.dt.float32
I32 = mybir.dt.int32
ALU = mybir.AluOpType
ACT = mybir.ActivationFunctionType
AX = mybir.AxisListType

P = 128
SEQ = 512
TILES = SEQ // P
D = 1024
DC = D // P
DEPTH = 2
BANK = 512

HEADS = 8
NOPE, ROPE, V_A, Q_LORA, KV_LORA = 64, 32, 64, 256, 128
HD = 64
QK_A = NOPE + ROPE
W = HEADS * HD
WC = W // P
SHIFT = 3 * W + 2 * HD
MV = 32
DECAY = 0.606531
GN_EPS = 64e-5
EPS = 1e-6
MASKED = -1e30
CH = 64
NCH = SEQ // CH
SUB = 16

COL = {}
_at = 0
for _name, _n in (("cq", Q_LORA), ("ckv", KV_LORA), ("kr", ROPE), ("gate_a", W), ("fq", W), ("fk", W), ("fv", W),
                  ("ff", HEADS), ("gate_b", W), ("shift", SHIFT), ("gate_c", W), ("ga", D), ("gb", D), ("gc", D)):
    COL[_name] = _at
    _at += _n
IN_COLS = _at


class Count:

    def __init__(self, sem):
        self.sem, self.base, self.total = sem, 0, 0

    def at(self, n):
        return self.sem, self.base + n

    def inc(self, n=1, times=1):
        self.total += n * times
        return self.sem, n


class Chip:

    def __init__(self, nc, ctx):
        self.nc, self.ctx = nc, ctx
        self.free, self.made = [], 0
        self.dirty, self.cleared = [], []
        self.bank = [ctx.enter_context(nc.psum_tensor(f"bank{i}", [P, BANK], F32)) for i in range(8)]

    def name_tables(self, t):
        self.ident, self.causal_add, self.ones, self.head_ones = t["ident"], t["causal_add"], t["ones"], t["head_ones"]
        self.chunk_masks = t["chunk_masks"].rearrange("p (n t) -> p n t", n=4)
        self.sub_lower, self.sub_upper, self.off_sub = t["sub_lower"], t["sub_upper"], t["off_sub"]
        self.before, self.block_starts, self.numbers, self.number = t["before"], t["block_starts"], t["numbers"], t["number"]
        self.chunk_keep, self.bucket_from, self.rank8 = t["chunk_keep"], t["bucket_from"], t["rank8"]
        self.cos = t["cos"].rearrange("p (t d) -> p t d", t=TILES)
        self.sin = t["sin"].rearrange("p (t d) -> p t d", t=TILES)

    def sb(self, name, shape, dt=F32):
        return self.ctx.enter_context(self.nc.sbuf_tensor(name, shape, dt))

    def new_count(self):
        self.made += 1
        return Count(self.ctx.enter_context(self.nc.semaphore(f"count{self.made}")))

    def clear_fresh(self):
        with self.stage("clear") as st:
            @st.block.sync
            def _(sp):
                for c in self.dirty:
                    sp.sem_clear(c.sem)
        self.cleared, self.dirty = self.dirty + self.cleared, []
        for c in self.cleared:
            c.total = 0

    @contextmanager
    def stage(self, name):
        st = Stage(self, name)
        with ExitStack() as ctx:
            st.ctx = ctx
            st.block = ctx.enter_context(self.nc.Block())
            yield st
        for c in st.counts:
            c.base += c.total
            c.total = 0
            self.free.append(c)


class Stage:
    serial = 0

    def __init__(self, chip, name):
        self.chip, self.name, self.counts = chip, name, []
        Stage.serial += 1
        self.id = Stage.serial

    def sb(self, name, shape, dt=F32):
        return self.ctx.enter_context(self.chip.nc.sbuf_tensor(f"{name}_{self.id}", shape, dt))

    def count(self, name, fresh=False):
        if fresh:
            c = self.chip.new_count() if not self.chip.cleared else self.chip.cleared.pop(0)
            self.chip.dirty.append(c)
            return c
        if self.chip.free:
            c = self.chip.free.pop(0)
        else:
            c = self.chip.new_count()
        self.counts.append(c)
        return c

    def chain(self, eng, name):
        c, n = self.count(name), [0]

        def link(ins):
            n[0] += 1
            ins.then_inc(*c.inc())
            eng.wait_ge(*c.at(n[0]))
        return link


def gemm(chip, name, loads, jobs, slots=3, stage=None):
    with (nullcontext(stage) if stage else chip.stage(name)) as st:
        weights = [st.sb(f"w{i}", [P, DC * 512]) for i in range(min(slots, len(loads)))]
        n_slots = len(weights)
        loaded = [[st.count("piece_loaded") for _ in range(2)] for _ in weights]
        summed = st.count("sums_ready")
        freed = {"act": st.count("bank_freed_by_act"), "dve": st.count("bank_freed_by_dve")}
        first_job, last_job = {}, {}
        for g, job in enumerate(jobs):
            first_job.setdefault(job[0], g)
            last_job[job[0]] = g
        pieces = [load(weights[i % n_slots]) for i, load in enumerate(loads)]

        def landed(i, n):
            return loaded[i % n_slots][n].at(16 * sum(len(pieces[j]) > n for j in range(i % n_slots, i + 1, n_slots)))

        def evacuated(g):
            who = jobs[g][3]
            return freed[who].at(sum(j[3] == who for j in jobs[:g + 1]))

        @st.block.sync
        def _(sp):
            for i, load in enumerate(loads):
                if i >= n_slots:
                    sp.wait_ge(*summed.at(last_job[i - n_slots] + 1))
                for n, (dst, src) in enumerate(pieces[i]):
                    sp.dma_start(dst, src).then_inc(*loaded[i % n_slots][n].inc(16))

        @st.block.tensor
        def _(pe):
            for g, job in enumerate(jobs):
                load, pairs, out = job[:3]
                if g >= 8:
                    pe.wait_ge(*evacuated(g - 8))
                todo, bank = pairs(weights[load % n_slots]), out(chip.bank[g % 8])
                for n, (lhsT, rhs) in enumerate(todo):
                    if first_job[load] == g and n % (len(todo) // len(pieces[load])) == 0:
                        pe.wait_ge(*landed(load, n * len(pieces[load]) // len(todo)))
                    ins = pe.matmul(bank, lhsT, rhs, start=(n == 0), stop=(n == len(todo) - 1))
                ins.then_inc(*summed.inc())

        def evacuate(eng, who):
            for g, job in enumerate(jobs):
                if job[3] == who:
                    eng.wait_ge(*summed.at(g + 1))
                    if len(job) > 5:
                        eng.wait_ge(*evacuated(job[5]))
                    job[4](eng, job[2](chip.bank[g % 8])).then_inc(*freed[who].inc())

        @st.block.scalar
        def _(act):
            evacuate(act, "act")

        @st.block.vector
        def _(dve):
            evacuate(dve, "dve")

    return evacuated


class Work:

    def __init__(self):
        self.loads, self.jobs = [], []

    def fm(self, act_fm, dram, c0, chunks, evac_of, eng="act", after=None):
        kc = dram.shape[0] // P
        for c in range(0, chunks, 4):
            n = min(4, chunks - c) * P
            self.loads.append(cols_of(dram, c0 + c * P, n))
            for i in range(n // P):
                job = fm_job(len(self.loads) - 1, act_fm, kc, n, i * P, P, eng, evac_of(c + i))
                self.jobs.append(job + ((after + c + i,) if after is not None else ()))
        return len(self.jobs) - chunks

    def tm(self, act_fm, dram, c0, n, evac, eng=None):
        kc = dram.shape[0] // P
        self.loads.append(cols_of(dram, c0, n))
        for j in tm_jobs(len(self.loads) - 1, act_fm, kc, n, 0, n, evac):
            self.jobs.append(j[:3] + (eng or j[3],) + j[4:])

    def run(self, chip, name):
        gemm(chip, name, self.loads, self.jobs)


def product(pe, out, pairs):
    for n, (lhsT, rhs) in enumerate(pairs):
        last = pe.matmul(out, lhsT, rhs, start=(n == 0), stop=(n == len(pairs) - 1))
    return last


def over(ap, shape, axis):
    return ap.unsqueeze(axis).to_broadcast(shape)



class Roots:

    def __init__(self, st):
        self.asked, self.rooted = st.count("square_ready"), st.count("root_ready")
        self.n = self.served = 0

    def serve(self, act, ap, factor=1.0):
        self.served += 1
        act.wait_ge(*self.asked.at(self.served))
        act.activation(ap, ap, ACT.Sqrt, scale=factor ** -2).then_inc(*self.rooted.inc())

    def __call__(self, dve, link, ap, ins):
        self.n += 1
        ins.then_inc(*self.asked.inc())
        dve.wait_ge(*self.rooted.at(self.n))
        link(dve.reciprocal(ap, ap))


def group_rms(dve, link, root, out, x, sq, r, n, gain=None):
    shape = list(x.shape)
    link(dve.tensor_tensor(sq, x, x, ALU.mult))
    link(dve.tensor_reduce(r, sq, AX.X, ALU.add))
    root(dve, link, r, dve.tensor_scalar(r, r, 1.0 / n, EPS, ALU.mult, ALU.add))
    link(dve.tensor_tensor(out, x, over(r, shape, 2), ALU.mult))
    if gain is not None:
        link(dve.tensor_tensor(out, out, over(gain, shape, 1), ALU.mult))


def rotate(dve, link, x, cos, sin, tmp, heads):
    h = ROPE // 2
    shape = [P, TILES, heads, h]
    c, s = over(cos, shape, 2), over(sin, shape, 2)
    x1, x2 = x[:, :, :, 0:h], x[:, :, :, h:ROPE]
    t = [tmp[:, i].rearrange("p (t h d) -> p t h d", t=TILES, h=heads) for i in range(4)]
    for i, (a, b) in enumerate(((x1, c), (x2, s), (x2, c), (x1, s))):
        ins = dve.tensor_tensor(t[i], a, b, ALU.mult)
        link(ins)
    link(dve.tensor_tensor(x1, t[0], t[1], ALU.subtract))
    link(dve.tensor_tensor(x2, t[2], t[3], ALU.add))



def norm_to_fm(chip, x, fm, finish, rows=None, normed_tm=None):
    with chip.stage("norm") as st:
        xn = normed_tm or st.sb("xn", [P, TILES, D])
        ss = st.sb("ss", [P, TILES])
        squared, normed = st.count("squares_summed"), st.count("tile_normed")
        turned, moved = st.count("chunk_transposed"), st.count("chunk_moved")

        root = Roots(st)

        @st.block.scalar
        def _(act):
            for t in range(TILES):
                act.activation(xn[:, t, :], x[:, t, :], ACT.Square, accum_out=ss[:, t:t + 1]).then_inc(*squared.inc())
            root.serve(act, ss[:, :])
            for c in range(DC):
                act.wait_ge(*turned.at(c + 1))
                finish(act, fm[:, c, :], chip.bank[c % 4][:, :], c).then_inc(*moved.inc())

        @st.block.vector
        def _(dve):
            link = st.chain(dve, "norm_step")
            dve.wait_ge(*squared.at(TILES))
            root(dve, link, ss[:, :], dve.tensor_scalar(ss[:, :], ss[:, :], 1.0 / D, EPS, ALU.mult, ALU.add))
            for t in range(TILES):
                if rows is None:
                    dve.tensor_scalar(xn[:, t, :], x[:, t, :], ss[:, t:t + 1], None, ALU.mult).then_inc(*normed.inc())
                else:
                    link(dve.scalar_tensor_tensor(xn[:, t, :], x[:, t, :], ss[:, t:t + 1], rows[0], ALU.mult, ALU.mult))
                    dve.tensor_tensor(xn[:, t, :], xn[:, t, :], rows[1], ALU.add).then_inc(*normed.inc())

        @st.block.tensor
        def _(pe):
            pe.wait_ge(*normed.at(TILES))
            for c in range(DC):
                if c >= 4:
                    pe.wait_ge(*moved.at(c - 3))
                for t in range(TILES):
                    last = pe.transpose(chip.bank[c % 4][:, t * P:(t + 1) * P], xn[:, t, c * P:(c + 1) * P], chip.ident)
                last.then_inc(*turned.inc())


def cols_of(dram, c0, n):
    kc = dram.shape[0] // P

    def load(slot):
        dst = slot[:, 0:kc * n].rearrange("p (k n) -> p k n", k=kc)
        src = dram[:, c0:c0 + n].rearrange("(k p) n -> p k n", p=P)
        if kc < 4:
            return [(dst, src)]
        return [(dst[:, a:a + kc // 2], src[:, a:a + kc // 2]) for a in (0, kc // 2)]
    return load


def tm_jobs(load, act_fm, kc, n, c0, cn, evac, start=0):
    jobs = []
    for t in range(TILES):
        def pairs(w, t=t):
            wv = w[:, 0:kc * n].rearrange("p (k n) -> p k n", k=kc)
            return [(act_fm[:, k, t * P:(t + 1) * P], wv[:, k, c0:c0 + cn]) for k in range(kc)]
        eng = "act" if t % 2 else "dve"
        jobs.append((load, pairs, lambda b, cn=cn: b[:, 0:cn], eng, evac(t)))
    return jobs


def fm_job(load, act_fm, kc, n, c0, cn, eng, evac):
    def pairs(w):
        wv = w[:, 0:kc * n].rearrange("p (k n) -> p k n", k=kc)
        return [(wv[:, k, c0:c0 + cn], act_fm[:, k, :]) for k in range(kc)]
    return (load, pairs, lambda b, cn=cn: b[0:cn, :], eng, evac)


def copy_to(dst):
    def fn(eng, psum):
        if eng.engine == mybir.EngineType.DVE:
            return eng.tensor_copy(dst, psum)
        return eng.activation(dst, psum, ACT.Copy)
    return fn


def attention(chip, name, q, k, v, dk, out_fm, gate, dv=HD, heads=HEADS, causal=True, scale=1.0, bias=None, masks=None,
              side=None):
    steps = heads * TILES
    with chip.stage(name) as st:
        qT = [st.sb(f"qT{i}", [dk, SEQ]) for i in range(2)]
        kT = [st.sb(f"kT{i}", [dk, SEQ]) for i in range(2)]
        prob = [st.sb(f"prob{i}", [P, SEQ]) for i in range(4)]
        pT = [st.sb(f"pT{i}", [P, TILES, SEQ]) for i in range(2)]
        nmax, sums = st.sb("nmax", [P, steps]), st.sb("sums", [P, steps])
        if bias is not None:
            bias_sb = [st.sb(f"bias{i}", [P, TILES, SEQ]) for i in range(2)]
            loaded = [st.count(f"bias{i}_loaded") for i in range(2)]
            parts = len(bias(0))
        turned, qmoved, kmoved = st.count("qk_transposed"), st.count("q_moved"), st.count("k_moved")
        scored, maxed, exped = st.count("scored"), st.count("max_found"), st.count("exp_done")
        normed, pturned, pmoved = st.count("probs_normed"), st.count("probs_transposed"), st.count("probs_moved")
        summed, stored = st.count("head_summed"), st.count("head_stored")
        side_h, side_jobs = side or (None, [])
        n_side = len(side_jobs)
        every = steps // max(n_side, 1)
        if side:
            side_w = [st.sb(f"side_w{i}", [P, DC, P]) for i in range(2)]
            side_loaded = [st.count(f"side_w{i}_loaded") for i in range(2)]
            side_summed, side_moved = st.count("side_summed"), st.count("side_moved")
        B = chip.bank
        width = [(i + 1) * P if causal else SEQ for i in range(TILES)]

        if bias is not None:
            @st.block.sync
            def _(sp):
                for h in range(heads):
                    if h >= 2:
                        sp.wait_ge(*maxed.at(TILES * (h - 1)))
                    for dst, src in bias(h):
                        sp.dma_start(dst(bias_sb[h % 2]), src).then_inc(*loaded[h % 2].inc(16))

        if side:
            @st.block.sync
            def _(sp):
                for n, (w, _) in enumerate(side_jobs):
                    if n >= 2:
                        sp.wait_ge(*side_summed.at(n - 1))
                    sp.dma_start(side_w[n % 2][:, :, :], w.rearrange("(k p) n -> p k n", p=P)).then_inc(*side_loaded[n % 2].inc(16))

        @st.block.tensor
        def _(pe):
            def side_product(n, part):
                if part == 0:
                    pe.wait_ge(*side_loaded[n % 2].at(16 * (n // 2 + 1)))
                    if n >= 1:
                        pe.wait_ge(*side_moved.at(n))
                for k_ in range(part * DC // every, (part + 1) * DC // every):
                    last = pe.matmul(B[7][:, :], side_w[n % 2][:, k_, :], side_h[:, k_, :], start=(k_ == 0), stop=(k_ == DC - 1))
                if part == every - 1:
                    last.then_inc(*side_summed.inc())

            def transpose_qk(h):
                if h >= 1:
                    pe.wait_ge(*qmoved.at(h))
                    pe.wait_ge(*kmoved.at(h))
                for t in range(TILES):
                    pe.transpose(B[0][0:dk, t * P:(t + 1) * P], q[:, t, h, :], chip.ident)
                    last = pe.transpose(B[1][0:dk, t * P:(t + 1) * P], k[:, t, h, :], chip.ident)
                last.then_inc(*turned.inc())

            def score(s):
                h, i = divmod(s, TILES)
                if i == 0:
                    pe.wait_ge(*qmoved.at(h + 1))
                    pe.wait_ge(*kmoved.at(h + 1))
                if s >= 2:
                    pe.wait_ge(*exped.at(s - 1))
                pe.matmul(B[2 + s % 2][:, 0:width[i]], qT[h % 2][:, i * P:(i + 1) * P], kT[h % 2][:, 0:width[i]],
                          start=True, stop=True).then_inc(*scored.inc())

            def transpose_probs(s):
                pe.wait_ge(*normed.at(s + 1))
                if s >= 2:
                    pe.wait_ge(*pmoved.at(s - 1))
                for j in range(width[s % TILES] // P):
                    last = pe.transpose(B[4 + s % 2][:, j * P:(j + 1) * P], prob[s % 4][:, j * P:(j + 1) * P], chip.ident)
                last.then_inc(*pturned.inc())

            def weigh(h):
                pe.wait_ge(*pmoved.at(TILES * (h + 1)))
                if h >= 1:
                    pe.wait_ge(*stored.at(h))
                for j in range(TILES):
                    a = j * P if causal else 0
                    p0 = out_fm(h).base_partition()
                    last = pe.matmul(B[6][p0:p0 + dv, a:SEQ], v(h, j), pT[h % 2][:, j, a:SEQ],
                                     start=(j == 0), stop=(j == TILES - 1))
                last.then_inc(*summed.inc())

            transpose_qk(0)
            for s in range(steps + 3):
                if s < steps:
                    score(s)
                    if s % TILES == 1 and s // TILES + 1 < heads:
                        transpose_qk(s // TILES + 1)
                    if s // every < n_side:
                        side_product(*divmod(s, every))
                if 2 <= s < steps + 2:
                    transpose_probs(s - 2)
                if s >= 3 and (s - 3) % TILES == TILES - 1:
                    weigh((s - 3) // TILES)

        @st.block.scalar
        def _(act):
            def move_q(h):
                act.wait_ge(*turned.at(h + 1))
                if h >= 2:
                    act.wait_ge(*scored.at(TILES * (h - 1)))
                act.activation(qT[h % 2][:, :], B[0][0:dk, :], ACT.Copy).then_inc(*qmoved.inc())

            move_q(0)
            for s in range(steps + 2):
                if s < steps:
                    act.wait_ge(*maxed.at(s + 1))
                    if s >= 4:
                        act.wait_ge(*pturned.at(s - 3))
                    n = width[s % TILES]
                    src = B[2 + s % 2][:, 0:n]
                    act.activation(prob[s % 4][:, 0:n], src, ACT.Exp, bias=nmax[:, s:s + 1],
                                   accum_out=sums[:, s:s + 1]).then_inc(*exped.inc())
                    if s % TILES == 1 and s // TILES + 1 < heads:
                        move_q(s // TILES + 1)
                if 0 < s <= steps and s % every == 0 and s // every <= n_side:
                    n = s // every - 1
                    act.wait_ge(*side_summed.at(n + 1))
                    act.activation(side_jobs[n][1], B[7][:, :], ACT.Copy).then_inc(*side_moved.inc())
                if s >= 2:
                    h, i = divmod(s - 2, TILES)
                    n = width[i]
                    act.wait_ge(*pturned.at(s - 1))
                    if h >= 2:
                        act.wait_ge(*summed.at(h - 1))
                    act.activation(pT[h % 2][:, 0:n // P, i * P:(i + 1) * P],
                                   B[4 + s % 2][:, 0:n].rearrange("p (j q) -> p j q", q=P), ACT.Copy).then_inc(*pmoved.inc())
            if side:
                act.wait_ge(*side_moved.at(n_side))
            for n in range(n_side):
                act.activation(side_jobs[n][1], side_jobs[n][1], ACT.Sigmoid)

        @st.block.vector
        def _(dve):
            link = st.chain(dve, "softmax_step")

            def move_k(h):
                dve.wait_ge(*turned.at(h + 1))
                if h >= 2:
                    dve.wait_ge(*scored.at(TILES * (h - 1)))
                dve.tensor_copy(kT[h % 2][:, :], B[1][0:dk, :]).then_inc(*kmoved.inc())

            def find_max(s):
                h, i = divmod(s, TILES)
                n = width[i]
                dve.wait_ge(*scored.at(s + 1))
                bank = B[2 + s % 2]
                if bias is None:
                    diag = bank[:, n - P:n]
                    link(dve.tensor_tensor(diag, diag, chip.causal_add, ALU.add))
                else:
                    if i == 0:
                        dve.wait_ge(*loaded[h % 2].at(16 * parts * (h // 2 + 1)))
                    link(dve.scalar_tensor_tensor(bank[:, :], bank[:, :], scale, bias_sb[h % 2][:, i, :], ALU.mult, ALU.add))
                    link(dve.tensor_tensor(bank[:, :], bank[:, :], masks[:, i, :], ALU.add))
                dve.tensor_reduce(nmax[:, s:s + 1], bank[:, 0:n], AX.X, ALU.max, negate=True).then_inc(*maxed.inc())

            def norm(s):
                n = width[s % TILES]
                dve.wait_ge(*exped.at(s + 1))
                link(dve.reciprocal(sums[:, s:s + 1], sums[:, s:s + 1]))
                dve.tensor_scalar(prob[s % 4][:, 0:n], prob[s % 4][:, 0:n], sums[:, s:s + 1], None,
                                  ALU.mult).then_inc(*normed.inc())

            def store(h):
                dve.wait_ge(*summed.at(h + 1))
                o = out_fm(h)
                src = B[6][o.base_partition():o.base_partition() + dv, :]
                if gate is None:
                    dve.tensor_copy(o, src).then_inc(*stored.inc())
                else:
                    dve.tensor_tensor(o, src, gate(h), ALU.mult).then_inc(*stored.inc())

            move_k(0)
            for s in range(steps + 4):
                if s < steps:
                    find_max(s)
                    if s % TILES == 1 and s // TILES + 1 < heads:
                        move_k(s // TILES + 1)
                if 1 <= s < steps + 1:
                    norm(s - 1)
                if s >= 3 and (s - 3) % TILES == TILES - 1 and s - 3 < steps:
                    store((s - 3) // TILES)


def head_rows(fm):
    return lambda h: fm[HD * (h % 2):HD * (h % 2) + HD, h // 2, :]


def gate_jobs(fm, w_in, c0, sg):
    return [(w_in[:, c0 + c * P:c0 + (c + 1) * P], sg[:, c, :]) for c in range(DC)]


def merge(chip, sg, o_fm, w_p, merged, first, gate=None):
    work = Work()
    after = None
    if gate is not None:
        h, w_in, c0 = gate
        after = work.fm(h, w_in, c0, DC, lambda c: lambda act, ps: act.activation(sg[:, c, :], ps, ACT.Sigmoid))
    dst = merged if first else sg
    work.fm(o_fm, w_p, 0, DC, lambda c: lambda dve, ps: dve.tensor_tensor(dst[:, c, :], ps, sg[:, c, :], ALU.mult), "dve", after)
    work.run(chip, "merge")
    if not first:
        with chip.stage("merge_sum") as st:
            @st.block.vector
            def _(dve):
                dve.tensor_tensor(merged[:, :, :], merged[:, :, :], sg[:, :, :], ALU.add)


def silu_gate(work, fm, dram, c0, gate):
    work.fm(fm, dram, c0, WC, lambda c: lambda act, ps: act.activation(gate[:, c, :], ps, ACT.Silu))



def mla(chip, l, io, par, row, fm, o_fm, sg):
    with ExitStack() as ctx:
        def sb(name, shape):
            return ctx.enter_context(chip.nc.sbuf_tensor(f"mla_{name}_{l}", shape, F32))
        w_in = io["w_in"][l]
        n_in = Q_LORA + KV_LORA + ROPE
        gate = sb("gate", [P, WC, SEQ])
        work = Work()
        silu_gate(work, fm, w_in, COL["gate_a"], gate)
        q, k = sb("q", [P, TILES, HEADS, QK_A]), sb("k", [P, TILES, HEADS, QK_A])
        v = sb("v", [P, TILES, HEADS, V_A])
        with ExitStack() as inner:
            def sbi(name, shape):
                return inner.enter_context(chip.nc.sbuf_tensor(f"mla_{name}_{l}", shape, F32))
            low = sbi("low", [P, TILES, n_in])
            cqT, ckvT = sbi("cqT", [P, 2, SEQ]), sbi("ckvT", [P, 1, SEQ])
            tmp, ss = sbi("tmp", [P, TILES, HEADS * QK_A]), sbi("ss", [P, TILES * HEADS])
            work.tm(fm, w_in, 0, n_in, lambda t: copy_to(low[:, t, :]))
            work.run(chip, "mla_in")
            with chip.stage("mla_norm") as st:
                normed, turned = st.count("low_normed"), st.count("low_transposed")
                root = Roots(st)

                @st.block.vector
                def _(dve):
                    link = st.chain(dve, "norm_step")
                    for a, n in ((0, Q_LORA), (Q_LORA, KV_LORA), (Q_LORA + KV_LORA, ROPE)):
                        gain = row("krope_g") if n == ROPE else None
                        group_rms(dve, link, root, low[:, :, a:a + n], low[:, :, a:a + n], tmp[:, :, 0:n], ss[:, 0:TILES], n, gain)
                    kr = low[:, :, Q_LORA + KV_LORA:n_in].unsqueeze(2)
                    rotate(dve, link, kr, chip.cos, chip.sin, tmp[:, :, 0:TILES * ROPE // 2], 1)
                    dve.tensor_copy(k[:, :, :, NOPE:QK_A],
                                    low[:, :, Q_LORA + KV_LORA:n_in].unsqueeze(2).to_broadcast([P, TILES, HEADS, ROPE])
                                    ).then_inc(*normed.inc())

                @st.block.tensor
                def _(pe):
                    pe.wait_ge(*normed.at(1))
                    for c in range(3):
                        for t in range(TILES):
                            last = pe.transpose(chip.bank[c][:, t * P:(t + 1) * P], low[:, t, c * P:(c + 1) * P], chip.ident)
                        last.then_inc(*turned.inc())

                @st.block.scalar
                def _(act):
                    for _ in range(3):
                        root.serve(act, ss[:, 0:TILES])
                    for c in range(3):
                        act.wait_ge(*turned.at(c + 1))
                        dst, gain = (cqT[:, c, :], par("qa_g", c)) if c < 2 else (ckvT[:, 0, :], par("kva_g", 0))
                        act.activation(dst, chip.bank[c][:, :], ACT.Copy, scale=gain)

            half = HEADS * QK_A // 2
            loads = [cols_of(io["mla_w_uq"][l], 0, 2 * half)] + [cols_of(io["mla_w_ukv"][l], 0, 2 * BANK)]
            jobs = []
            for c in range(2):
                jobs += tm_jobs(0, cqT, 2, 2 * half, c * half, half,
                                lambda t, c=c: copy_to(q[:, t, :, :].rearrange("p h d -> p (h d)")[:, c * half:(c + 1) * half]))
            for c in range(2):
                def pairs_of(t, c):
                    def pairs(w):
                        return [(ckvT[:, 0, t * P:(t + 1) * P], w[:, c * BANK:(c + 1) * BANK])]
                    return pairs
                for t in range(TILES):
                    def split(eng, ps, t=t, c=c):
                        kv = ps.rearrange("p (h d) -> p h d", h=4)
                        eng.tensor_copy(k[:, t, 4 * c:4 * c + 4, 0:NOPE], kv[:, :, 0:NOPE])
                        return eng.tensor_copy(v[:, t, 4 * c:4 * c + 4, :], kv[:, :, NOPE:2 * NOPE])
                    jobs.append((1, pairs_of(t, c), lambda b: b[:, :], "dve", split))
            gemm(chip, "mla_up", loads, jobs)
            with chip.stage("mla_heads") as st:
                root = Roots(st)

                @st.block.scalar
                def _(act):
                    root.serve(act, ss[:, :], QK_A ** -0.5)
                    root.serve(act, ss[:, :])

                @st.block.vector
                def _(dve):
                    link = st.chain(dve, "heads_step")
                    G = TILES * HEADS
                    qg = q[:, :, :, :].rearrange("p t h d -> p (t h) d")
                    kg = k[:, :, :, :].rearrange("p t h d -> p (t h) d")[:, :, 0:NOPE]
                    t96 = tmp[:, :, :].rearrange("p t (h d) -> p (t h) d", h=HEADS)
                    group_rms(dve, link, root, qg, qg, t96, ss[:, :], QK_A, row("q_g"))
                    rotate(dve, link, q[:, :, :, NOPE:QK_A], chip.cos, chip.sin,
                           tmp[:, :, 0:G * ROPE // 2], HEADS)
                    group_rms(dve, link, root, kg, kg, t96[:, :, 0:NOPE], ss[:, :], NOPE, row("knope_g"))
        attention(chip, "mla_attention", q, k, lambda h, j: v[:, j, h, :], QK_A, head_rows(o_fm), head_rows(gate),
                  side=(fm, gate_jobs(fm, w_in, COL["ga"], sg)))


def fox(chip, l, io, par, row, fm, o_fm, sg):
    DK = HD + 2
    with ExitStack() as ctx:
        def sb(name, shape):
            return ctx.enter_context(chip.nc.sbuf_tensor(f"fox_{name}_{l}", shape, F32))
        w_in = io["w_in"][l]
        gate = sb("gate", [P, WC, SEQ])
        work = Work()
        silu_gate(work, fm, w_in, COL["gate_b"], gate)
        q, k = sb("q", [P, TILES, HEADS, DK]), sb("k", [P, TILES, HEADS, DK])
        v = sb("v", [P, TILES, HEADS, HD])
        with ExitStack() as inner:
            def sbi(name, shape):
                return inner.enter_context(chip.nc.sbuf_tensor(f"fox_{name}_{l}", shape, F32))
            ff = sbi("ff", [HEADS, 3, SEQ])
            tmp, ss = sbi("tmp", [P, TILES, HEADS, HD]), sbi("ss", [P, TILES * HEADS])
            work.loads.append(cols_of(w_in, COL["ff"], HEADS))
            work.jobs.append(fm_job(len(work.loads) - 1, fm, DC, HEADS, 0, HEADS, "act",
                                    lambda act, ps: act.activation(ff[:, 0, :], ps, ACT.Identity, bias=par("b_f", 0)[0:HEADS])))
            for name, dst in (("fq", q), ("fk", k), ("fv", v)):
                def into(t, dst=dst):
                    def fn(eng, ps):
                        return copy_to(dst[:, t, :, 0:HD])(eng, ps.rearrange("p (h d) -> p h d", h=HEADS))
                    return fn
                work.tm(fm, w_in, COL[name], W, into)
            work.run(chip, "fox_in")

            with chip.stage("fox_heads") as st:
                absed, exped, logged = st.count("abs_ready"), st.count("exp_ready"), st.count("log_ready")
                summed, turned = st.count("cumsum_ready"), st.count("cumsum_transposed")
                root = Roots(st)

                @st.block.scalar
                def _(act):
                    act.wait_ge(*absed.at(1))
                    act.activation(ff[:, 1, :], ff[:, 1, :], ACT.Exp).then_inc(*exped.inc())
                    act.wait_ge(*exped.at(1))
                    act.activation(ff[:, 1, :], ff[:, 1, :], ACT.Ln, bias=1.0).then_inc(*logged.inc())
                    root.serve(act, ss[:, :], HD ** -0.5)
                    root.serve(act, ss[:, :])

                @st.block.vector
                def _(dve):
                    link = st.chain(dve, "heads_step")
                    link(dve.tensor_scalar(ff[:, 1, :], ff[:, 0, :], -1.0, None, ALU.mult))
                    dve.tensor_tensor(ff[:, 1, :], ff[:, 0, :], ff[:, 1, :], ALU.min).then_inc(*absed.inc())
                    link(dve.memset(ff[:, 2, :], 1.0))
                    dve.wait_ge(*logged.at(1))
                    link(dve.scalar_tensor_tensor(ff[:, 0, :], ff[:, 0, :], 0.0, ff[:, 1, :], ALU.min, ALU.subtract))
                    dve.tensor_tensor_scan(ff[:, 1, :], ff[:, 2, :], ff[:, 0, :], 0.0, ALU.mult, ALU.add).then_inc(*summed.inc())
                    G = TILES * HEADS
                    for x, gain in ((q, "fox_q_g"), (k, "fox_k_g")):
                        xg = x[:, :, :, :].rearrange("p t h d -> p (t h) d")[:, :, 0:HD]
                        group_rms(dve, link, root, xg, xg, tmp[:, :, :, :].rearrange("p t h d -> p (t h) d"), ss[:, :], HD,
                                  row(gain))
                    dve.wait_ge(*turned.at(1))
                    cum = chip.bank[0][:, 0:G].rearrange("p (t h) -> p t h", t=TILES)
                    dve.tensor_copy(q[:, :, :, HD], cum)
                    dve.memset(q[:, :, :, HD + 1], 1.0)
                    dve.memset(k[:, :, :, HD], 1.0)
                    dve.tensor_scalar(k[:, :, :, HD + 1], cum, -1.0, None, ALU.mult)

                @st.block.tensor
                def _(pe):
                    pe.wait_ge(*summed.at(1))
                    for t in range(TILES):
                        last = pe.transpose(chip.bank[0][:, t * HEADS:(t + 1) * HEADS], ff[:, 1, t * P:(t + 1) * P],
                                            chip.ident[0:HEADS, 0:HEADS])
                    last.then_inc(*turned.inc())
        attention(chip, "fox_attention", q, k, lambda h, j: v[:, j, h, :], DK, head_rows(o_fm), head_rows(gate),
                  side=(fm, gate_jobs(fm, w_in, COL["gb"], sg)))


def rwkv(chip, l, io, par, fm, o_fm, v_first):
    nc = chip.nc
    w_in = io["w_in"][l]
    with ExitStack() as ctx:
        def sb(name, shape):
            return ctx.enter_context(nc.sbuf_tensor(f"rwkv_{name}_{l}", shape, F32))
        bonus = o_fm
        left = sb("left", [P, WC, 2, SEQ])
        right = sb("right", [P, WC, 2, SEQ])
        vT = sb("v", [P, WC, SEQ])
        p_end = sb("p_end", [P, WC, NCH])
        with ExitStack() as inner:
            def sbi(name, shape):
                return inner.enter_context(nc.sbuf_tensor(f"rwkv_{name}_{l}", shape, F32))
            shifted = sbi("shifted", [P, 9, SEQ])
            r, k, lora = shifted[:, 0:4, :], shifted[:, 4:8, :], shifted[:, 8, :]
            lw = sbi("lw", [P, WC, SEQ])
            a = sbi("a", [P, WC, SEQ])
            wup = sbi("wup", [P, 2, W])
            lead = sbi("lead", [P, 2, SEQ + 1])
            n_chunks = SHIFT // P
            with chip.stage("rwkv_in") as st:
                weights = [st.sb(f"w{i}", [P, DC, P]) for i in range(3)]
                loaded = [st.count(f"w{i}_loaded") for i in range(3)]
                small = st.count("lora_loaded")
                summed, moved, freed = st.count("sums_ready"), st.count("chunk_moved"), st.count("chunk_shifted")

                @st.block.sync
                def _(sp):
                    sp.dma_start(wup[0:HD, 0, :], io["rwkv_w_up"][l]).then_inc(*small.inc(16))
                    sp.dma_start(wup[HD:P, 0, :], io["rwkv_a_up"][l]).then_inc(*small.inc(16))
                    for c in range(n_chunks):
                        if c >= 3:
                            sp.wait_ge(*summed.at(c - 2))
                        c0 = COL["shift"] + c * P
                        sp.dma_start(weights[c % 3][:, :, :], w_in[:, c0:c0 + P].rearrange("(k p) n -> p k n", p=P)
                                     ).then_inc(*loaded[c % 3].inc(16))
                    sp.wait_ge(*small.at(32))

                @st.block.tensor
                def _(pe):
                    for c in range(n_chunks):
                        pe.wait_ge(*loaded[c % 3].at(16 * (c // 3 + 1)))
                        if c >= 4:
                            pe.wait_ge(*moved.at(c - 3))
                        product(pe, chip.bank[c % 4][:, :], [(weights[c % 3][:, k_, :], fm[:, k_, :]) for k_ in range(DC)]
                                ).then_inc(*summed.inc())

                @st.block.scalar
                def _(act):
                    for n in range(2):
                        act.activation(lead[:, n, 0:1], chip.ident[:, 0:1], ACT.Copy, scale=0.0)
                    for c in range(n_chunks):
                        act.wait_ge(*summed.at(c + 1))
                        if c >= 2:
                            act.wait_ge(*freed.at(c - 1))
                        act.activation(lead[:, c % 2, 1:SEQ + 1], chip.bank[c % 4][:, :], ACT.Copy).then_inc(*moved.inc())

                @st.block.vector
                def _(dve):
                    link = st.chain(dve, "shift_step")
                    diff = st.sb("diff", [P, SEQ])
                    for c in range(n_chunks):
                        dst = r[:, c, :] if c < 4 else k[:, c - 4, :] if c < 8 else vT[:, c - 8, :] if c < 12 else lora
                        dve.wait_ge(*moved.at(c + 1))
                        x = lead[:, c % 2, :]
                        link(dve.tensor_tensor(diff[:, :], x[:, 0:SEQ], x[:, 1:SEQ + 1], ALU.subtract))
                        ins = dve.scalar_tensor_tensor(dst, diff[:, :], par("mu", c), x[:, 1:SEQ + 1], ALU.mult, ALU.add)
                        ins.then_inc(*freed.inc())
                        dve.wait_ge(*freed.at(c + 1))

            with chip.stage("rwkv_lora") as st:
                tanhed, summed, used = st.count("tanh_ready"), st.count("sums_ready"), st.count("sums_used")
                if l == 0:
                    @st.block.vector
                    def _(dve):
                        dve.tensor_copy(v_first[:, :, :], vT[:, :, :])
                else:
                    nu = lead[:, :, 0:SEQ]
                    vdown, vup, vd = st.sb("vdown", [P, WC, MV]), st.sb("vup", [MV, W]), st.sb("vd", [MV, SEQ])
                    vloaded, vdowned, vmoved = st.count("v_loaded"), st.count("v_down_done"), st.count("v_down_moved")
                    vsummed, nued, vdone = st.count("v_up_done"), st.count("nu_ready"), st.count("v_mixed")

                    @st.block.sync
                    def _(sp):
                        sp.dma_start(vdown[:, :, :], io["rwkv_v_down"][l - 1].rearrange("(k p) n -> p k n", p=P)
                                     ).then_inc(*vloaded.inc(16))
                        sp.dma_start(vup[:, :], io["rwkv_v_up"][l - 1]).then_inc(*vloaded.inc(16))

                    @st.block.vector
                    def _(dve):
                        link = st.chain(dve, "mix_step")
                        dve.wait_ge(*vdowned.at(1))
                        dve.tensor_copy(vd[:, :], chip.bank[4][0:MV, :]).then_inc(*vmoved.inc())
                        for c in range(WC):
                            diff = st.sb(f"vdiff{c}", [P, SEQ])
                            link(dve.tensor_tensor(diff[:, :], v_first[:, c, :], vT[:, c, :], ALU.subtract))
                            dve.wait_ge(*nued.at(c + 1))
                            link(dve.tensor_tensor(diff[:, :], diff[:, :], nu[:, c % 2, :], ALU.mult))
                            dve.tensor_tensor(vT[:, c, :], vT[:, c, :], diff[:, :], ALU.add).then_inc(*vdone.inc())

                @st.block.scalar
                def _(act):
                    act.activation(lora[0:HD, :], lora[0:HD, :], ACT.Tanh).then_inc(*tanhed.inc())
                    for c in range(WC):
                        act.wait_ge(*summed.at(c + 1))
                        act.activation(lw[:, c, :], chip.bank[2 * (c % 2)][:, :], ACT.Sigmoid, bias=par("w0", c))
                        act.activation(a[:, c, :], chip.bank[2 * (c % 2) + 1][:, :], ACT.Sigmoid,
                                       bias=par("a0", c)).then_inc(*used.inc())
                    if l > 0:
                        for c in range(WC):
                            act.wait_ge(*vsummed.at(c + 1))
                            if c >= 2:
                                act.wait_ge(*vdone.at(c - 1))
                            act.activation(nu[:, c % 2, :], chip.bank[5 + c % 2][:, :], ACT.Sigmoid,
                                           bias=par("v0", c)).then_inc(*nued.inc())

                @st.block.tensor
                def _(pe):
                    pe.wait_ge(*tanhed.at(1))
                    for c in range(WC):
                        if c >= 2:
                            pe.wait_ge(*used.at(c - 1))
                        cols = slice(c * P, (c + 1) * P)
                        pe.matmul(chip.bank[2 * (c % 2)][:, :], wup[0:HD, 0, cols], lora[0:HD, :], start=True, stop=True)
                        pe.matmul(chip.bank[2 * (c % 2) + 1][:, :], wup[HD:P, 0, cols], lora[HD:P, :],
                                  start=True, stop=True).then_inc(*summed.inc())
                    if l > 0:
                        pe.wait_ge(*vloaded.at(32))
                        product(pe, chip.bank[4][0:MV, :], [(vdown[:, c, :], vT[:, c, :]) for c in range(WC)]
                                ).then_inc(*vdowned.inc())
                        pe.wait_ge(*vmoved.at(1))
                        for c in range(WC):
                            if c >= 2:
                                pe.wait_ge(*nued.at(c - 1))
                            pe.matmul(chip.bank[5 + c % 2][:, :], vup[:, c * P:(c + 1) * P], vd[:, :],
                                      start=True, stop=True).then_inc(*vsummed.inc())

            with chip.stage("rwkv_operands") as st:
                cum, kk, e = st.sb("cum", [P, SEQ]), st.sb("kk", [P, SEQ]), st.sb("e", [P, 3, SEQ])
                km, sq = st.sb("km", [P, SEQ]), st.sb("sq", [P, SEQ])
                cummed, exped, consumed = st.count("cum_ready"), st.count("exps_ready"), st.count("exps_used")
                squared, normed = st.count("squares_ready"), st.count("norms_ready")
                rked, bonused = st.count("rk_ready"), st.count("bonus_summed")
                root = Roots(st)

                @st.block.tensor
                def _(pe):
                    for c in range(WC):
                        pe.wait_ge(*squared.at(c + 1))
                        pe.matmul(chip.bank[0][:, :], chip.head_ones, sq[:, :], start=True, stop=True).then_inc(*normed.inc())
                        pe.wait_ge(*rked.at(c + 1))
                        pe.matmul(chip.bank[1][:, :], chip.head_ones, sq[:, :], start=True, stop=True).then_inc(*bonused.inc())

                @st.block.scalar
                def _(act):
                    for c in range(WC):
                        act.wait_ge(*cummed.at(c + 1))
                        act.activation(e[:, 0, :], cum[:, :], ACT.Exp).then_inc(*exped.inc())
                        act.activation(e[:, 1, :], cum[:, :], ACT.Exp, scale=-1.0).then_inc(*exped.inc())
                        act.activation(e[:, 2, :], e[:, 2, :], ACT.Exp).then_inc(*exped.inc())
                        root.serve(act, sq[:, :])

                @st.block.vector
                def _(dve):
                    link = st.chain(dve, "operand_step")
                    for c in range(WC):
                        link(dve.tensor_scalar(lw[:, c, :], lw[:, c, :], -DECAY, None, ALU.mult))
                        link(dve.tensor_tensor_scan(cum[:, :], chip.chunk_keep, lw[:, c, :], 0.0, ALU.mult, ALU.add))
                        dve.tensor_tensor(e[:, 2, :], cum[:, :], lw[:, c, :], ALU.subtract).then_inc(*cummed.inc())
                        link(dve.tensor_scalar(kk[:, :], k[:, c, :], par("k_k", c), None, ALU.mult))
                        dve.tensor_tensor(sq[:, :], kk[:, :], kk[:, :], ALU.mult).then_inc(*squared.inc())
                        link(dve.tensor_scalar(km[:, :], a[:, c, :], 1.0, par("k_a", c), ALU.subtract, ALU.mult))
                        link(dve.scalar_tensor_tensor(km[:, :], km[:, :], 1.0, k[:, c, :], ALU.add, ALU.mult))
                        dve.wait_ge(*normed.at(c + 1))
                        root(dve, link, sq[:, :], dve.tensor_scalar(sq[:, :], chip.bank[0][:, :], 1e-24, None, ALU.max))
                        link(dve.tensor_tensor(kk[:, :], kk[:, :], sq[:, :], ALU.mult))
                        link(dve.tensor_tensor(sq[:, :], r[:, c, :], km[:, :], ALU.mult))
                        link(dve.tensor_scalar(sq[:, :], sq[:, :], par("r_k", c), None, ALU.mult))
                        dve.sem_inc(rked.sem, 1)
                        rked.inc()
                        dve.wait_ge(*exped.at(3 * c + 3))
                        link(dve.tensor_copy(p_end[:, c, :], e[:, 0, :].rearrange("p (n c) -> p n c", c=CH)[:, :, CH - 1]))
                        link(dve.tensor_tensor(right[:, c, 0, :], kk[:, :], e[:, 2, :], ALU.mult))
                        link(dve.tensor_tensor(right[:, c, 1, :], r[:, c, :], e[:, 0, :], ALU.mult))
                        link(dve.tensor_tensor(left[:, c, 1, :], km[:, :], e[:, 1, :], ALU.mult))
                        link(dve.tensor_tensor(kk[:, :], kk[:, :], a[:, c, :], ALU.mult))
                        link(dve.tensor_tensor(left[:, c, 0, :], kk[:, :], e[:, 1, :], ALU.mult))
                        dve.wait_ge(*bonused.at(c + 1))
                        link(dve.tensor_tensor(bonus[:, c, :], chip.bank[1][:, :], vT[:, c, :], ALU.mult))

        y = sb("y", [P, TILES, W])
        rwkv_core(chip, l, left, right, vT, p_end, y)

        gate, ln = sb("gate", [P, WC, SEQ]), sb("ln", [P, WC, SEQ])
        work = Work()
        silu_gate(work, fm, w_in, COL["gate_c"], gate)
        work.run(chip, "rwkv_gate")
        with chip.stage("rwkv_out") as st:
            sq, ms = st.sb("sq", [P, TILES * HEADS, HD]), st.sb("ms", [P, 2, TILES * HEADS])
            normed, turned, scaled = st.count("y_normed"), st.count("y_transposed"), st.count("y_scaled")
            root = Roots(st)

            @st.block.vector
            def _(dve):
                link = st.chain(dve, "out_step")
                yg = y[:, :, :].rearrange("p t (h d) -> p (t h) d", h=HEADS)
                shape = [P, TILES * HEADS, HD]
                link(dve.tensor_reduce(ms[:, 0, :], yg, AX.X, ALU.add))
                link(dve.tensor_scalar(ms[:, 0, :], ms[:, 0, :], 1.0 / HD, None, ALU.mult))
                link(dve.tensor_tensor(yg, yg, over(ms[:, 0, :], shape, 2), ALU.subtract))
                link(dve.tensor_tensor(sq[:, :, :], yg, yg, ALU.mult))
                link(dve.tensor_reduce(ms[:, 1, :], sq[:, :, :], AX.X, ALU.add))
                root(dve, link, ms[:, 1, :], dve.tensor_scalar(ms[:, 1, :], ms[:, 1, :], 1.0 / HD, GN_EPS, ALU.mult, ALU.add))
                dve.tensor_tensor(yg, yg, over(ms[:, 1, :], shape, 2), ALU.mult).then_inc(*normed.inc())
                for c in range(WC):
                    dve.wait_ge(*scaled.at(c + 1))
                    link(dve.tensor_tensor(o_fm[:, c, :], ln[:, c, :], bonus[:, c, :], ALU.add))
                    link(dve.tensor_tensor(o_fm[:, c, :], o_fm[:, c, :], gate[:, c, :], ALU.mult))

            @st.block.tensor
            def _(pe):
                pe.wait_ge(*normed.at(1))
                for c in range(WC):
                    for t in range(TILES):
                        last = pe.transpose(chip.bank[c][:, t * P:(t + 1) * P], y[:, t, c * P:(c + 1) * P], chip.ident)
                    last.then_inc(*turned.inc())

            @st.block.scalar
            def _(act):
                root.serve(act, ms[:, 1, :])
                for c in range(WC):
                    act.wait_ge(*turned.at(c + 1))
                    act.activation(ln[:, c, :], chip.bank[c][:, :], ACT.Identity, scale=par("lnx_g", c),
                                   bias=par("lnx_b", c)).then_inc(*scaled.inc())


def rwkv_core(chip, l, left, right, vT, p_end, y):
    nc = chip.nc
    with ExitStack() as ctx:
        def sb(name, shape):
            return ctx.enter_context(nc.sbuf_tensor(f"core_{name}_{l}", shape, F32))
        btm, ktm = sb("btm", [P, TILES, W]), sb("ktm", [P, TILES, W])
        vpar = sb("vpar", [P, 2, TILES, W])
        G = [sb(f"G{s}", [P, 4, 4, P]) for s in range(2)]
        M, Q, E, X = ([sb(f"{n}{s}", [P, 4, P]) for s in range(2)] for n in ("M", "Q", "E", "X"))
        M2, Q2 = ([sb(f"{n}{s}", [P, 4, P]) for s in range(2)] for n in ("M2", "Q2"))
        XT = M2
        state = [sb(f"state{s}", [P, 2, P]) for s in range(2)]
        neg_w = [sb(f"neg_w{s}", [P, 4, HD]) for s in range(2)]
        upd = [[sb(f"upd{s}{c}", [P, 4, HD]) for c in range(2)] for s in range(2)]

        with chip.stage("rwkv_turn") as st:
            turned, moved, zeroed = st.count("transposed"), st.count("moved"), st.count("zeroed")
            srcs = [("b", c) for c in range(WC)] + [("k", c) for c in range(WC)] + [("v", c) for c in range(WC)]

            def source(kind, c):
                return left[:, c, 0, :] if kind == "b" else left[:, c, 1, :] if kind == "k" else vT[:, c, :]

            @st.block.gpsimd
            def _(pool):
                for s in range(2):
                    pool.memset(state[s][:, :, :], 0.0)
                    pool.memset(neg_w[s][:, :, :], 0.0)
                    for c in range(2):
                        pool.memset(upd[s][c][:, :, :], 0.0)
                pool.memset(vpar[:, :, :, :], 0.0).then_inc(*zeroed.inc())

            @st.block.tensor
            def _(pe):
                for n, (kind, c) in enumerate(srcs):
                    if n >= 4:
                        pe.wait_ge(*moved.at(n - 3))
                    for t in range(TILES):
                        last = pe.transpose(chip.bank[n % 4][:, t * P:(t + 1) * P], source(kind, c)[:, t * P:(t + 1) * P],
                                            chip.ident)
                    last.then_inc(*turned.inc())

            @st.block.vector
            def _(dve):
                dve.wait_ge(*zeroed.at(1))
                for n, (kind, c) in enumerate(srcs):
                    dve.wait_ge(*turned.at(n + 1))
                    src = chip.bank[n % 4][:, :].rearrange("p (t f) -> p t f", t=TILES)
                    cols = slice(c * P, (c + 1) * P)
                    if kind == "v":
                        dve.tensor_copy(vpar[0:CH, 0, :, cols], src[0:CH])
                        dve.tensor_copy(vpar[CH:P, 1, :, cols], src[CH:P]).then_inc(*moved.inc())
                    else:
                        dve.tensor_copy((btm if kind == "b" else ktm)[:, :, cols], src).then_inc(*moved.inc())

        def phases(s, t):
            heads = range(4 * s, 4 * s + 4)
            tok = slice(t * P, (t + 1) * P)

            def half(h):
                return slice(HD * (h % 2), HD * (h % 2) + HD)

            def all_heads(bank):
                return bank[:, :].rearrange("p (h n) -> p h n", h=4)

            def each(pe, bank, lhsT, rhs):
                for i in range(4):
                    last = pe.matmul(bank[:, i * P:(i + 1) * P], lhsT[s][:, i, :], rhs[s][:, i, :], start=True, stop=True)
                return last

            def p_scores(pe, b):
                for i, h in enumerate(heads):
                    for n in range(2):
                        last = pe.matmul(b[i][:, 2 * n * P:2 * (n + 1) * P].rearrange("p (n t) -> p n t", n=2),
                                         left[half(h), h // 2, n, tok], right[half(h), h // 2, :, tok], start=True, stop=True)
                return last

            def e_scores(dve, link, b):
                for i in range(4):
                    last = dve.tensor_tensor(G[s][:, i, :, :], b[i][:, :].rearrange("p (n t) -> p n t", n=4),
                                             chip.chunk_masks, ALU.mult)
                return last
            yield p_scores, e_scores

            def p_turned(pe, b):
                for i, h in enumerate(heads):
                    last = pe.matmul(b[h % 2][:, (i // 2) * P:(i // 2 + 1) * P], right[half(h), h // 2, 0, tok],
                                     left[half(h), h // 2, 0, tok], start=True, stop=True)
                return last

            def e_turned(dve, link, b):
                for o in range(2):
                    dve.tensor_tensor(Q[s][:, :, :].rearrange("p (a o) n -> p a o n", o=2)[:, :, o, :],
                                      b[o][:, 0:2 * P].rearrange("p (a n) -> p a n", a=2),
                                      over(chip.sub_lower, [P, 2, P], 1), ALU.mult)
                dve.tensor_tensor(E[s][:, :, :], G[s][:, :, 0, :], over(chip.off_sub, [P, 4, P], 1), ALU.mult)
                link(dve.tensor_tensor(M[s][:, :, :], G[s][:, :, 0, :], over(chip.sub_upper, [P, 4, P], 1), ALU.mult))
                return dve.tensor_tensor(X[s][:, :, :], over(chip.ident, [P, 4, P], 1), M[s][:, :, :], ALU.subtract)
            yield p_turned, e_turned

            def square(m, q, m2, q2, update, last_one):
                def p(pe, b):
                    each(pe, b[0], q, m)
                    last = each(pe, b[1], m, q)
                    if update:
                        last = each(pe, b[2], q, X)
                    return last

                def e(dve, link, b):
                    dve.tensor_copy(m2[s][:, :, :], all_heads(b[0]))
                    last = dve.tensor_copy(q2[s][:, :, :], all_heads(b[1]))
                    if update:
                        last = dve.tensor_tensor(X[s][:, :, :], X[s][:, :, :], all_heads(b[2]), ALU.add)
                    return last
                return p, e
            yield square(M, Q, M2, Q2, False, False)
            yield square(M2, Q2, M, Q, True, False)
            yield square(M, Q, M2, Q2, True, True)

            def p_last(pe, b):
                return each(pe, b[0], Q2, X)

            def e_add(dve, link, b):
                return dve.tensor_tensor(X[s][:, :, :], X[s][:, :, :], all_heads(b[0]), ALU.add)
            yield p_last, e_add

            def p_xt(pe, b):
                for i in range(4):
                    last = pe.transpose(b[0][:, i * P:(i + 1) * P], X[s][:, i, :], chip.ident)
                return last
            yield p_xt, lambda dve, link, b: dve.tensor_copy(XT[s][:, :, :], all_heads(b[0]))

            def p_f(pe, b):
                each(pe, b[0], XT, E)
                return each(pe, b[1], E, XT)

            def e_f(dve, link, b):
                dve.tensor_copy(M[s][:, :, :], all_heads(b[0]))
                return dve.tensor_copy(Q[s][:, :, :], all_heads(b[1]))
            yield p_f, e_f
            yield (lambda pe, b: each(pe, b[0], M, Q)), (lambda dve, link, b: dve.tensor_copy(Q2[s][:, :, :], all_heads(b[0])))
            yield (lambda pe, b: each(pe, b[0], Q2, X)), e_add

            def e_sub(dve, link, b):
                return dve.tensor_tensor(X[s][:, :, :], X[s][:, :, :], all_heads(b[0]), ALU.subtract)
            yield (lambda pe, b: each(pe, b[0], Q, X)), e_sub

            for par_ in range(2):
                rows = slice(par_ * CH, (par_ + 1) * CH)

                def heads_v(i, par_=par_):
                    return vpar[:, par_, t, (4 * s + i) * HD:(4 * s + i + 1) * HD]

                def p_w(pe, b, heads_v=heads_v):
                    for pr in range(2):
                        pe.matmul(b[0][:, pr * P:(pr + 1) * P], right[:, 2 * s + pr, 0, tok], state[s][:, pr, :],
                                  start=True, stop=False, skip_group_check=True)
                        for i in (2 * pr, 2 * pr + 1):
                            last = pe.matmul(b[0][:, i * HD:(i + 1) * HD], G[s][:, i, 2, :], heads_v(i),
                                             start=False, stop=(i % 2 == 1), skip_group_check=True)
                    return last

                def e_w(dve, link, b, rows=rows):
                    return dve.tensor_scalar(neg_w[s][rows, :, :], b[0][rows, 0:4 * HD].rearrange("p (h v) -> p h v", h=4),
                                             -1.0, None, ALU.mult)
                yield p_w, e_w

                def p_u(pe, b):
                    for i in range(4):
                        last = pe.matmul(b[0][:, i * HD:(i + 1) * HD], X[s][:, i, :], neg_w[s][:, i, :], start=True, stop=True)
                    return last

                def e_u(dve, link, b, rows=rows, par_=par_):
                    return dve.tensor_copy(upd[s][par_][rows, :, :], b[0][rows, 0:4 * HD].rearrange("p (h v) -> p h v", h=4))
                yield p_u, e_u

                def p_y(pe, b, par_=par_, heads_v=heads_v):
                    for pr in range(2):
                        pe.matmul(b[1][:, pr * P:(pr + 1) * P], right[:, 2 * s + pr, 1, tok], state[s][:, pr, :],
                                  start=True, stop=False, skip_group_check=True)
                        for i in (2 * pr, 2 * pr + 1):
                            pe.matmul(b[1][:, i * HD:(i + 1) * HD], G[s][:, i, 1, :], upd[s][par_][:, i, :],
                                      start=False, stop=False, skip_group_check=True)
                            pe.matmul(b[1][:, i * HD:(i + 1) * HD], G[s][:, i, 3, :], heads_v(i),
                                      start=False, stop=(i % 2 == 1), skip_group_check=True)
                    for pr in range(2):
                        c0 = (2 * s + pr) * P
                        pe.matmul(b[0][:, pr * P:(pr + 1) * P], btm[:, t, c0:c0 + P],
                                  upd[s][par_][:, 2 * pr:2 * pr + 2, :], start=True, stop=False)
                        last = pe.matmul(b[0][:, pr * P:(pr + 1) * P], ktm[:, t, c0:c0 + P],
                                         vpar[:, par_, t, c0:c0 + P], start=False, stop=True)
                    return last

                def e_y(dve, link, b, rows=rows, par_=par_):
                    dve.tensor_copy(y[rows, t, 4 * s * HD:(4 * s + 4) * HD], b[1][rows, 0:4 * HD])
                    link(dve.tensor_tensor(state[s][:, :, :], b[0][:, 0:2 * P].rearrange("p (r v) -> p r v", r=2),
                                           state[s][:, :, :], ALU.add))
                    for pr in range(2):
                        last = dve.scalar_tensor_tensor(state[s][:, pr, :], state[s][:, pr, :],
                                                        p_end[:, 2 * s + pr, 2 * t + par_:2 * t + par_ + 1],
                                                        chip.head_ones, ALU.mult, ALU.mult)
                    return last
                yield p_y, e_y

        with chip.stage("rwkv_chunks") as st:
            done, moved = st.count("products_done"), st.count("results_moved")
            rounds = [ph for t in range(TILES) for pair in zip(phases(0, t), phases(1, t)) for ph in pair]

            @st.block.tensor
            def _(pe):
                for n, (products, _) in enumerate(rounds):
                    if n >= 2:
                        pe.wait_ge(*moved.at(n - 1))
                    products(pe, chip.bank[4 * (n % 2):4 * (n % 2) + 4]).then_inc(*done.inc())

            @st.block.vector
            def _(dve):
                link = st.chain(dve, "chunk_step")
                for n, (_, move) in enumerate(rounds):
                    dve.wait_ge(*done.at(n + 1))
                    move(dve, link, chip.bank[4 * (n % 2):4 * (n % 2) + 4]).then_inc(*moved.inc())



CONV_A, CONV_B = 3, 31
NUM_BUCKETS, MAX_DISTANCE = 32, 128
IDX_HEADS, IDX_DIM = 8, 32
TOPK = min(256, SEQ // 4)
TAKEN = -3e38
DIFF_HEADS, DIFF_V = 4, 128
BIAS_HEADS = HEADS + DIFF_HEADS
GROUPS, PER_GROUP = 4, 8
EXPERTS = GROUPS * PER_GROUP
D_EXP = 512
FC = D_EXP // P
SLOTS = 64
ITEMS = 2 * SEQ // SLOTS + EXPERTS + 4
FAR = 16384.0

P2_AT = {}
N_P2 = 0
for _name, _n in (("c", DC), ("conv_a", CONV_A * WC), ("conv_b", CONV_B * WC), ("conv_b_bias", WC), ("ln_g", WC),
                  ("ln_b", WC), ("diff_norm_g", 1)):
    P2_AT[_name] = N_P2
    N_P2 += _n
CD = {}
_at = 0
for _name, _n in (("q_c", W), ("k_c", W), ("v_c", W), ("q_idx", IDX_HEADS * IDX_DIM), ("k_idx", IDX_DIM),
                  ("w_idx", IDX_HEADS), ("q_d", W), ("k_d", W), ("v_d", W)):
    CD[_name] = _at
    _at += _n


def modulation(chip, i, io, par, mod):
    with ExitStack() as ctx:
        cond = ctx.enter_context(chip.nc.sbuf_tensor(f"cond_{i}", [P, DC, P], F32))
        gains = ctx.enter_context(chip.nc.sbuf_tensor(f"gains_{i}", [P, 2, D], F32))
        with chip.stage("condition") as st:
            loaded = st.count("rows_loaded")

            @st.block.scalar
            def _(act):
                c = par("c")
                act.activation(cond[:, :, :], over(c, [P, DC, P], 2), ACT.Silu)

            @st.block.sync
            def _(sp):
                sp.dma_start(mod[:, :, :].rearrange("p a d -> p (a d)"), io["ada_b"][i:i + 1, :].to_broadcast([P, 6 * D])
                             ).then_inc(*loaded.inc(16))
                for n in range(2):
                    sp.dma_start(gains[:, n, :], io["norm_rows"][2 * i + n:2 * i + n + 1, :].to_broadcast([P, D])
                                 ).then_inc(*loaded.inc(16))
                sp.wait_ge(*loaded.at(48))
        loads, jobs = [], []
        flat = mod[:, :, :].rearrange("p a d -> p (a d)")
        for c in range(6 * D // BANK):
            loads.append(cols_of(io["ada_w"][i], c * BANK, BANK))

            def pairs(w):
                wv = w[:, :].rearrange("p (k n) -> p k n", k=DC)
                return [(cond[:, k, :], wv[:, k, :]) for k in range(DC)]

            def add(dve, ps, c=c):
                dst = flat[:, c * BANK:(c + 1) * BANK]
                return dve.tensor_tensor(dst, dst, ps, ALU.add)
            jobs.append((c, pairs, lambda b: b[:, :], "dve", add))
        gemm(chip, "modulation", loads, jobs)
        with chip.stage("scales") as st:
            @st.block.vector
            def _(dve):
                for n in range(2):
                    s = mod[:, 3 * n + 1, :]
                    dve.scalar_tensor_tensor(s, s, 1.0, gains[:, n, :], ALU.add, ALU.mult)


def plain(act, out, ps, c):
    return act.activation(out, ps, ACT.Copy)


def add_gated(chip, name, x, y_fm, w, gate_row):
    with ExitStack() as ctx:
        y = ctx.enter_context(chip.nc.sbuf_tensor(f"{name}_y_{Stage.serial}", [P, TILES, D], F32))
        loads, jobs = [], []
        for c in range(2):
            loads.append(cols_of(w, c * BANK, BANK))
            cols = slice(c * BANK, (c + 1) * BANK)

            def gated(t, cols=cols):
                return lambda dve, ps: dve.tensor_tensor(y[:, t, cols], ps, gate_row[:, cols], ALU.mult)
            jobs += [j[:3] + ("dve",) + j[4:] for j in tm_jobs(c, y_fm, DC, BANK, 0, BANK, gated)]
        gemm(chip, name, loads, jobs)
        with chip.stage("residual") as st:
            @st.block.vector
            def _(dve):
                dve.tensor_tensor(x[:, :, :], x[:, :, :], y[:, :, :], ALU.add)


def conv_mixers(chip, io, par, fm, x, gate_row):
    w_in = io["ab_w_in"][0]
    with ExitStack() as ctx:
        def sb(name, shape):
            return ctx.enter_context(chip.nc.sbuf_tensor(f"conv_{name}", shape, F32))
        y_fm = sb("y", [P, DC, SEQ])
        with ExitStack() as inner:
            def sbi(name, shape):
                return inner.enter_context(chip.nc.sbuf_tensor(f"conv_{name}", shape, F32))
            ua, ub = sbi("ua", [P, WC, CONV_A - 1 + SEQ]), sbi("ub", [P, WC, CONV_B - 1 + SEQ])
            gb, acc = sbi("gate_b", [P, WC, SEQ]), sbi("acc", [P, WC, SEQ])
            sq = sbi("sq", [P, WC, SEQ])
            la, lb = CONV_A - 1, CONV_B - 1
            work = Work()
            glu = work.fm(fm, w_in, 4 * W, WC, lambda c: lambda act, ps: act.activation(sq[:, c, :], ps, ACT.Sigmoid))
            work.fm(fm, w_in, 3 * W, WC, lambda c: lambda dve, ps: dve.tensor_tensor(ub[:, c, lb:], ps, sq[:, c, :], ALU.mult),
                    "dve", glu)
            work.run(chip, "conv_in")
            with chip.stage("conv") as st:
                tapped = st.count("tap_added")
                squared, summed, centred, varied = st.count("squared"), st.count("means"), st.count("centred"), st.count("variances")
                root = Roots(st)
                meanb, rstd = st.sb("mean", [P, SEQ]), st.sb("rstd", [P, SEQ])
                work = Work()
                work.fm(fm, w_in, W, WC, lambda c: copy_to(y_fm[:, WC + c, :]))
                work.fm(fm, w_in, 2 * W, WC, lambda c: copy_to(ua[:, c, la:]))
                work.fm(fm, w_in, 0, WC, lambda c: copy_to(gb[:, c, :]))
                projected = gemm(chip, "conv_in", work.loads, work.jobs, stage=st)

                @st.block.vector
                def _(dve):
                    link = st.chain(dve, "conv_step")
                    link(dve.memset(ua[:, :, 0:la], 0.0))
                    link(dve.memset(ub[:, :, 0:lb], 0.0))

                    def convolve(u, taps, name, dst, n):
                        for j in range(taps):
                            for c in range(WC):
                                o, s, wj = dst[:, c, :], u[:, c, j:j + SEQ], par(name)[:, j * WC + c:j * WC + c + 1]
                                if j == 0 and name == "conv_b":
                                    ins = dve.tensor_scalar(o, s, wj, par("conv_b_bias")[:, c:c + 1], ALU.mult, ALU.add)
                                elif j == 0:
                                    ins = dve.tensor_scalar(o, s, wj, None, ALU.mult)
                                else:
                                    dve.wait_ge(*tapped.at(n - WC + 1))
                                    ins = dve.scalar_tensor_tensor(o, s, wj, o, ALU.mult, ALU.add)
                                ins.then_inc(*tapped.inc())
                                n += 1
                        dve.wait_ge(*tapped.at(n))
                        return n

                    n = convolve(ub, CONV_B, "conv_b", acc, 0)
                    dve.sem_inc(squared.sem, 1)
                    squared.inc()
                    dve.wait_ge(*projected(len(work.jobs) - 1))
                    link(dve.tensor_tensor(ua[:, :, la:], ua[:, :, la:], y_fm[:, WC:, :], ALU.mult))
                    convolve(ua, CONV_A, "conv_a", y_fm, n)
                    link(dve.tensor_tensor(y_fm[:, 0:WC, :], y_fm[:, 0:WC, :], gb[:, :, :], ALU.mult))
                    dve.wait_ge(*summed.at(1))
                    link(dve.tensor_scalar(meanb[:, :], chip.bank[0][:, :], 1.0 / W, None, ALU.mult))
                    link(dve.tensor_tensor(acc[:, :, :], acc[:, :, :], over(meanb[:, :], [P, WC, SEQ], 1), ALU.subtract))
                    dve.tensor_tensor(sq[:, :, :], acc[:, :, :], acc[:, :, :], ALU.mult).then_inc(*squared.inc())
                    dve.wait_ge(*varied.at(1))
                    root(dve, link, rstd[:, :], dve.tensor_scalar(rstd[:, :], chip.bank[1][:, :], 1.0 / W, EPS, ALU.mult, ALU.add))
                    dve.tensor_tensor(acc[:, :, :], acc[:, :, :], over(rstd[:, :], [P, WC, SEQ], 1), ALU.mult).then_inc(*centred.inc())

                @st.block.tensor
                def _(pe):
                    pe.wait_ge(*squared.at(1))
                    pe.wait_ge(*projected(len(work.jobs) - 1))
                    product(pe, chip.bank[0][:, :], [(chip.ones, acc[:, c, :]) for c in range(WC)]).then_inc(*summed.inc())
                    pe.wait_ge(*squared.at(2))
                    product(pe, chip.bank[1][:, :], [(chip.ones, sq[:, c, :]) for c in range(WC)]).then_inc(*varied.inc())

                @st.block.scalar
                def _(act):
                    root.serve(act, rstd[:, :])
                    act.wait_ge(*centred.at(1))
                    for c in range(WC):
                        act.activation(y_fm[:, WC + c, :], acc[:, c, :], ACT.Silu, scale=par("ln_g")[:, c:c + 1],
                                       bias=par("ln_b")[:, c:c + 1])
        add_gated(chip, "conv_out", x, y_fm, io["ab_w_out"][0], gate_row)


def position_bias(chip, io, scratch):
    Q4 = P // 4
    with chip.stage("position_bias") as st:
        table, before = st.sb("table", [P, 4 * BIAS_HEADS]), st.sb("before", [P, 4 * BIAS_HEADS])
        posi, pos = st.sb("posi", [P, SEQ + P], I32), st.sb("pos", [P, SEQ + P])
        steps_ = [st.sb(f"step{i}", [P, SEQ]) for i in range(4)]
        outs = [st.sb(f"out{i}", [4 * BIAS_HEADS, 4, SEQ]) for i in range(3)]
        cleared, loaded, ready = st.count("cleared"), st.count("loaded"), st.count("table_ready")
        stepped, summed, moved, stored = st.count("steps_ready"), st.count("summed"), st.count("moved"), [
            st.count(f"stored{i}") for i in range(3)]

        @st.block.gpsimd
        def _(pool):
            pool.memset(table[:, :], 0.0)
            pool.memset(before[:, :], 0.0).then_inc(*cleared.inc())

        @st.block.sync
        def _(sp):
            sp.wait_ge(*cleared.at(1))
            for n in range(4):
                rows, cols = slice(Q4 * n, Q4 * (n + 1)), slice(BIAS_HEADS * n, BIAS_HEADS * (n + 1))
                sp.dma_start(table[rows, cols], io["rel_bias"]).then_inc(*loaded.inc(16))
                sp.dma_start(before[Q4 * n + 1:Q4 * (n + 1), cols], io["rel_bias"][0:NUM_BUCKETS - 1, :]).then_inc(*loaded.inc(16))
                sp.dma_start(posi[rows, SEQ:SEQ + P], io["pos_quarter"][n:n + 1, :].to_broadcast([Q4, P])).then_inc(*loaded.inc(16))
            sp.dma_start(posi[:, 0:SEQ], io["pos_row"].to_broadcast([P, SEQ])).then_inc(*loaded.inc(16))
            for b in range(P // 4):
                sp.wait_ge(*moved.at(4 * (b + 1)))
                dst = scratch.rearrange("a t n k -> a (t n) k")[:, 4 * b:4 * b + 4, :]
                sp.dma_start(dst, outs[b % 3][:, :, :]).then_inc(*stored[b % 3].inc(16))
            for i in range(3):
                sp.wait_ge(*stored[i].at(stored[i].total))

        @st.block.vector
        def _(dve):
            link = st.chain(dve, "bias_step")
            dve.wait_ge(*loaded.at(16 * 13))
            link(dve.tensor_tensor(table[:, :], table[:, :], before[:, :], ALU.subtract))
            link(dve.tensor_copy(pos[:, :], posi[:, :]))
            link(dve.tensor_scalar(pos[:, SEQ:SEQ + P], pos[:, SEQ:SEQ + P], chip.bucket_from, None, ALU.subtract))
            for g in range(P):
                if g >= 4:
                    dve.wait_ge(*summed.at(g - 3))
                dve.tensor_scalar(steps_[g % 4][:, :], pos[:, 0:SEQ], pos[:, SEQ + g:SEQ + g + 1], None, ALU.is_le
                                  ).then_inc(*stepped.inc())

        @st.block.tensor
        def _(pe):
            for g in range(P):
                pe.wait_ge(*stepped.at(g + 1))
                if g >= 8:
                    pe.wait_ge(*moved.at(g - 7))
                pe.matmul(chip.bank[g % 8][0:4 * BIAS_HEADS, :], table[:, :], steps_[g % 4][:, :], start=True, stop=True
                          ).then_inc(*summed.inc())

        @st.block.scalar
        def _(act):
            for g in range(P):
                b = g // 4
                if g % 4 == 0 and b >= 3:
                    act.wait_ge(*stored[b % 3].at(16 * (b // 3)))
                act.wait_ge(*summed.at(g + 1))
                act.activation(outs[b % 3][:, g % 4, :], chip.bank[g % 8][0:4 * BIAS_HEADS, :], ACT.Copy).then_inc(*moved.inc())


def attn_mixers(chip, io, par, fm, x, gate_row, scratch):
    w_in = io["cd_w_in"][0]
    lambda_init = 0.8 - 0.6 * float(np.exp(-0.3))
    with ExitStack() as ctx:
        def sb(name, shape, dt=F32):
            return ctx.enter_context(chip.nc.sbuf_tensor(f"attn_{name}", shape, dt))
        y_fm = sb("y", [P, DC, SEQ])
        causal = sb("causal", [P, TILES, SEQ])
        masks = sb("masks", [P, TILES, SEQ])

        def heads_in(names, dsts, eng=None, stage=None):
            work = Work()
            for name, dst in zip(names, dsts):
                work.tm(fm, w_in, CD[name], W, lambda t, dst=dst: copy_to(dst[:, t, :, :].rearrange("p h d -> p (h d)")), eng=eng)
            gemm(chip, "attn_in", work.loads, work.jobs, stage=stage)

        def bias_of(h):
            def part(n):
                rows = slice(32 * n, 32 * n + 32)
                return lambda buf: buf[rows, :, :]
            return [(part(n), scratch[n * BIAS_HEADS + h].rearrange("t n k -> n t k")) for n in range(4)]

        with ExitStack() as outer:
            q, k, v = (outer.enter_context(chip.nc.sbuf_tensor(f"topk_{n}", [P, TILES, HEADS, HD], F32)) for n in "qkv")
            with ExitStack() as inner:
                def sbi(name, shape, dt=F32):
                    return inner.enter_context(chip.nc.sbuf_tensor(f"idx_{name}", shape, dt))
                qiT, kiT, wi = sbi("q", [P, 2, SEQ]), sbi("k", [P, SEQ]), sbi("w", [P, TILES, IDX_HEADS])
                posi, pos = sbi("posi", [P, SEQ + TILES], I32), sbi("pos", [P, SEQ + TILES])
                nq, nk = IDX_HEADS * IDX_DIM, IDX_DIM

                def k_four(slot):
                    view = slot[:, 0:DC * P].rearrange("p (k r n) -> p k r n", k=DC, r=4)
                    return view, w_in[:, CD["k_idx"]:CD["k_idx"] + nk].rearrange("(k p) n -> p k n", p=P)
                loads = [cols_of(w_in, CD["q_idx"], nq), cols_of(w_in, CD["w_idx"], IDX_HEADS)]
                jobs = [fm_job(0, fm, DC, nq, c * P, P, "act", copy_to(qiT[:, c, :])) for c in range(2)]
                jobs += [j[:3] + ("act",) + j[4:] for j in tm_jobs(1, fm, DC, IDX_HEADS, 0, IDX_HEADS,
                         lambda t: lambda act, ps: act.activation(wi[:, t, :], ps, ACT.Copy, scale=(IDX_DIM * IDX_HEADS) ** -0.5))]
                gemm(chip, "index_in", loads, jobs)
                with chip.stage("index_key") as st:
                    wk = st.sb("wk", [P, DC, 4, nk])
                    loaded, summed = st.count("loaded"), st.count("summed")
                    converted = st.count("converted")

                    @st.block.sync
                    def _(sp):
                        for r in range(4):
                            sp.dma_start(wk[:, :, r, :], w_in[:, CD["k_idx"]:CD["k_idx"] + nk].rearrange("(k p) n -> p k n", p=P)
                                         ).then_inc(*loaded.inc(16))
                        sp.dma_start(posi[:, 0:SEQ], io["pos_row"].to_broadcast([P, SEQ])).then_inc(*converted.inc(16))
                        sp.dma_start(posi[:, SEQ:SEQ + TILES], io["pos_col"]).then_inc(*converted.inc(16))

                    @st.block.tensor
                    def _(pe):
                        pe.wait_ge(*loaded.at(64))
                        product(pe, chip.bank[0][:, :], [(wk[:, k, :, :].rearrange("p r n -> p (r n)"), fm[:, k, :]) for k in range(DC)]
                                ).then_inc(*summed.inc())

                    @st.block.scalar
                    def _(act):
                        act.wait_ge(*summed.at(1))
                        act.activation(kiT[:, :], chip.bank[0][:, :], ACT.Copy)

                    @st.block.vector
                    def _(dve):
                        link = st.chain(dve, "mask_step")
                        dve.wait_ge(*converted.at(32))
                        link(dve.tensor_copy(pos[:, :], posi[:, :]))
                        for t in range(TILES):
                            dve.tensor_scalar(causal[:, t, :], pos[:, 0:SEQ], pos[:, SEQ + t:SEQ + t + 1], MASKED, ALU.is_gt, ALU.mult)

                with chip.stage("top_keys") as st:
                    rel = [st.sb(f"rel{i}", [P, SEQ]) for i in range(2)]
                    best = st.sb("best", [P, TILES, 8])
                    summed, rectified, added = st.count("index_scored"), st.count("rectified"), st.count("added")

                    @st.block.tensor
                    def _(pe):
                        for n in range(TILES * IDX_HEADS):
                            t, h = divmod(n, IDX_HEADS)
                            if n >= 4:
                                pe.wait_ge(*rectified.at(n - 3))
                            rows = slice(IDX_DIM * (h % 4), IDX_DIM * (h % 4 + 1))
                            pe.matmul(chip.bank[n % 4][:, :], qiT[rows, h // 4, t * P:(t + 1) * P], kiT[rows, :], start=True, stop=True,
                                      tile_position=(IDX_DIM * (h % 4), 0)).then_inc(*summed.inc())

                    @st.block.scalar
                    def _(act):
                        for n in range(TILES * IDX_HEADS):
                            act.wait_ge(*summed.at(n + 1))
                            if n >= 2:
                                act.wait_ge(*added.at(n - 1))
                            act.activation(rel[n % 2][:, :], chip.bank[n % 4][:, :], ACT.Relu).then_inc(*rectified.inc())

                    @st.block.tensor
                    def _(pe):
                        pe.wait_ge(*rectified.at(TILES * IDX_HEADS))
                    heads_in(("q_c", "k_c", "v_c"), (q, k, v), eng="act", stage=st)

                    @st.block.vector
                    def _(dve):
                        link = st.chain(dve, "top_step")
                        for n in range(TILES * IDX_HEADS):
                            t, h = divmod(n, IDX_HEADS)
                            dve.wait_ge(*rectified.at(n + 1))
                            base = causal[:, t, :] if h == 0 else masks[:, t, :]
                            dve.scalar_tensor_tensor(masks[:, t, :], rel[n % 2][:, :], wi[:, t, h:h + 1], base, ALU.mult, ALU.add
                                                     ).then_inc(*added.inc())
                            dve.wait_ge(*added.at(n + 1))
                        for _ in range(TOPK // 8):
                            for t in range(TILES):
                                link(dve.max(best[:, t, :], masks[:, t, :]))
                                link(dve.match_replace(masks[:, t, :], best[:, t, :], masks[:, t, :], TAKEN))
                        for t in range(TILES):
                            link(dve.tensor_scalar(masks[:, t, :], masks[:, t, :], TAKEN / 2, MASKED, ALU.is_gt, ALU.mult))
                            link(dve.tensor_tensor(masks[:, t, :], masks[:, t, :], causal[:, t, :], ALU.add))

            attention(chip, "topk_attention", q, k, lambda h, j: v[:, j, h, :], HD, head_rows(y_fm), None, causal=False,
                      scale=HD ** -0.5, bias=bias_of, masks=masks)
        with ExitStack() as inner:
            def sbi(name, shape):
                return inner.enter_context(chip.nc.sbuf_tensor(f"diff_{name}", shape, F32))
            maps = sbi("maps", [P, 2 * DIFF_HEADS, SEQ])
            q, k, v = (sbi(n, [P, TILES, 2 * DIFF_HEADS, HD]) for n in "qkv")
            heads_in(("q_d", "k_d", "v_d"), (q, k, v))
            vd = v[:, :, :, :].rearrange("p t (h a) d -> p t h (a d)", a=2)
            attention(chip, "diff_attention", q, k, lambda h, j: vd[:, j, h // 2, :], HD, lambda h: maps[:, h, :], None, dv=DIFF_V,
                      causal=False, scale=HD ** -0.5, bias=lambda h: bias_of(HEADS + h // 2), masks=causal)
            with chip.stage("diff_out") as st:
                lam, pr, ex = st.sb("lam", [P, 4, HD]), st.sb("pr", [P, 2, HD]), st.sb("ex", [P, 4])
                sq, rr = st.sb("sq", [P, DIFF_HEADS, SEQ]), st.sb("rr", [P, DIFF_HEADS, SEQ])
                loaded, dotted, exped = st.count("loaded"), st.count("dotted"), st.count("exped")
                squared, summed = st.count("squared"), st.count("summed")
                root = Roots(st)

                @st.block.sync
                def _(sp):
                    sp.dma_start(lam[:, :, :].rearrange("p a d -> p (a d)"), io["diff_lam"].to_broadcast([P, 4 * HD])
                                 ).then_inc(*loaded.inc(16))

                @st.block.scalar
                def _(act):
                    act.wait_ge(*dotted.at(1))
                    act.activation(ex[:, 0:2], ex[:, 0:2], ACT.Exp).then_inc(*exped.inc())
                    for h in range(DIFF_HEADS):
                        root.serve(act, rr[:, h, :], 1.0 - lambda_init)

                @st.block.tensor
                def _(pe):
                    pe.wait_ge(*squared.at(1))
                    for h in range(DIFF_HEADS):
                        pe.matmul(chip.bank[h][:, :], chip.ones, sq[:, h, :], start=True, stop=True).then_inc(*summed.inc())

                @st.block.vector
                def _(dve):
                    link = st.chain(dve, "diff_step")
                    dve.wait_ge(*loaded.at(16))
                    link(dve.tensor_tensor(pr[:, :, :], lam[:, 0::2, :], lam[:, 1::2, :], ALU.mult))
                    dve.tensor_reduce(ex[:, 0:2], pr[:, :, :], AX.X, ALU.add).then_inc(*dotted.inc())
                    dve.wait_ge(*exped.at(1))
                    link(dve.tensor_tensor(ex[:, 2:3], ex[:, 1:2], ex[:, 0:1], ALU.subtract))
                    link(dve.tensor_scalar(ex[:, 2:3], ex[:, 2:3], lambda_init, None, ALU.subtract))
                    for h in range(DIFF_HEADS):
                        link(dve.scalar_tensor_tensor(maps[:, 2 * h, :], maps[:, 2 * h + 1, :], ex[:, 2:3], maps[:, 2 * h, :],
                                                      ALU.mult, ALU.add))
                    dve.tensor_tensor(sq[:, :, :], maps[:, 0::2, :], maps[:, 0::2, :], ALU.mult).then_inc(*squared.inc())
                    for h in range(DIFF_HEADS):
                        dve.wait_ge(*summed.at(h + 1))
                        root(dve, link, rr[:, h, :], dve.tensor_scalar(rr[:, h, :], chip.bank[h][:, :], 1.0 / DIFF_V, EPS,
                                                                       ALU.mult, ALU.add))
                        link(dve.scalar_tensor_tensor(y_fm[:, WC + h, :], maps[:, 2 * h, :], par("diff_norm_g"), rr[:, h, :],
                                                      ALU.mult, ALU.mult))
        add_gated(chip, "attn_out", x, y_fm, io["cd_w_out"][0], gate_row)


def route(chip, i, io, fm, gates, routed):
    n_r = GROUPS + EXPERTS
    with ExitStack() as ctx:
        lg = ctx.enter_context(chip.nc.sbuf_tensor(f"logits_{i}", [P, TILES, n_r], F32))
        gemm(chip, "router", [cols_of(io["router_w"][i], 0, n_r)],
             [j[:3] + ("dve",) + j[4:] for j in tm_jobs(0, fm, DC, n_r, 0, n_r, lambda t: copy_to(lg[:, t, :]))])
        with chip.stage("route") as st:
            rb, m = st.sb("rb", [P, n_r]), st.sb("m", [P, 8, TILES])
            a4, g4, t4 = (st.sb(n, [P, TILES, GROUPS]) for n in ("a4", "g4", "t4"))
            fine, sel = st.sb("fine", [P, TILES, GROUPS, PER_GROUP]), st.sb("sel", [P, TILES, PER_GROUP])
            o1, o2, t8 = (st.sb(n, [P, TILES, PER_GROUP]) for n in ("o1", "o2", "t8"))
            loaded, shifted, exped = st.count("loaded"), st.count("shifted"), st.count("exped")

            @st.block.sync
            def _(sp):
                sp.dma_start(rb[:, :], io["router_b"][i:i + 1, :].to_broadcast([P, n_r])).then_inc(*loaded.inc(16))

            @st.block.scalar
            def _(act):
                act.wait_ge(*shifted.at(1))
                act.activation(a4[:, :, :], a4[:, :, :], ACT.Exp).then_inc(*exped.inc())
                act.wait_ge(*shifted.at(2))
                act.activation(m[:, 3, :], m[:, 3, :], ACT.Exp).then_inc(*exped.inc())

            @st.block.vector
            def _(dve):
                link = st.chain(dve, "route_step")

                def first_best(onehot, x, best, tmp, n):
                    shape = [P, TILES, n]
                    link(dve.tensor_reduce(best, x, AX.X, ALU.max))
                    link(dve.tensor_tensor(tmp, x, over(best, shape, 2), ALU.is_equal))
                    link(dve.tensor_tensor(tmp, tmp, over(chip.rank8[:, 0:n], shape, 1), ALU.mult))
                    link(dve.tensor_reduce(m[:, 7, :], tmp, AX.X, ALU.max))
                    link(dve.tensor_tensor(onehot, tmp, over(m[:, 7, :], shape, 2), ALU.is_equal))

                dve.wait_ge(*loaded.at(16))
                link(dve.tensor_tensor(lg[:, :, :], lg[:, :, :], over(rb[:, :], [P, TILES, n_r], 1), ALU.add))
                lgg = lg[:, :, 0:GROUPS]
                first_best(g4[:, :, :], lgg, m[:, 0, :], t4[:, :, :], GROUPS)
                dve.tensor_tensor(a4[:, :, :], lgg, over(m[:, 0, :], [P, TILES, GROUPS], 2), ALU.subtract).then_inc(*shifted.inc())
                dve.wait_ge(*exped.at(1))
                link(dve.tensor_reduce(m[:, 1, :], a4[:, :, :], AX.X, ALU.add))
                link(dve.reciprocal(m[:, 1, :], m[:, 1, :]))
                shape = [P, TILES, GROUPS, PER_GROUP]
                for t in range(TILES):
                    link(dve.tensor_tensor(fine[:, t], lg[:, t, GROUPS:n_r].rearrange("p (g e) -> p g e", g=GROUPS),
                                           over(g4[:, t, :], shape[:1] + shape[2:], 2), ALU.mult))
                    link(dve.tensor_reduce(sel[:, t, :], fine[:, t].rearrange("p g e -> p e g"), AX.X, ALU.add))
                first_best(o1[:, :, :], sel[:, :, :], m[:, 2, :], t8[:, :, :], PER_GROUP)
                link(dve.scalar_tensor_tensor(sel[:, :, :], o1[:, :, :], TAKEN, sel[:, :, :], ALU.mult, ALU.add))
                first_best(o2[:, :, :], sel[:, :, :], m[:, 3, :], t8[:, :, :], PER_GROUP)
                dve.tensor_tensor(m[:, 3, :], m[:, 3, :], m[:, 2, :], ALU.subtract).then_inc(*shifted.inc())
                dve.wait_ge(*exped.at(2))
                link(dve.tensor_scalar(m[:, 4, :], m[:, 3, :], 1.0, None, ALU.add))
                link(dve.reciprocal(m[:, 4, :], m[:, 4, :]))
                link(dve.tensor_tensor(m[:, 4, :], m[:, 4, :], m[:, 1, :], ALU.mult))
                link(dve.tensor_tensor(m[:, 5, :], m[:, 4, :], m[:, 3, :], ALU.mult))
                e8 = [P, TILES, PER_GROUP]
                link(dve.tensor_tensor(t8[:, :, :], o1[:, :, :], o2[:, :, :], ALU.add))
                link(dve.tensor_tensor(o1[:, :, :], o1[:, :, :], over(m[:, 4, :], e8, 2), ALU.mult))
                link(dve.tensor_tensor(o2[:, :, :], o2[:, :, :], over(m[:, 5, :], e8, 2), ALU.mult))
                link(dve.tensor_tensor(o1[:, :, :], o1[:, :, :], o2[:, :, :], ALU.add))
                for dst, src in ((gates, o1), (routed, t8)):
                    dv = dst[:, :, :].rearrange("p t (g e) -> p t g e", g=GROUPS)
                    for t in range(TILES):
                        link(dve.tensor_tensor(dv[:, t], over(g4[:, t, :], shape[:1] + shape[2:], 2),
                                               over(src[:, t, :], shape[:1] + shape[2:], 1), ALU.mult))


def plan(chip, i, gates, routed, slot_of, gate_of, counts):
    E = EXPERTS
    with chip.stage("plan") as st:
        slot, t3 = st.sb("slot", [P, TILES, E]), st.sb("t3", [P, E, TILES * 2])
        blocks, first = st.sb("blocks", [P, E]), st.sb("first", [P, E])
        last = st.sb("last", [P, E])
        slotT, gateT = st.sb("slotT", [E, SEQ]), st.sb("gateT", [E, SEQ])
        rangeT, hot = st.sb("rangeT", [E, 2]), st.sb("hot", [E, ITEMS])
        row = st.sb("row", [1, 1 + ITEMS])
        half = st.sb("half", [1, ITEMS])
        ranked, placed, turned, taken = st.count("ranked"), st.count("placed"), st.count("turned"), st.count("hot_ready")
        tabled = st.count("tables_done")
        B = chip.bank

        @st.block.tensor
        def _(pe):
            for t in range(TILES):
                product(pe, B[0][:, t * E:(t + 1) * E], [(chip.before, routed[:, t, :])] +
                        [(chip.ones, routed[:, u, :]) for u in range(t)])
            product(pe, B[0][:, TILES * E:(TILES + 1) * E], [(chip.ones, routed[:, u, :]) for u in range(TILES)]
                    ).then_inc(*ranked.inc())
            pe.wait_ge(*placed.at(1))
            for t in range(TILES):
                pe.transpose(B[1][0:E, t * P:(t + 1) * P], slot[:, t, :], chip.ident)
                pe.transpose(B[2][0:E, t * P:(t + 1) * P], gates[:, t, :], chip.ident)
            pe.transpose(B[3][0:E, 0:P], first[:, :], chip.ident)
            pe.transpose(B[3][0:E, P:2 * P], last[:, :], chip.ident).then_inc(*turned.inc())
            pe.wait_ge(*taken.at(1))
            for t in range(TILES):
                pe.matmul(B[4][:, t * ITEMS:(t + 1) * ITEMS], slotT[:, t * P:(t + 1) * P], hot[:, :], start=True, stop=True)
                pe.matmul(B[5][:, t * ITEMS:(t + 1) * ITEMS], gateT[:, t * P:(t + 1) * P], hot[:, :], start=True, stop=True)
            pe.matmul(B[6][0:1, 0:ITEMS], chip.number[0:E, :], hot[:, :], start=True, stop=True).then_inc(*tabled.inc())

        @st.block.vector
        def _(dve):
            link = st.chain(dve, "plan_step")
            dve.wait_ge(*ranked.at(1))
            total = B[0][:, TILES * E:(TILES + 1) * E]
            link(dve.tensor_tensor(t3[:, :, :], over(total, [P, E, SEQ // SLOTS], 2),
                                   over(chip.block_starts, [P, E, SEQ // SLOTS], 1), ALU.is_gt))
            link(dve.tensor_reduce(blocks[:, :], t3[:, :, :], AX.X, ALU.add))
            link(dve.tensor_tensor_scan(last[:, :], chip.ones[:, 0:E], blocks[:, :], 0.0, ALU.mult, ALU.add))
            link(dve.tensor_tensor(first[:, :], last[:, :], blocks[:, :], ALU.subtract))
            link(dve.tensor_scalar(slot[:, :, :], routed[:, :, :], 1.0, -FAR, ALU.subtract, ALU.mult))
            link(dve.tensor_tensor(slot[:, :, :], slot[:, :, :], B[0][:, 0:TILES * E].rearrange("p (t e) -> p t e", t=TILES), ALU.add))
            link(dve.tensor_scalar(blocks[:, :], first[:, :], float(SLOTS), None, ALU.mult))
            dve.tensor_tensor(slot[:, :, :], slot[:, :, :], over(blocks[:, :], [P, TILES, E], 1), ALU.add).then_inc(*placed.inc())
            link(dve.tensor_scalar(half[:, :], chip.numbers[0:1, 0:ITEMS], 2.0, None, ALU.mult))
            link(dve.tensor_scalar(half[:, :], half[:, :], last[0:1, E - 1:E], None, ALU.is_lt))
            link(dve.tensor_reduce(row[:, 0:1], half[:, :], AX.X, ALU.add))
            dve.wait_ge(*turned.at(1))
            link(dve.tensor_copy(rangeT[:, 0:1], B[3][0:E, 0:1]))
            link(dve.tensor_copy(rangeT[:, 1:2], B[3][0:E, P:P + 1]))
            link(dve.tensor_copy(slotT[:, :], B[1][0:E, :]))
            link(dve.tensor_copy(gateT[:, :], B[2][0:E, :]))
            link(dve.tensor_scalar(hot[:, :], chip.numbers[0:E, 0:ITEMS], rangeT[:, 0:1], None, ALU.is_ge))
            dve.scalar_tensor_tensor(hot[:, :], chip.numbers[0:E, 0:ITEMS], rangeT[:, 1:2], hot[:, :], ALU.is_lt, ALU.mult
                                     ).then_inc(*taken.inc())
            dve.wait_ge(*tabled.at(1))
            shape = [P, TILES, ITEMS]
            link(dve.scalar_tensor_tensor(slot_of[:, :, :], over(chip.numbers[:, 0:ITEMS], shape, 1), -float(SLOTS),
                                          B[4][:, 0:TILES * ITEMS].rearrange("p (t j) -> p t j", t=TILES), ALU.mult, ALU.add))
            link(dve.tensor_copy(gate_of[:, :, :], B[5][:, 0:TILES * ITEMS].rearrange("p (t j) -> p t j", t=TILES)))
            link(dve.tensor_copy(row[:, 1:1 + ITEMS], B[6][0:1, 0:ITEMS]))
            link(dve.tensor_copy(counts[:, :], row[:, :]))


def item_experts(chip, i, io, h, slot_of, gate_of, counts, acc):
    B = chip.bank
    n_spread = TILES * 2
    with chip.stage("items") as st:
        wg, wu = ([st.sb(f"{n}{s}", [P, DC, D_EXP]) for s in range(2)] for n in ("wg", "wu"))
        wd = [st.sb(f"wd{s}", [P, FC, D]) for s in range(2)]
        pick, spread = st.sb("pick", [P, TILES, 2, SLOTS]), st.sb("spread", [P, TILES, 2, SLOTS])
        spreadT, y = st.sb("spreadT", [P, SEQ]), st.sb("y", [P, D])
        hs = st.sb("hs", [P, DC, P])
        hid, hidT = st.sb("hid", [P, D_EXP]), st.sb("hidT", [P, FC, P])

        def one(name):
            return st.count(name, fresh=True)
        gate_loaded, up_loaded, down_loaded = one("gate_loaded"), one("up_loaded"), one("down_loaded")
        gate_done, up_done, down_done = one("gate_done"), one("up_done"), one("down_done")
        silued, hidden, hturned, hmoved = one("silu"), one("hidden"), one("hidden_turned"), one("hidden_moved")
        picked, gathered, filled = one("picked"), one("gathered"), one("slots_filled")
        weighed, turned, tmoved = one("spread_ready"), one("spread_turned"), one("spread_moved")
        yready, spreaded, added, cleared = one("y_ready"), one("spread_product"), one("added"), one("cleared")

        def pairs_of(eng):
            return eng.value_load(counts[0:1, 0:1], min_val=1, max_val=ITEMS // 2 - 1)

        @st.block.gpsimd
        def _(pool):
            pool.memset(spreadT[:, :], 0.0)
            pool.memset(y[:, :], 0.0)
            pool.memset(acc[:, :, :], 0.0).then_inc(*cleared.inc())

        @st.block.sync
        def _(sp):
            def expert_of(name, e):
                w = io[name].rearrange("l e a n -> (l e) a n")
                return w[bass.ds(e + i * EXPERTS, 1), :, :].rearrange("o (k p) n -> p (o k) n", p=P)
            with sp.Fori(0, pairs_of(sp)) as p:
                e = [sp.value_load(counts[0:1, bass.ds(p * 2 + s + 1, 1)], min_val=0, max_val=EXPERTS - 1) for s in range(2)]
                sp.wait_ge(*gate_done.at(p + 1))
                for s in range(2):
                    sp.dma_start(wg[s][:, :, :], expert_of("moe_w_gate", e[s])).then_inc(*gate_loaded.inc(16))
                sp.wait_ge(*up_done.at(p + 1))
                for s in range(2):
                    sp.dma_start(wu[s][:, :, :], expert_of("moe_w_up", e[s])).then_inc(*up_loaded.inc(16))
                sp.wait_ge(*down_done.at(p + 1))
                for s in range(2):
                    sp.dma_start(wd[s][:, :, :], expert_of("moe_w_down", e[s])).then_inc(*down_loaded.inc(16))

        @st.block.tensor
        def _(pe):
            for c in (gate_done, up_done, down_done):
                pe.sem_inc(c.sem, 1)

            def gather(q):
                pe.wait_ge(*picked.at(q + 1))
                pe.wait_ge(*filled.at(q + 1))
                for k in range(DC):
                    ins = product(pe, B[6 + k // 4][:, (k % 4) * P:(k % 4 + 1) * P],
                                  [(h[:, t, k * P:(k + 1) * P], pick[:, t, :, :].rearrange("p a s -> p (a s)")) for t in range(TILES)])
                ins.then_inc(*gathered.inc())

            def side_by_side(bank, chunks, lhs, weights, cols):
                for k in range(chunks):
                    for s in range(2):
                        rows = slice(s * SLOTS, (s + 1) * SLOTS)
                        ins = pe.matmul(bank[rows, :], lhs[:, k, rows], weights[s][:, k, cols], start=(k == 0), stop=(k == chunks - 1))
                return ins

            def spread_back(p):
                pe.wait_ge(*tmoved.at(p + 1))
                pe.wait_ge(*yready.at(p + 1))
                for n in range(n_spread):
                    t, d = divmod(n, 2)
                    pe.wait_ge(*added.at(n_spread * p + n + 1))
                    pe.matmul(B[4 + n % 2][:, :], spreadT[:, t * P:(t + 1) * P], y[:, d * BANK:(d + 1) * BANK],
                              start=True, stop=True).then_inc(*spreaded.inc())
            pe.wait_ge(*cleared.at(1))
            gather(0)
            n = pairs_of(pe)
            with pe.Fori(0, n) as p:
                pe.wait_ge(*filled.at(p + 2))
                pe.wait_ge(*yready.at(p + 1))
                pe.wait_ge(*gate_loaded.at(32 * p + 32))
                side_by_side(B[0], DC, hs, wg, slice(0, D_EXP)).then_inc(*gate_done.inc())
                pe.wait_ge(*up_loaded.at(32 * p + 32))
                side_by_side(B[1], DC, hs, wu, slice(0, D_EXP)).then_inc(*up_done.inc())
                spread_back(p)
                pe.wait_ge(*hidden.at(p + 1))
                for f in range(FC):
                    ins = pe.transpose(B[2][:, f * P:(f + 1) * P], hid[:, f * P:(f + 1) * P], chip.ident)
                ins.then_inc(*hturned.inc())
                pe.wait_ge(*weighed.at(p + 1))
                for t in range(TILES):
                    ins = pe.transpose(B[3][:, t * P:(t + 1) * P], spread[:, t, :, :].rearrange("p a s -> p (a s)"), chip.ident)
                ins.then_inc(*turned.inc())
                pe.wait_ge(*hmoved.at(p + 1))
                pe.wait_ge(*down_loaded.at(32 * p + 32))
                for d in range(2):
                    ins = side_by_side(B[d], FC, hidT, wd, slice(d * BANK, (d + 1) * BANK))
                ins.then_inc(*down_done.inc())
                gather(p + 1)
            spread_back(n)

        @st.block.scalar
        def _(act):
            act.wait_ge(*cleared.at(1))
            act.sem_inc(yready.sem, 1)
            act.sem_inc(filled.sem, 1)

            def fill(q):
                act.wait_ge(*gathered.at(q + 1))
                for n in range(2):
                    ins = act.activation(hs[:, 4 * n:4 * n + 4, :], B[6 + n][:, :].rearrange("p (k n) -> p k n", k=4), ACT.Copy)
                ins.then_inc(*filled.inc())
            fill(0)
            with act.Fori(0, pairs_of(act)) as p:
                act.wait_ge(*gate_done.at(p + 2))
                act.activation(hid[:, :], B[0][:, :], ACT.Silu).then_inc(*silued.inc())
                act.wait_ge(*hturned.at(p + 1))
                act.activation(hidT[:, :, :], B[2][:, :].rearrange("p (f n) -> p f n", f=FC), ACT.Copy).then_inc(*hmoved.inc())
                act.wait_ge(*down_done.at(p + 2))
                for n in range(2):
                    ins = act.activation(y[:, n * BANK:(n + 1) * BANK], B[n][:, :], ACT.Copy)
                ins.then_inc(*yready.inc())
                fill(p + 1)

        @st.block.vector
        def _(dve):
            dve.sem_inc(added.sem, 2)
            dve.wait_ge(*cleared.at(1))
            dve.sem_inc(tmoved.sem, 1)
            slots = over(chip.numbers[:, 0:SLOTS], [P, TILES, SLOTS], 1)

            def make_pick(q):
                for a in range(2):
                    ins = dve.tensor_tensor(pick[:, :, a, :], slots,
                                            slot_of[:, :, bass.ds(q * 2 + a, 1)].to_broadcast([P, TILES, SLOTS]), ALU.is_equal)
                ins.then_inc(*picked.inc())

            def add_spread(p):
                for n in range(n_spread):
                    t, d = divmod(n, 2)
                    dve.wait_ge(*spreaded.at(n_spread * p + n + 1))
                    dst = acc[:, t, d * BANK:(d + 1) * BANK]
                    dve.tensor_tensor(dst, dst, B[4 + n % 2][:, :], ALU.add).then_inc(*added.inc())
            make_pick(0)
            n = pairs_of(dve)
            with dve.Fori(0, n) as p:
                dve.wait_ge(*picked.at(p + 1))
                for a in range(2):
                    ins = dve.tensor_tensor(spread[:, :, a, :], pick[:, :, a, :],
                                            gate_of[:, :, bass.ds(p * 2 + a, 1)].to_broadcast([P, TILES, SLOTS]), ALU.mult)
                ins.then_inc(*weighed.inc())
                dve.wait_ge(*gathered.at(p + 1))
                dve.wait_ge(*weighed.at(p + 1))
                make_pick(p + 1)
                dve.wait_ge(*silued.at(p + 1))
                dve.wait_ge(*up_done.at(p + 2))
                dve.tensor_tensor(hid[:, :], B[1][:, :], hid[:, :], ALU.mult).then_inc(*hidden.inc())
                add_spread(p)
                dve.wait_ge(*turned.at(p + 1))
                dve.tensor_copy(spreadT[:, :], B[3][:, :]).then_inc(*tmoved.inc())
            add_spread(n)


def experts(chip, i, io, x, norm_rows, gate_row):
    with ExitStack() as ctx:
        def sb(name, shape, dt=F32):
            return ctx.enter_context(chip.nc.sbuf_tensor(f"experts_{name}_{i}", shape, dt))
        acc, h = sb("acc", [P, TILES, D]), sb("h", [P, TILES, D])
        slot_of, gate_of = sb("slot_of", [P, TILES, ITEMS]), sb("gate_of", [P, TILES, ITEMS])
        counts = sb("counts", [1, 1 + ITEMS], I32)
        with ExitStack() as inner:
            gates, routed = (inner.enter_context(chip.nc.sbuf_tensor(f"{n}_{i}", [P, TILES, EXPERTS], F32)) for n in ("gates", "routed"))
            fm = inner.enter_context(chip.nc.sbuf_tensor(f"experts_fm_{i}", [P, DC, SEQ], F32))
            norm_to_fm(chip, x, fm, plain, norm_rows, h)
            route(chip, i, io, fm, gates, routed)
            plan(chip, i, gates, routed, slot_of, gate_of, counts)
        item_experts(chip, i, io, h, slot_of, gate_of, counts, acc)
        chip.clear_fresh()
        with chip.stage("moe_residual") as st:
            @st.block.vector
            def _(dve):
                link = st.chain(dve, "residual_step")
                link(dve.tensor_tensor(acc[:, :, :], acc[:, :, :], over(gate_row, [P, TILES, D], 1), ALU.mult))
                dve.tensor_tensor(x[:, :, :], x[:, :, :], acc[:, :, :], ALU.add)


def second_block(chip, io, x):
    nc = chip.nc
    with ExitStack() as ctx:
        def sb(name, shape):
            return ctx.enter_context(nc.sbuf_tensor(name, shape, F32))
        mod = sb("mod", [P, 6, D])
        params = sb("params2", [P, N_P2])
        scratch = nc.dram_tensor("bias_scratch", [4 * BIAS_HEADS, TILES, P // 4, SEQ], F32, kind="Internal").ap()

        def par(name):
            n = {"c": DC, "conv_a": CONV_A * WC, "conv_b": CONV_B * WC, "diff_norm_g": 1}.get(name, WC)
            return params[:, P2_AT[name]:P2_AT[name] + n]
        with chip.stage("params") as st:
            loaded = st.count("params_loaded")

            @st.block.sync
            def _(sp):
                sp.dma_start(params[:, :], io["params_2"]).then_inc(*loaded.inc(16))
                sp.wait_ge(*loaded.at(16))
        for i in range(DEPTH):
            modulation(chip, i, io, par, mod)
            with nc.sbuf_tensor(f"mixer_fm_{i}", [P, DC, SEQ], F32) as fm:
                norm_to_fm(chip, x, fm, plain, (mod[:, 1, :], mod[:, 0, :]))
                if i == 0:
                    conv_mixers(chip, io, par, fm, x, mod[:, 2, :])
                else:
                    position_bias(chip, io, scratch)
                    attn_mixers(chip, io, par, fm, x, mod[:, 2, :], scratch)
            experts(chip, i, io, x, (mod[:, 4, :], mod[:, 3, :]), mod[:, 5, :])
        with chip.stage("final_norm") as st:
            sq, ss, g = st.sb("sq", [P, TILES, D]), st.sb("ss", [P, TILES]), st.sb("g", [P, D])
            squared, loaded = st.count("squares_summed"), st.count("gain_loaded")
            root = Roots(st)

            @st.block.sync
            def _(sp):
                sp.dma_start(g[:, :], io["norm_rows"][2 * DEPTH:2 * DEPTH + 1, :].to_broadcast([P, D])).then_inc(*loaded.inc(16))

            @st.block.scalar
            def _(act):
                for t in range(TILES):
                    act.activation(sq[:, t, :], x[:, t, :], ACT.Square, accum_out=ss[:, t:t + 1]).then_inc(*squared.inc())
                root.serve(act, ss[:, :])

            @st.block.vector
            def _(dve):
                link = st.chain(dve, "final_step")
                dve.wait_ge(*squared.at(TILES))
                root(dve, link, ss[:, :], dve.tensor_scalar(ss[:, :], ss[:, :], 1.0 / D, EPS, ALU.mult, ALU.add))
                dve.wait_ge(*loaded.at(16))
                for t in range(TILES):
                    dve.scalar_tensor_tensor(x[:, t, :], x[:, t, :], ss[:, t:t + 1], g[:, :], ALU.mult, ALU.mult)


def first_block(chip, io, x, params, rows):
    nc = chip.nc
    with ExitStack() as ctx:
        def sb(name, shape):
            return ctx.enter_context(nc.sbuf_tensor(name, shape, F32))
        fm = sb("fm", [P, DC, SEQ])
        v_first = sb("v_first", [P, WC, SEQ])
        merged = sb("merged", [P, DC, SEQ])
        o_fm = sb("o_fm", [P, WC, SEQ])
        for l in range(DEPTH):
            def par(name, c, l=l):
                at = PAR_AT[name, l] + c
                return params[:, at:at + 1]

            def row(name, l=l):
                at, n = ROW_AT[name, l]
                return rows[:, at:at + n]

            def by_gain(act, out, ps, c, par=par):
                return act.activation(out, ps, ACT.Copy, scale=par("norm_g", c))
            norm_to_fm(chip, x, fm, by_gain)
            with nc.sbuf_tensor(f"merge_gate_{l}", [P, DC, SEQ], F32) as sg:
                mla(chip, l, io, par, row, fm, o_fm, sg)
                merge(chip, sg, o_fm, io["w_pa"][l], merged, True)
                fox(chip, l, io, par, row, fm, o_fm, sg)
                merge(chip, sg, o_fm, io["w_pb"][l], merged, False)
            rwkv(chip, l, io, par, fm, o_fm, v_first)
            with nc.sbuf_tensor(f"merge_gate_c_{l}", [P, DC, SEQ], F32) as sg:
                merge(chip, sg, o_fm, io["w_pc"][l], merged, False, (fm, io["w_in"][l], COL["gc"]))
            loads, jobs = [], []
            for c in range(2):
                loads.append(cols_of(io["w_out"][l], c * BANK, BANK))

                def add(t, c=c):
                    dst = x[:, t, c * BANK:(c + 1) * BANK]
                    return lambda dve, ps: dve.tensor_tensor(dst, dst, ps, ALU.add)
                jobs += [j[:3] + ("dve",) + j[4:] for j in tm_jobs(c, merged, DC, BANK, 0, BANK, add)]
            gemm(chip, "out", loads, jobs)



PAR_LIST = [("norm_g", DC), ("qa_g", 2), ("kva_g", 1), ("mu", SHIFT // P), ("w0", WC), ("a0", WC), ("k_k", WC),
            ("k_a", WC), ("r_k", WC), ("lnx_g", WC), ("lnx_b", WC), ("v0", WC), ("b_f", 1)]
PAR_AT, N_PAR = {}, 0
for _l in range(DEPTH):
    for _name, _n in PAR_LIST:
        PAR_AT[_name, _l] = N_PAR
        N_PAR += _n
ROW_LIST = [("q_g", QK_A), ("knope_g", NOPE), ("krope_g", ROPE), ("fox_q_g", HD), ("fox_k_g", HD)]
ROW_AT, N_ROW = {}, 0
for _l in range(DEPTH):
    for _name, _n in ROW_LIST:
        ROW_AT[_name, _l] = (N_ROW, _n)
        N_ROW += _n


def bucket_starts():
    exact = NUM_BUCKETS // 2
    n = np.arange(exact, 4 * MAX_DISTANCE, dtype=np.float32)
    ratio = np.log(n / np.float32(exact)) / np.float32(np.log(MAX_DISTANCE / exact))
    bucket = np.minimum(exact + (ratio * (NUM_BUCKETS - exact)).astype(np.int32), NUM_BUCKETS - 1)
    starts = [-2.0 ** 31] + list(range(1, exact)) + [n[np.argmax(bucket >= b)] for b in range(exact, NUM_BUCKETS)]
    return np.array(starts, np.float32)


def shape_constants():
    i = np.arange(P)
    row, col = i[:, None], i[None, :]
    same = (row // CH) == (col // CH)
    sub = (row // SUB) == (col // SUB)
    strict, incl = same & (row < col), same & (row <= col)
    inv = np.float32(10000.0) ** (-np.arange(0, ROPE, 2, dtype=np.float32) / np.float32(ROPE))
    ang = np.arange(SEQ, dtype=np.float32)[:, None] * inv[None, :].astype(np.float32)
    def tok(a):
        return a.reshape(TILES, P, -1).transpose(1, 0, 2).reshape(P, -1)
    keep = np.tile((np.arange(SEQ) % CH != 0)[None, :], (P, 1))
    parts = [("ident", row == col), ("causal_add", np.where(col <= row, 0.0, MASKED)),
             ("head_ones", (row // HD) == (col // HD)),
             ("chunk_masks", np.concatenate([strict, incl, strict, incl], 1)),
             ("sub_lower", sub & (row > col)), ("sub_upper", sub & (row < col)), ("off_sub", ~sub),
             ("ones", np.ones((P, P))), ("bucket_from", np.tile(bucket_starts(), 4)[:, None]),
             ("rank8", np.tile(np.arange(8, 0, -1)[None, :], (P, 1))),
             ("before", row < col), ("block_starts", np.tile(SLOTS * np.arange(SEQ // SLOTS)[None, :], (P, 1))),
             ("numbers", np.tile(np.arange(max(SLOTS, ITEMS))[None, :], (P, 1))), ("number", i[:, None]),
             ("chunk_keep", keep), ("cos", tok(np.cos(ang))), ("sin", tok(np.sin(ang)))]
    at, where = 0, {}
    for name, a in parts:
        where[name] = (at, a.shape[1])
        at += a.shape[1]
    return np.concatenate([a.astype(np.float32) for _, a in parts], 1), where


def program(nc, io, out):
    with ExitStack() as ctx:
        chip = Chip(nc, ctx)
        x = chip.sb("x", [P, TILES, D])
        const, where = shape_constants()
        consts = chip.sb("consts", [P, const.shape[1]])
        params = chip.sb("params", [P, N_PAR])
        rows = chip.sb("rows", [P, N_ROW])
        chip.name_tables({name: consts[:, at:at + n] for name, (at, n) in where.items()})
        with chip.stage("start") as st:
            loaded = st.count("inputs_loaded")

            @st.block.sync
            def _(sp):
                sp.dma_start(x[:, :, :], io["x"].rearrange("o (t p) d -> p (o t) d", p=P)).then_inc(*loaded.inc(16))
                sp.dma_start(consts[:, :], io["shape_consts"]).then_inc(*loaded.inc(16))
                sp.dma_start(params[:, :], io["params"]).then_inc(*loaded.inc(16))
                sp.dma_start(rows[:, :], io["rows"].to_broadcast([P, N_ROW])).then_inc(*loaded.inc(16))
                sp.wait_ge(*loaded.at(64))
        first_block(chip, io, x, params, rows)
        second_block(chip, io, x)
        with chip.stage("end") as st:
            stored = st.count("output_stored")

            @st.block.sync
            def _(sp):
                sp.dma_start(out.rearrange("o (t p) d -> p (o t) d", p=P), x[:, :, :]).then_inc(*stored.inc(16))
                sp.wait_ge(*stored.at(16))



SECOND = ["ada_w", "ab_w_in", "ab_w_out", "cd_w_in", "cd_w_out", "moe_w_gate", "moe_w_up", "moe_w_down"]
WHOLE = ["x", "w_in", "mla_w_uq", "mla_w_ukv", "rwkv_w_up", "rwkv_a_up", "rwkv_v_down", "rwkv_v_up",
         "w_pa", "w_pb", "w_pc", "w_out"]


def laid_out(inputs):
    def pad(v, n):
        v = np.asarray(v, np.float32).reshape(-1)
        return np.concatenate([v, np.zeros(n * P - v.size, np.float32)]).reshape(n, P).T
    of = {"norm_g": "norm_g", "qa_g": "mla_qa_g", "kva_g": "mla_kva_g", "mu": "rwkv_mu", "w0": "rwkv_w0", "a0": "rwkv_a0",
          "k_k": "rwkv_k_k", "k_a": "rwkv_k_a", "r_k": "rwkv_r_k", "lnx_g": "rwkv_lnx_g", "lnx_b": "rwkv_lnx_b", "b_f": "fox_b_f"}
    cols, rows = [], []
    for l in range(DEPTH):
        for name, n in PAR_LIST:
            if name == "v0":
                cols.append(pad(inputs["rwkv_v0"][l - 1] if l else np.zeros(0), n))
            else:
                cols.append(pad(inputs[of[name]][l], n))
        for name, n in ROW_LIST:
            rows.append(np.asarray(inputs[name if name.startswith("fox") else "mla_" + name][l]).reshape(1, n))
    arrays = {name: np.ascontiguousarray(inputs[name]) for name in WHOLE}
    arrays["params"] = np.ascontiguousarray(np.concatenate(cols, 1))
    arrays["rows"] = np.ascontiguousarray(np.concatenate(rows, 1))
    arrays["shape_consts"] = shape_constants()[0]
    arrays.update({name: np.ascontiguousarray(inputs[name + "_2"]) for name in SECOND})
    arrays["ada_b"] = np.ascontiguousarray(inputs["ada_b_2"])
    arrays["norm_rows"] = np.ascontiguousarray(np.concatenate(
        [np.asarray(inputs["norm_g_2"]).reshape(2 * DEPTH, D), np.asarray(inputs["final_norm_g_2"]).reshape(1, D)]))
    taps = [np.asarray(inputs[n][0]) for n in ("ab_conv_a_2", "ab_conv_b_2")]
    parts = [pad(inputs["c_2"], DC)] + [pad(t[j], WC) for t in taps for j in range(t.shape[0])]
    parts += [pad(inputs[n], WC) for n in ("ab_conv_b_bias_2", "ab_ln_g_2", "ab_ln_b_2")] + [pad(inputs["diff_norm_g_2"], 1)]
    arrays["params_2"] = np.ascontiguousarray(np.concatenate(parts, 1))
    arrays["router_w"] = np.ascontiguousarray(np.concatenate([inputs["moe_wr_g_2"], inputs["moe_wr_e_2"]], 2))
    arrays["router_b"] = np.ascontiguousarray(np.concatenate([inputs["moe_br_g_2"], inputs["moe_br_e_2"]], 1))
    arrays["diff_lam"] = np.asarray(inputs["diff_lam_2"]).reshape(1, 4 * HD)
    arrays["rel_bias"] = np.ascontiguousarray(inputs["rel_bias_2"])
    pos = np.asarray(inputs["positions_2"]).reshape(SEQ)
    arrays["pos_row"] = pos.reshape(1, SEQ)
    arrays["pos_col"] = np.ascontiguousarray(pos.reshape(TILES, P).T)
    arrays["pos_quarter"] = np.ascontiguousarray(pos.reshape(TILES, 4, P // 4).transpose(1, 0, 2).reshape(4, P))
    return arrays


def kernel(**inputs):
    import concourse.bacc as _bacc
    from concourse.bass_utils import run_bass_kernel_spmd as _run

    nc = _bacc.Bacc("TRN2", target_bir_lowering=False, num_devices=1)
    arrays = {f"in_{k}": v for k, v in laid_out(inputs).items()}
    io = {k[3:]: nc.dram_tensor(k, v.shape, mybir.dt.from_np(v.dtype), kind="ExternalInput").ap() for k, v in arrays.items()}
    out = nc.dram_tensor("out", (1, SEQ, D), F32, kind="ExternalOutput").ap()
    program(nc, io, out)
    r = _run(nc, [arrays], core_ids=[0])
    return r.results[0]["out"]
```
